# Optimizing a Trainium2 kernel written in Bass

```python
import jax, jax.numpy as jnp
from jax import lax
import numpy as np

D_MODEL = 1024
BATCH = 1
SEQ = 512
DEPTH = 1

CTX_LEN = 256
GRID_W = 64
N_MOD = 6

POOL_WINDOWS = (2, 4, 8, 16)
N_POOL_GROUPS = len(POOL_WINDOWS)
POOL_GROUP_DIM = D_MODEL // 8
D_POOL = N_POOL_GROUPS * POOL_GROUP_DIM

HEAD_DIM = 64
N_HEADS = D_MODEL // HEAD_DIM
D_RWKV = N_HEADS * HEAD_DIM
N_DIR = 2
LORA_W = 64
LORA_A = 64
LORA_G = 128
SHORT_CONV = 3
D_CONV = 3 * D_RWKV + N_DIR * LORA_W + N_DIR * LORA_A + LORA_G
N_BRANCHES = 2
D_IN = D_POOL + D_CONV + N_BRANCHES * D_MODEL
GN_EPS = 64e-5
RMS_EPS = 1e-6
DECAY_OFFSET = 0.5

N_GROUPS = 4
EXPERTS_PER_GROUP = 8
N_EXPERTS = N_GROUPS * EXPERTS_PER_GROUP
TOP_K = 2
D_EXPERT = D_MODEL // 4

kernel_name = 'hybrid_pool_rwkv7_hmoe_dit'

def rmsnorm(x, g):
    xf = x.astype(jnp.float32)
    return xf * lax.rsqrt(jnp.mean(xf * xf, axis=-1, keepdims=True) + RMS_EPS) * g

def modulate(h, shift, scale):
    return h * (1.0 + scale) + shift

def short_conv(u, w):
    pad = SHORT_CONV // 2
    return lax.conv_general_dilated(
        u, w[:, None, :].astype(u.dtype), window_strides=(1,), padding=[(pad, pad)],
        dimension_numbers=('NWC', 'WIO', 'NWC'), feature_group_count=u.shape[-1])

def box_mean(u, axis, win):
    n = u.shape[axis]
    lo = win // 2
    hi = win - lo - 1
    cs = jnp.cumsum(u, axis=axis)
    cs = jnp.concatenate([jnp.zeros_like(lax.slice_in_dim(cs, 0, 1, axis=axis)), cs], axis=axis)
    t = jnp.arange(n)
    upper = jnp.minimum(t + hi + 1, n)
    lower = jnp.maximum(t - lo, 0)
    total = jnp.take(cs, upper, axis=axis) - jnp.take(cs, lower, axis=axis)
    shape = [1] * u.ndim
    shape[axis] = n
    return total / (upper - lower).astype(u.dtype).reshape(shape)

def pool_mix(u, pool_w, pool_scale, rows):
    b, t, _ = u.shape
    uf = u.astype(jnp.float32).reshape(b, t, N_POOL_GROUPS, POOL_GROUP_DIM)
    diffs = []
    for gi, win in enumerate(POOL_WINDOWS):
        ug = uf[:, :, gi]
        if rows is None:
            m = box_mean(ug, 1, win)
        else:
            grid = ug.reshape(b, rows, GRID_W, POOL_GROUP_DIM)
            m = box_mean(box_mean(grid, 1, win), 2, win).reshape(b, t, POOL_GROUP_DIM)
        diffs.append(m - ug)
    d = jnp.stack(diffs, axis=2)
    y = jnp.einsum('btgc,gcd->btgd', d, pool_w)
    return y.reshape(b, t, D_POOL) * pool_scale

def rwkv7_scan(s0, r, w, k, v, kk, bb, reverse):
    xs = tuple(jnp.moveaxis(a, 1, 0) for a in (r, w, k, v, kk, bb))

    def step(s, inp):
        r_t, w_t, k_t, v_t, kk_t, b_t = inp
        sa = jnp.einsum('bhvk,bhk->bhv', s, -kk_t)
        s = s * w_t[:, :, None, :] + sa[..., None] * b_t[:, :, None, :] + v_t[..., None] * k_t[:, :, None, :]
        return s, jnp.einsum('bhvk,bhk->bhv', s, r_t)

    s_fin, ys = lax.scan(step, s0, xs, reverse=reverse)
    return jnp.moveaxis(ys, 0, 1), s_fin

def group_norm(y, wgt, bias):
    mu = jnp.mean(y, axis=-1, keepdims=True)
    var = jnp.mean(jnp.square(y - mu), axis=-1, keepdims=True)
    yn = (y - mu) * lax.rsqrt(var + GN_EPS)
    b, t = y.shape[:2]
    return yn.reshape(b, t, D_RWKV) * wgt + bias

def rwkv_time_mix(rw, init_states, w0, w2, a0, a2, g2, k_k, k_a, r_k, lnx_w, lnx_b):
    b, t, _ = rw.shape
    rw = rw.astype(jnp.float32)

    def heads(a):
        return a.reshape(b, t, N_HEADS, HEAD_DIM)

    r = rw[..., :D_RWKV]
    k = rw[..., D_RWKV:2 * D_RWKV]
    v = rw[..., 2 * D_RWKV:3 * D_RWKV]
    o = 3 * D_RWKV
    xw = rw[..., o:o + N_DIR * LORA_W].reshape(b, t, N_DIR, LORA_W)
    o += N_DIR * LORA_W
    xa = rw[..., o:o + N_DIR * LORA_A].reshape(b, t, N_DIR, LORA_A)
    o += N_DIR * LORA_A
    xg = rw[..., o:o + LORA_G]
    g = jax.nn.sigmoid(xg) @ g2
    kk = heads(k * k_k)
    kk = kk / jnp.maximum(jnp.linalg.norm(kk, axis=-1, keepdims=True), 1e-12)
    r_h, v_h = heads(r), heads(v)
    outs, finals = [], []
    for d in range(N_DIR):
        w_log = -jax.nn.softplus(-(w0[d] + jnp.tanh(xw[:, :, d]) @ w2[d])) - DECAY_OFFSET
        decay = jnp.exp(-jnp.exp(w_log))
        a = jax.nn.sigmoid(a0[d] + xa[:, :, d] @ a2[d])
        k_d = heads(k * (1.0 + (a - 1.0) * k_a))
        y, s_fin = rwkv7_scan(init_states[d], r_h, heads(decay), k_d, v_h, kk, kk * heads(a), reverse=(d == 1))
        bonus = (jnp.sum(r_h * k_d * r_k, axis=-1, keepdims=True) * v_h).reshape(b, t, D_RWKV)
        outs.append(group_norm(y, lnx_w, lnx_b) + bonus)
        finals.append(s_fin)
    return (outs[0] + outs[1]) * g, finals

def merge_branches(pool_y, rwkv_y, gate_logits, pool_proj, rwkv_proj, w_out):
    g_pool = jax.nn.sigmoid(gate_logits[..., :D_MODEL])
    g_rwkv = jax.nn.sigmoid(gate_logits[..., D_MODEL:])
    return (g_pool * (pool_y @ pool_proj) + g_rwkv * (rwkv_y @ rwkv_proj)) @ w_out

def hier_moe(u, rg_w, rg_b, re_w, re_b, w_gate, w_up, w_down):
    b, t, d = u.shape
    flat = u.reshape(b * t, d)
    n = flat.shape[0]
    group_p = jax.nn.softmax((flat @ rg_w + rg_b).astype(jnp.float32), axis=-1)
    g_idx = jnp.argmax(group_p, axis=-1)
    p_group = jnp.max(group_p, axis=-1, keepdims=True)
    e_logits = (flat @ re_w + re_b).astype(jnp.float32).reshape(n, N_GROUPS, EXPERTS_PER_GROUP)
    e_p = jax.nn.softmax(e_logits[jnp.arange(n), g_idx], axis=-1)
    top_p, top_i = lax.top_k(e_p, TOP_K)
    top_p = top_p / jnp.sum(top_p, axis=-1, keepdims=True)
    within = jnp.einsum('nk,nke->ne', top_p, jax.nn.one_hot(top_i, EXPERTS_PER_GROUP, dtype=jnp.float32))
    gates = (jax.nn.one_hot(g_idx, N_GROUPS, dtype=jnp.float32)[:, :, None]
             * (p_group * within)[:, None, :]).reshape(n, N_EXPERTS)
    y = jnp.zeros((n, d), jnp.float32)
    for e in range(N_EXPERTS):
        h = jax.nn.silu(flat @ w_gate[e]) * (flat @ w_up[e])
        y = y + gates[:, e:e + 1] * (h @ w_down[e])
    return y.reshape(b, t, d)

def setup_inputs(seed: int = 0) -> dict:
    key = jax.random.key(seed)
    ks = iter(jax.random.split(key, 40))
    L = DEPTH

    def nrm(shape, scale):
        return jax.random.normal(next(ks), shape, jnp.float32) * scale

    conv_base = jnp.array([0.25, 0.5, 0.25], jnp.float32)[None, :, None]
    return {
        'x': nrm((BATCH, SEQ, D_MODEL), 1.0),
        'c': nrm((BATCH, D_MODEL), 1.0),
        'ctx': nrm((BATCH, CTX_LEN, D_MODEL), 1.0),
        'c_ctx': nrm((D_MODEL,), 1.0),
        'ada_w': nrm((L, D_MODEL, N_MOD * D_MODEL), 0.5 * D_MODEL ** -0.5),
        'ada_b': nrm((L, N_MOD * D_MODEL), 0.02),
        'norm_gains': 1.0 + nrm((L, 4, D_MODEL), 0.05),
        'w_in': nrm((L, D_MODEL, D_IN), D_MODEL ** -0.5),
        'conv_w': conv_base + nrm((L, SHORT_CONV, D_CONV), 0.05),
        'pool_w': nrm((L, N_POOL_GROUPS, POOL_GROUP_DIM, POOL_GROUP_DIM), POOL_GROUP_DIM ** -0.5),
        'pool_scale': 1.0 + nrm((L, D_POOL), 0.05),
        'pool_proj': nrm((L, D_POOL, D_MODEL), D_POOL ** -0.5),
        'w0': jax.random.uniform(next(ks), (L, N_DIR, D_RWKV), jnp.float32, -6.0, 0.0),
        'w2': nrm((L, N_DIR, LORA_W, D_RWKV), 0.1),
        'a0': nrm((L, N_DIR, D_RWKV), 0.5),
        'a2': nrm((L, N_DIR, LORA_A, D_RWKV), 0.1),
        'g2': nrm((L, LORA_G, D_RWKV), LORA_G ** -0.5),
        'k_k': 0.85 + nrm((L, D_RWKV), 0.05),
        'k_a': 1.0 + nrm((L, D_RWKV), 0.05),
        'r_k': nrm((L, N_HEADS, HEAD_DIM), 0.1),
        'lnx_w': 1.0 + nrm((L, D_RWKV), 0.05),
        'lnx_b': nrm((L, D_RWKV), 0.02),
        'rwkv_proj': nrm((L, D_RWKV, D_MODEL), D_RWKV ** -0.5),
        'w_out': nrm((L, D_MODEL, D_MODEL), D_MODEL ** -0.5),
        'router_group_w': nrm((L, D_MODEL, N_GROUPS), D_MODEL ** -0.5),
        'router_group_b': nrm((L, N_GROUPS), 0.01),
        'router_expert_w': nrm((L, D_MODEL, N_EXPERTS), D_MODEL ** -0.5),
        'router_expert_b': nrm((L, N_EXPERTS), 0.01),
        'expert_w_gate': nrm((L, N_EXPERTS, D_MODEL, D_EXPERT), D_MODEL ** -0.5),
        'expert_w_up': nrm((L, N_EXPERTS, D_MODEL, D_EXPERT), D_MODEL ** -0.5),
        'expert_w_down': nrm((L, N_EXPERTS, D_EXPERT, D_MODEL), D_EXPERT ** -0.5),
    }

def reference(x, c, ctx, c_ctx, ada_w, ada_b, norm_gains, w_in, conv_w, pool_w, pool_scale,
              pool_proj, w0, w2, a0, a2, g2, k_k, k_a, r_k, lnx_w, lnx_b, rwkv_proj, w_out,
              router_group_w, router_group_b, router_expert_w, router_expert_b,
              expert_w_gate, expert_w_up, expert_w_down):
    b = x.shape[0]
    rows = x.shape[1] // GRID_W
    zero_state = jnp.zeros((b, N_HEADS, HEAD_DIM, HEAD_DIM), jnp.float32)
    h_lat = x.astype(jnp.float32)
    h_ctx = ctx.astype(jnp.float32)
    for l in range(DEPTH):
        last = l == DEPTH - 1
        sh1, sc1, gt1, sh2, sc2, gt2 = jnp.split(
            (jax.nn.silu(c) @ ada_w[l] + ada_b[l])[:, None, :], N_MOD, axis=-1)
        csh1, csc1, cgt1, csh2, csc2, cgt2 = jnp.split(
            (jax.nn.silu(c_ctx) @ ada_w[l] + ada_b[l])[None, None, :], N_MOD, axis=-1)
        rw_params = (w0[l], w2[l], a0[l], a2[l], g2[l], k_k[l], k_a[l], r_k[l], lnx_w[l], lnx_b[l])
        moe_params = (router_group_w[l], router_group_b[l], router_expert_w[l], router_expert_b[l],
                      expert_w_gate[l], expert_w_up[l], expert_w_down[l])

        p_ctx = modulate(rmsnorm(h_ctx, norm_gains[l, 0]), csh1, csc1) @ w_in[l]
        p_lat = modulate(rmsnorm(h_lat, norm_gains[l, 0]), sh1, sc1) @ w_in[l]
        y_ctx_rwkv, ctx_states = rwkv_time_mix(
            short_conv(p_ctx[..., D_POOL:D_POOL + D_CONV], conv_w[l]), (zero_state, zero_state), *rw_params)
        y_lat_rwkv, _ = rwkv_time_mix(
            short_conv(p_lat[..., D_POOL:D_POOL + D_CONV], conv_w[l]), ctx_states, *rw_params)
        m_lat = merge_branches(pool_mix(p_lat[..., :D_POOL], pool_w[l], pool_scale[l], rows), y_lat_rwkv,
                               p_lat[..., D_POOL + D_CONV:], pool_proj[l], rwkv_proj[l], w_out[l])
        h_lat = h_lat + gt1 * rmsnorm(m_lat, norm_gains[l, 1])

        f_lat = hier_moe(modulate(rmsnorm(h_lat, norm_gains[l, 2]), sh2, sc2), *moe_params)
        h_lat = h_lat + gt2 * rmsnorm(f_lat, norm_gains[l, 3])

        if not last:
            m_ctx = merge_branches(pool_mix(p_ctx[..., :D_POOL], pool_w[l], pool_scale[l], None), y_ctx_rwkv,
                                   p_ctx[..., D_POOL + D_CONV:], pool_proj[l], rwkv_proj[l], w_out[l])
            h_ctx = h_ctx + cgt1 * rmsnorm(m_ctx, norm_gains[l, 1])
            f_ctx = hier_moe(modulate(rmsnorm(h_ctx, norm_gains[l, 2]), csh2, csc2), *moe_params)
            h_ctx = h_ctx + cgt2 * rmsnorm(f_ctx, norm_gains[l, 3])
    return h_lat.astype(x.dtype)


_drawn_inputs = setup_inputs


def setup_inputs(seed=0):
    import zlib

    import numpy as np

    out = dict(_drawn_inputs(seed))
    spreads = {}
    factors = {'lnx_b': 3.52}
    for name, (base, spread) in spreads.items():
        noise = np.random.default_rng([zlib.crc32(name.encode()), seed]).standard_normal(out[name].shape)
        drawn = base * np.exp(spread * noise) if base else spread * noise
        out[name] = __import__('jax').numpy.asarray(drawn.astype(out[name].dtype))
    for name, factor in factors.items():
        out[name] = (out[name] * factor).astype(out[name].dtype)
    return out
```

```python
from contextlib import ExitStack

import concourse.bass as bass
import numpy as np
from concourse import mybir

F32 = mybir.dt.float32
U32 = mybir.dt.uint32
I32 = mybir.dt.int32
ALU = mybir.AluOpType
ACT = mybir.ActivationFunctionType
AX = mybir.AxisListType
ds = bass.ds

P = 128
D = 1024
KT = D // P
SEQ, CTX = 512, 256
TOK = CTX + SEQ
HD = 64
C = 64
CTX_CHUNKS, LAT_CHUNKS = CTX // C, SEQ // C
CHUNKS = CTX_CHUNKS + LAT_CHUNKS
GRID_W = 64
WINDOWS = (2, 4, 8, 16)
NG, EPG, NE = 4, 8, 32
FE = 256
GN_EPS, RMS_EPS = 64e-5, 1e-6
DECAY = float(np.exp(-0.5))
ADA_N = 6 * D // 512
NPAR = 16
(P_CR, P_CK, P_CV, P_W0, P_A0, P_KK, P_KA, P_RK) = (0, 3, 6, 9, 11, 13, 14, 15)
PREPW = (3 * KT + 2) * P
LEVELS = (2, 4, 8, 16)

MASKS = ["ident", "heads", "strict_up", "strict_low", "incl_up", "incl_low"]
MASKS += ["before", "ones"]
MASKS += [f"up{b}" for b in (1, 2, 4, 8, 16, 32)] + [f"low{b}" for b in (1, 2, 4, 8, 16, 32)]
NM = len(MASKS)


def mask_table():
    r, c = np.arange(P)[:, None], np.arange(P)[None, :]
    same = (r // HD) == (c // HD)
    t = {"ident": r == c, "heads": same, "strict_up": same & (r < c), "strict_low": same & (r > c),
         "incl_up": same & (r <= c), "incl_low": same & (r >= c),
         "before": r < c, "ones": r + c >= 0}
    for b in (1, 2, 4, 8, 16, 32):
        low = (r // (2 * b) == c // (2 * b)) & (r // b % 2 == 1) & (c // b % 2 == 0)
        t[f"low{b}"], t[f"up{b}"] = low, low.T
    return np.ascontiguousarray(np.stack([t[m] for m in MASKS], 1).astype(np.float32))


def pool_table():
    rows = SEQ // GRID_W

    def mean(n, win):
        lo = win // 2
        hi = win - lo - 1
        m = np.zeros((n, n))
        for t in range(n):
            a, b = max(t - lo, 0), min(t + hi + 1, n)
            m[a:b, t] = 1.0 / (b - a)
        return m

    out = [np.kron(mean(rows, w), mean(GRID_W, w)) - np.eye(SEQ) for w in WINDOWS]
    return np.ascontiguousarray(np.stack(out).reshape(4, SEQ // P, P, SEQ).transpose(0, 2, 1, 3).astype(np.float32))


def flat(ap, at, n):
    names = "abcdefg"[:len(ap.shape)]
    return ap.rearrange(f"{' '.join(names)} -> ({' '.join(names)})")[ds(at, n)]


class Order:

    def __init__(self, sem, names):
        self.sem, self.names, self.at = sem, names, {n: k + 1 for k, n in enumerate(names)}
        self.next = 0

    def done(self, name, ins):
        assert self.names[self.next % len(self.names)] == name, (name, self.names[self.next % len(self.names)])
        self.next += 1
        ins.then_inc(self.sem, 1)

    def value(self, name, i=0):
        return i * len(self.names) + self.at[name]


def modulation(nc, g, I):
    with ExitStack() as ctx:
        sb = lambda n, s, d=F32: ctx.enter_context(nc.sbuf_tensor(n, s, d))
        sem = lambda n: ctx.enter_context(nc.semaphore(n))
        cvec = sb("cvec", [P, 2, KT])
        sig = sb("csig", [P, 2, KT])
        silu = sb("csilu", [P, 2, KT])
        lhs = sb("clhs", [P, 2, KT, P])
        ones = sb("ones_row", [1, P])
        bias = sb("ada_bias", [1, 6 * D])
        w = sb("ada_tile", [P, 2, KT, 512])
        first = sb("mod_first", [P, 2 * D])
        rest = sb("mod_rest", [P, 2, 512])
        gains = sb("mod_gains", [P, 4, D])
        ps = [ctx.enter_context(nc.psum_tensor(f"mod_ps{k}", [P, 512], F32)) for k in range(2)]
        pt = [ctx.enter_context(nc.psum_tensor(f"mod_pt{k}", [P, 4, P], F32)) for k in range(4)]
        small, wload, silu_ready, lhs_ready = sem("small"), [sem("wload0"), sem("wload1")], sem("silu"), sem("lhs")
        block_done, evac, turned, rest_out, mod_ready = sem("block_done"), sem("evac"), sem("turned"), [sem("ro0"), sem("ro1")], sem("mod_ready")
        NF = 2 * D // 512
        with nc.Block() as block:
            @block.sync
            def _(sp):
                sp.dma_start(cvec[:, :, :], I["cvecs"]).then_inc(small, 16)
                sp.dma_start(bias[:, :], I["ada_b"]).then_inc(small, 16)
                sp.dma_start(g["masks"][:, :, :], I["masks"]).then_inc(small, 16)
                sp.dma_start(g["chan"][:, :], I["chan"]).then_inc(small, 16)
                with sp.Fori(0, ADA_N // 2) as i:
                    for u in range(2):
                        at = sp.snap(i * 2 * P * KT * 512 + u * P * KT * 512)
                        sp.wait_ge(block_done, i * 2)
                        sp.dma_start(w[:, u, :, :], flat(I["ada_w"], at, P * KT * 512).rearrange("(p k n) -> p k n", p=P, k=KT)).then_inc(wload[u], 16)

            @block.scalar
            def _(act):
                act.wait_ge(small, 64)
                act.activation(sig[:, :, :], cvec[:, :, :], ACT.Sigmoid).then_inc(silu_ready, 1)

            @block.vector
            def _(dve):
                dve.memset(ones[:, :], 1.0)
                dve.wait_ge(silu_ready, 1)
                dve.tensor_tensor(silu[:, :, :], sig[:, :, :], cvec[:, :, :], ALU.mult)
                dve.drain()
                for h in range(2):
                    dve.tensor_copy(lhs[:, 0, :, h * 64:h * 64 + 64], silu[:, h, :].unsqueeze(2).to_broadcast([P, KT, 64]))
                dve.tensor_copy(lhs[:, 1, :, :], silu[:, 0, :].unsqueeze(2).to_broadcast([P, KT, P]))
                dve.drain().then_inc(lhs_ready, 1)
                for n in range(NF):
                    dve.wait_ge(block_done, n + 1)
                    dve.tensor_copy(first[:, n * 512:n * 512 + 512], ps[n % 2][:, :]).then_inc(evac, 1)
                with dve.Fori(0, (ADA_N - NF) // 2) as i:
                    for u in range(2):
                        dve.wait_ge(block_done, i * 2 + NF + u + 1)
                        dve.wait_ge(rest_out[u], i * 16)
                        dve.tensor_copy(rest[:, u, :], ps[u][:, :]).then_inc(evac, 1)
                for t in range(4):
                    dve.wait_ge(turned, t + 1)
                    dve.tensor_copy(g["mod"][:, t * 4:t * 4 + 4, :], pt[t][:, :, 0::64])
                dve.drain()
                sc, gain = g["mod"][:, KT:2 * KT, :], g["chan"][:, 0:KT].unsqueeze(2).to_broadcast([P, KT, 2])
                dve.scalar_tensor_tensor(out=sc, in0=sc, scalar=1.0, in1=gain, op0=ALU.add, op1=ALU.mult).then_inc(mod_ready, 1)

            @block.tensor
            def _(pe):
                pe.wait_ge(small, 64)
                pe.wait_ge(lhs_ready, 1)

                def one(n, u, which, i=None):
                    pe.wait_ge(wload[u], ((n // 2) + 1) * 16 if i is None else (i + NF // 2 + 1) * 16)
                    for k in range(KT):
                        pe.matmul(ps[u][:, :], lhs[:, which, k, :], w[:, u, k, :], start=(k == 0), stop=False)
                    at = n * 512 if i is None else pe.snap(i * 1024 + (NF + u) * 512)
                    pe.matmul(ps[u][:, :], ones[:, :], bias[:, ds(at, 512)], start=False, stop=True).then_inc(block_done, 1)

                for n in range(NF):
                    if n >= 2:
                        pe.wait_ge(evac, n - 1)
                    one(n, n % 2, 0)
                with pe.Fori(0, (ADA_N - NF) // 2) as i:
                    for u in range(2):
                        pe.wait_ge(evac, i * 2 + NF + u - 1)
                        one(None, u, 1, i)
                pe.wait_ge(evac, NF)
                for t in range(4):
                    for k in range(4):
                        n = (t * 4 + k) * P
                        last = pe.transpose(pt[t][:, k, :], first[:, n:n + P], g["ident"])
                    last.then_inc(turned, 1)

            @block.gpsimd
            def _(pool):
                with pool.Fori(0, (ADA_N - NF) // 2) as i:
                    for u in range(2):
                        blk = pool.snap(i * 1024 + u * 512)
                        pool.wait_ge(evac, i * 2 + NF + u + 1)
                        pool.dma_start(g["mod_rows"][:, ds(blk, 512)], rest[:, u, :]).then_inc(rest_out[u], 16)
                for u in range(2):
                    pool.wait_ge(rest_out[u], (ADA_N - NF) // 2 * 16)


def norm_and_turn(nc, g, I):
    with ExitStack() as ctx:
        sb = lambda n, s, d=F32: ctx.enter_context(nc.sbuf_tensor(n, s, d))
        sem = lambda n: ctx.enter_context(nc.semaphore(n))
        NT = TOK // P
        xs = sb("x_tiles", [P, NT, D])
        xn = sb("x_normed", [P, 2, D])
        sq = sb("x_sq", [P, D])
        st = sb("x_stat", [P, 4, NT])
        tmp = sb("x_tmp", [P, KT, P])
        pt = [ctx.enter_context(nc.psum_tensor(f"x_pt{k}", [P, KT, P], F32)) for k in range(2)]
        loaded = [sem(f"x_loaded{t}") for t in range(NT)]
        summed, root, normed, turned, evac = sem("summed"), sem("root"), sem("normed"), sem("x_turned"), sem("x_evac")
        meaned = sem("meaned")
        with nc.Block() as block:
            @block.sync
            def _(sp):
                for t in range(NT):
                    src = I["ctx"][t * P:t * P + P, :] if t < CTX // P else I["x"][(t - 2) * P:(t - 1) * P, :]
                    sp.dma_start(xs[:, t, :], src).then_inc(loaded[t], 16)

            @block.scalar
            def _(act):
                for t in range(NT):
                    act.wait_ge(loaded[t], 16)
                    act.activation(sq[:, :], xs[:, t, :], ACT.Square, accum_out=st[:, 0, t:t + 1])
                    act.drain().then_inc(summed, 1)
                act.wait_ge(meaned, 1)
                act.activation(st[:, 2, :], st[:, 1, :], ACT.Sqrt).then_inc(root, 1)

            @block.vector
            def _(dve):
                dve.wait_ge(summed, NT)
                dve.tensor_scalar(st[:, 1, :], st[:, 0, :], 1.0 / D, RMS_EPS, ALU.mult, ALU.add).then_inc(meaned, 1)
                dve.wait_ge(root, 1)
                dve.reciprocal(st[:, 3, :], st[:, 2, :])
                dve.drain()
                for t in range(NT + 1):
                    if t < NT:
                        if t >= 2:
                            dve.wait_ge(turned, t - 1)
                        dve.tensor_scalar(xn[:, t % 2, :], xs[:, t, :], st[:, 3, t:t + 1], None, ALU.mult).then_inc(normed, 1)
                    if t >= 1:
                        s = t - 1
                        which = 1 if s < CTX // P else 0
                        scale = g["mod"][:, KT:2 * KT, which:which + 1].to_broadcast([P, KT, P])
                        shift = g["mod"][:, 0:KT, which:which + 1].to_broadcast([P, KT, P])
                        dve.wait_ge(turned, s + 1)
                        dve.tensor_tensor(tmp[:, :, :], pt[s % 2][:, :, :], scale, ALU.mult).then_inc(evac, 1)
                        dve.drain()
                        dve.tensor_tensor(g["hT"][:, :, s * P:s * P + P], tmp[:, :, :], shift, ALU.add)
                        dve.drain()

            @block.tensor
            def _(pe):
                for t in range(NT):
                    pe.wait_ge(normed, t + 1)
                    if t >= 2:
                        pe.wait_ge(evac, t - 1)
                    for k in range(KT):
                        last = pe.transpose(pt[t % 2][:, k, :], xn[:, t % 2, k * P:k * P + P], g["ident"])
                    last.then_inc(turned, 1)


def low_rank_inputs(nc, g, I):
    with ExitStack() as ctx:
        sb = lambda n, s, d=F32: ctx.enter_context(nc.sbuf_tensor(n, s, d))
        sem = lambda n: ctx.enter_context(nc.semaphore(n))
        w = sb("lr_w", [P, 3, KT, P])
        y = sb("lr_y", [P, 3, TOK])
        ps = [[ctx.enter_context(nc.psum_tensor(f"lr_ps{j}{k}", [P, 512], F32)) for k in range(2)] for j in range(3)]
        wl, mm, cv = sem("lr_loaded"), sem("lr_mm"), sem("lr_conv")
        hT, xw, xa, xg, chan = g["hT"], g["xw"], g["xa"], g["xg"], g["chan"]
        with nc.Block() as block:
            @block.sync
            def _(sp):
                sp.dma_start(w[:, :, :, :], I["w_lr"]).then_inc(wl, 16)

            @block.tensor
            def _(pe):
                pe.wait_ge(wl, 16)
                for j in range(3):
                    for part, (a, n) in enumerate(((CTX, SEQ), (0, CTX))):
                        if j == 2 and part == 1:
                            continue
                        for k in range(KT):
                            last = pe.matmul(ps[j][part][:, 0:n], w[:, j, k, :], hT[:, k, a:a + n], start=(k == 0), stop=(k == KT - 1))
                    last.then_inc(mm, 1)

            @block.vector
            def _(dve):
                for z in (xw, xa):
                    dve.memset(z[:, :, :], 0.0)
                dve.drain()
                for j in range(3):
                    dve.wait_ge(mm, j + 1)
                    tap = lambda q: chan[:, 16 + 3 * j + q:17 + 3 * j + q]
                    for part, (a, n) in enumerate(((CTX, SEQ), (0, CTX))):
                        if j == 2 and part == 1:
                            continue
                        s = ps[j][part]
                        dve.tensor_scalar(y[:, j, a:a + n], s[:, 0:n], tap(1), None, ALU.mult)
                        dve.drain()
                        dve.scalar_tensor_tensor(out=y[:, j, a + 1:a + n], in0=s[:, 0:n - 1], scalar=tap(0), in1=y[:, j, a + 1:a + n], op0=ALU.mult, op1=ALU.add)
                        dve.drain()
                        dve.scalar_tensor_tensor(out=y[:, j, a:a + n - 1], in0=s[:, 1:n], scalar=tap(2), in1=y[:, j, a:a + n - 1], op0=ALU.mult, op1=ALU.add)
                        dve.drain()
                    dve.drain().then_inc(cv, 1)
                for d in range(2):
                    h = slice(64 * d, 64 * d + 64)
                    dve.tensor_copy(xa[h, d, :], y[h, 1, :])

            @block.scalar
            def _(act):
                act.wait_ge(cv, 1)
                for d in range(2):
                    h = slice(64 * d, 64 * d + 64)
                    act.activation(xw[h, d, :], y[h, 0, :], ACT.Tanh)
                act.wait_ge(cv, 3)
                act.activation(xg[:, :], y[:, 2, CTX:TOK], ACT.Sigmoid)


def prepare(nc, g, I):
    with ExitStack() as ctx:
        sb = lambda n, s, d=F32: ctx.enter_context(nc.sbuf_tensor(n, s, d))
        sem = lambda n: ctx.enter_context(nc.semaphore(n))
        w = sb("pr_w", [P, 2, PREPW])
        par = sb("pr_par", [P, 2, NPAR])
        rk = sb("pr_rk", [P, P])
        r, k, v = sb("pr_r", [P, TOK]), sb("pr_k", [P, TOK]), sb("pr_v", [P, TOK])
        kraw, ksq, kk = sb("pr_kraw", [P, TOK]), sb("pr_ksq", [P, TOK]), sb("pr_kk", [P, TOK])
        norm, rnorm = sb("pr_norm", [P, TOK]), sb("pr_rnorm", [P, TOK])
        s_dec, rate = sb("pr_s", [P, 2, TOK]), sb("pr_rate", [P, 2, TOK])
        reset = sb("pr_reset", [P, 2, CHUNKS, C])
        cum, cumx = sb("pr_cum", [P, 2, TOK]), sb("pr_cumx", [P, 2, TOK])
        e_in, e_out, e_prev = (sb(f"pr_e{j}", [P, TOK]) for j in range(3))
        kd, bb = sb("pr_kd", [P, 2, TOK]), sb("pr_bb", [P, TOK])
        k_ka, k_rest = sb("pr_kka", [P, TOK]), sb("pr_krest", [P, TOK])
        rkd = sb("pr_rkd", [P, SEQ])
        KR = sb("pr_KR", [P, 2, CHUNKS, 2, C])
        BK = sb("pr_BK", [P, 2, CHUNKS, 2, C])
        one_less = sb("pr_1ka", [P, 1])
        bank = [ctx.enter_context(nc.psum_tensor(f"pr_ps{j}", [P, 512], F32)) for j in range(8)]
        B_R, B_K, B_V, B_KC, B_VC = bank[0:5]
        LRB = [(B_R, bank[5]), (bank[6], bank[7])]
        wload = [sem("pr_wl0"), sem("pr_wl1")]
        pe_s, act_s, dve_s, pool_s = sem("pr_pe"), sem("pr_act"), sem("pr_dve"), sem("pr_pool")
        stored = [sem("pr_st0"), sem("pr_st1")]
        vstored = sem("pr_vst")
        hT, heads, ident = g["hT"], g["mask"]("heads"), g["ident"]
        pe_o = Order(pe_s, ["r", "k", "v", "w0", "a0", "w1", "a1", "norm", "bonus"])
        act_o = Order(act_s, ["tap_r", "tap_k", "tap_v", "sig_w0", "sig_a0", "sig_w1", "sig_a1", "ksq", "root",
                              "exp0", "exp1"])
        dve_o = Order(dve_s, ["conv_r", "conv_k", "conv_v", "kraw", "kk", "cum0", "cum1", "dec0",
                              "kds", "dec1", "bonus", "rk"])
        pool_o = Order(pool_s, ["kd0", "kd1"])
        lat = slice(CTX, TOK)
        parts = ((CTX, SEQ), (0, CTX))

        def body(u):
            wv = w[:, u, :].rearrange("p (j n) -> p j n", n=P)
            pr = lambda q: par[:, u, q:q + 1]
            return wv, pr

        with nc.Block() as block:
            @block.sync
            def _(sp):
                for u in range(2):
                    sp.dma_start(w[:, u, :], I["w_prep"][u]).then_inc(wload[u], 16)
                    sp.dma_start(par[:, u, :], I["p_prep"][u]).then_inc(wload[u], 16)

                NV, NO = CHUNKS * P * C, CHUNKS * P * 2 * C

                def store(m, at, at_v):
                    sp.wait_ge(dve_s, m * len(dve_o.names) + dve_o.at["conv_v"])
                    sp.dma_start(flat(g["v_dram"], at_v, NV).rearrange("(c p t) -> p c t", c=CHUNKS, p=P),
                                 v[:, :].rearrange("p (c t) -> p c t", t=C)).then_inc(vstored, 16)
                    for d in range(2):
                        sp.wait_ge(dve_s, m * len(dve_o.names) + dve_o.at[f"dec{d}"])
                        for dst, src in ((g["kr_dram"], KR), (g["bk_dram"], BK)):
                            sp.dma_start(flat(dst[d], at, NO).rearrange("(c p t) -> p c t", c=CHUNKS, p=P),
                                         src[:, d, :, :, :].rearrange("p c b t -> p c (b t)")).then_inc(stored[d], 16)

                with sp.Fori(0, KT // 2 - 1) as i:
                    for u in range(2):
                        m = i * 2 + u
                        at, at_v = sp.snap(i * 2 * NO + u * NO), sp.snap(i * 2 * NV + u * NV)
                        nxt_w = sp.snap(i * 2 * P * PREPW + (u + 2) * P * PREPW)
                        nxt_p = sp.snap(i * 2 * P * NPAR + (u + 2) * P * NPAR)
                        store(m, at, at_v)
                        sp.wait_ge(dve_s, m * len(dve_o.names) + dve_o.at["rk"])
                        sp.dma_start(w[:, u, :], flat(I["w_prep"], nxt_w, P * PREPW).rearrange("(p n) -> p n", p=P)).then_inc(wload[u], 16)
                        sp.dma_start(par[:, u, :], flat(I["p_prep"], nxt_p, P * NPAR).rearrange("(p n) -> p n", p=P)).then_inc(wload[u], 16)
                for m in (KT - 2, KT - 1):
                    store(m, m * NO, m * NV)
                for u in range(2):
                    sp.wait_ge(stored[u], KT * 32)
                sp.wait_ge(vstored, KT * 16)

            @block.tensor
            def _(pe):
                with pe.Fori(0, KT // 2) as i:
                    for u in range(2):
                        wv, pr = body(u)
                        m = i * 2 + u
                        base = lambda o: m * len(o.names)
                        pe.wait_ge(wload[u], (i + 1) * 32)

                        def project(j, lat_bank, ctx_bank, name):
                            for kt in range(KT):
                                last = pe.matmul(lat_bank[:, :], wv[:, j * KT + kt, :], hT[:, kt, lat], start=(kt == 0), stop=(kt == KT - 1))
                            if ctx_bank is not None:
                                for kt in range(KT):
                                    last = pe.matmul(ctx_bank[:, 0:CTX], wv[:, j * KT + kt, :], hT[:, kt, 0:CTX], start=(kt == 0), stop=(kt == KT - 1))
                            pe_o.done(name, last)

                        pe.wait_ge(dve_s, base(dve_o))
                        project(0, B_R, None, "r")
                        project(1, B_K, B_KC, "k")
                        project(2, B_V, B_VC, "v")
                        for q, (name, maps, src, d) in enumerate((("w0", 0, g["xw"], 0), ("a0", 1, g["xa"], 0), ("w1", 0, g["xw"], 1), ("a1", 1, g["xa"], 1))):
                            if q == 0:
                                pe.wait_ge(dve_s, base(dve_o) + dve_o.at["conv_r"])
                            if q >= 2:
                                pe.wait_ge(act_s, base(act_o) + act_o.at[("sig_w0", "sig_a0")[q - 2]])
                            for part, (a, n) in enumerate(parts):
                                last = pe.matmul(LRB[q % 2][part][:, 0:n], wv[:, 3 * KT + maps, :], src[:, d, a:a + n], start=True, stop=True)
                            pe_o.done(name, last)
                        pe.wait_ge(act_s, base(act_o) + act_o.at["ksq"])
                        for part, (a, n) in enumerate(parts):
                            last = pe.matmul(LRB[0][part][:, 0:n], heads, ksq[:, a:a + n], start=True, stop=True)
                        pe_o.done("norm", last)
                        pe.wait_ge(dve_s, base(dve_o) + dve_o.at["kds"])
                        last = pe.matmul(LRB[1][0][:, :], rk[:, :], rkd[:, :], start=True, stop=True)
                        pe_o.done("bonus", last)

            @block.scalar
            def _(act):
                with act.Fori(0, KT // 2) as i:
                    for u in range(2):
                        wv, pr = body(u)
                        m = i * 2 + u
                        base = lambda o: m * len(o.names)
                        act.wait_ge(wload[u], (i + 1) * 32)
                        act.wait_ge(dve_s, base(dve_o))
                        act.wait_ge(pool_s, base(pool_o))
                        act.wait_ge(vstored, m * 16)
                        for name, y, b, bc, q in (("r", r, B_R, None, P_CR), ("k", k, B_K, B_KC, P_CK), ("v", v, B_V, B_VC, P_CV)):
                            act.wait_ge(pe_s, base(pe_o) + pe_o.at[name])
                            last = act.activation(y[:, lat], b[:, :], ACT.Copy, scale=pr(q + 1))
                            if bc is not None:
                                last = act.activation(y[:, 0:CTX], bc[:, 0:CTX], ACT.Copy, scale=pr(q + 1))
                            act_o.done(f"tap_{name}", last)
                        for q, (name, y, d, p0) in enumerate((("w0", s_dec, 0, P_W0), ("a0", rate, 0, P_A0), ("w1", s_dec, 1, P_W0 + 1), ("a1", rate, 1, P_A0 + 1))):
                            act.wait_ge(pe_s, base(pe_o) + pe_o.at[name])
                            for part, (a, n) in enumerate(parts):
                                last = act.activation(y[:, d, a:a + n], LRB[q % 2][part][:, 0:n], ACT.Sigmoid, bias=pr(p0))
                            act_o.done(f"sig_{name}", last)
                        act.wait_ge(dve_s, base(dve_o) + dve_o.at["kraw"])
                        act_o.done("ksq", act.activation(ksq[:, :], kraw[:, :], ACT.Square))
                        act.wait_ge(pe_s, base(pe_o) + pe_o.at["norm"])
                        for part, (a, n) in enumerate(parts):
                            last = act.activation(norm[:, a:a + n], LRB[0][part][:, 0:n], ACT.Sqrt)
                        act_o.done("root", last)
                        for d in range(2):
                            act.wait_ge(dve_s, base(dve_o) + dve_o.at[f"cum{d}"])
                            if d:
                                act.wait_ge(dve_s, base(dve_o) + dve_o.at["dec0"])
                            act.activation(e_in[:, :], cum[:, d, :], ACT.Exp, scale=-DECAY)
                            act.activation(e_out[:, :], cum[:, d, :], ACT.Exp, scale=DECAY)
                            act_o.done(f"exp{d}", act.activation(e_prev[:, :], cumx[:, d, :], ACT.Exp, scale=-DECAY))

            @block.gpsimd
            def _(pool):
                with pool.Fori(0, KT // 2) as i:
                    for u in range(2):
                        wv, pr = body(u)
                        m = i * 2 + u
                        base = lambda o: m * len(o.names)
                        pool.wait_ge(dve_s, base(dve_o) + dve_o.at["kraw"])
                        for d in range(2):
                            pool.wait_ge(act_s, base(act_o) + act_o.at[f"sig_a{d}"])
                            pool.tensor_tensor(kd[:, d, :], rate[:, d, :], k_ka[:, :], ALU.mult)
                            pool.drain()
                            pool_o.done(f"kd{d}", pool.tensor_tensor(kd[:, d, :], kd[:, d, :], k_rest[:, :], ALU.add))

            @block.vector
            def _(dve):
                dve.memset(reset[:, :, :, :], 1.0)
                dve.memset(KR[:, :, 0:CTX_CHUNKS, 1, :], 0.0)
                dve.drain()
                dve.memset(reset[:, 0, :, 0:1], 0.0)
                dve.memset(reset[:, 1, :, C - 1:C], 0.0)
                dve.drain()
                with dve.Fori(0, KT // 2) as i:
                    for u in range(2):
                        wv, pr = body(u)
                        m = i * 2 + u
                        base = lambda o: m * len(o.names)
                        mreg = dve.snap(i * 2 + u)
                        dve.wait_ge(wload[u], (i + 1) * 32)
                        dve.tensor_scalar(one_less[:, :], pr(P_KA), -1.0, 1.0, ALU.mult, ALU.add)
                        for name, y, b, bc, q in (("r", r, B_R, None, P_CR), ("k", k, B_K, B_KC, P_CK), ("v", v, B_V, B_VC, P_CV)):
                            dve.wait_ge(act_s, base(act_o) + act_o.at[f"tap_{name}"])
                            todo = [(b, 0, CTX, SEQ)] + ([(bc, 0, 0, CTX)] if bc is not None else [])
                            for tap in (0, 2):
                                for s, o, a, n in todo:
                                    dst = y[:, a + 1:a + n] if tap == 0 else y[:, a:a + n - 1]
                                    src = s[:, o:o + n - 1] if tap == 0 else s[:, o + 1:o + n]
                                    last = dve.scalar_tensor_tensor(out=dst, in0=src, scalar=pr(q + tap), in1=dst, op0=ALU.mult, op1=ALU.add)
                                if tap == 0:
                                    dve.drain()
                            dve_o.done(f"conv_{name}", last)
                        dve.drain()
                        dve.tensor_scalar(k_ka[:, :], k[:, :], pr(P_KA), None, ALU.mult)
                        dve.tensor_scalar(k_rest[:, :], k[:, :], one_less[:, 0:1], None, ALU.mult)
                        dve_o.done("kraw", dve.tensor_scalar(kraw[:, :], k[:, :], pr(P_KK), None, ALU.mult))
                        dve.wait_ge(act_s, base(act_o) + act_o.at["root"])
                        dve.tensor_scalar(norm[:, :], norm[:, :], 1e-12, None, ALU.max)
                        dve.drain()
                        dve.reciprocal(rnorm[:, :], norm[:, :])
                        dve.drain()
                        dve_o.done("kk", dve.tensor_tensor(kk[:, :], kraw[:, :], rnorm[:, :], ALU.mult))
                        for d in range(2):
                            f = slice(None, None, 1 if d == 0 else -1)
                            rs = reset[:, d, :, :].rearrange("p c t -> p (c t)")
                            dve.tensor_tensor_scan(cum[:, d, f], rs[:, f], s_dec[:, d, f], 0.0, ALU.mult, ALU.add)
                            dve.drain()
                            dve_o.done(f"cum{d}", dve.tensor_tensor(cumx[:, d, :], cum[:, d, :], s_dec[:, d, :], ALU.subtract))
                        for d in range(2):
                            chunks = lambda x: x.rearrange("p (c t) -> p c t", t=C)
                            dve.wait_ge(act_s, base(act_o) + act_o.at[f"exp{d}"])
                            dve.wait_ge(stored[d], m * 32)
                            dve.tensor_tensor(KR[:, d, :, 0, :], chunks(kk[:, :]), chunks(e_prev[:, :]), ALU.mult)
                            dve.tensor_tensor(KR[:, d, CTX_CHUNKS:, 1, :], chunks(r[:, lat]), chunks(e_in[:, lat]), ALU.mult)
                            dve.tensor_tensor(bb[:, :], kk[:, :], rate[:, d, :], ALU.mult)
                            dve.tensor_copy(g["decay_end"][:, d, :, ds(mreg, 1)], chunks(e_in[:, :])[:, :, (C - 1) * (1 - d):(C - 1) * (1 - d) + 1])
                            dve.drain()
                            dve.tensor_tensor(BK[:, d, :, 0, :], chunks(bb[:, :]), chunks(e_out[:, :]), ALU.mult)
                            dve.wait_ge(pool_s, base(pool_o) + pool_o.at[f"kd{d}"])
                            dve_o.done(f"dec{d}", dve.tensor_tensor(BK[:, d, :, 1, :], chunks(kd[:, d, :]), chunks(e_out[:, :]), ALU.mult))
                            if d == 0:
                                dve.tensor_scalar(rk[:, :], heads, pr(P_RK), None, ALU.mult)
                                dve.wait_ge(pool_s, base(pool_o) + pool_o.at["kd1"])
                                dve.tensor_tensor(rkd[:, :], kd[:, 0, lat], kd[:, 1, lat], ALU.add)
                                dve.drain()
                                dve.tensor_tensor(rkd[:, :], rkd[:, :], r[:, lat], ALU.mult)
                                dve.drain()
                                dve_o.done("kds", dve.engine_nop())
                        dve.wait_ge(pe_s, base(pe_o) + pe_o.at["bonus"])
                        dve_o.done("bonus", dve.tensor_tensor(g["bonus"][:, ds(mreg, 1), :], LRB[1][0][:, :].unsqueeze(1), v[:, lat].unsqueeze(1), ALU.mult))
                        dve.drain()
                        dve_o.done("rk", dve.engine_nop())


def recurrence(nc, g, part, S, yn):
    n = (CTX_CHUNKS, LAT_CHUNKS)[part]
    first = (0, CTX_CHUNKS)[part]
    with_y = part == 1
    H = KT // 2
    with ExitStack() as ctx:
        sb = lambda nm, s, d=F32: ctx.enter_context(nc.sbuf_tensor(f"{nm}_{part}", s, d))
        sem = lambda nm: ctx.enter_context(nc.semaphore(f"{nm}_{part}"))
        KR = [sb(f"rc_KR{d}", [P, KT, 2, C]) for d in range(2)]
        inputs = ["K", "B", "Kh", "V"] + ["R"] * with_y
        bd = [{x: sb(f"rc_{x}bd{d}", [P, KT, P]) for x in inputs} for d in range(2)]
        mats = ["M", "Aak", "Bt", "Kt", "Vt", "T", "Tt", "G", "U"] + ["Arb", "Ark"] * with_y
        W = {x: sb(f"rc_{x}", [P, KT, P]) for x in mats}
        PC = sb("rc_PC", [P, 2, KT])
        if with_y:
            Y, Yc, Yq, Rs = (sb(f"rc_y{j}", [P, KT, C]) for j in range(4))
        bank = [ctx.enter_context(nc.psum_tensor(f"rc_ps{j}_{part}", [P, H, P], F32)) for j in range(8)]
        loaded = [sem("rc_loaded0"), sem("rc_loaded1")]
        pe_s, act_s, dve_s = sem("rc_pe"), sem("rc_act"), sem("rc_dve")
        cleared, x_seen = sem("rc_cleared"), sem("rc_x_seen")

        stages = ["B", "Kh", "Bt", "Kt", "Vt", "T1"]
        for b in LEVELS:
            stages += [f"G{b}", f"X{b}", f"Tt{b}"]
        stages += ["G32", "X32", "X", "U"] + ["Y"] * with_y + ["S"]
        tail = ["mean", "var"] * with_y
        by_act = {"Bt", "Kt", "Vt", "T1", "X", "U"} | {f"G{b}" for b in (*LEVELS, 32)} | {f"Tt{b}" for b in LEVELS}
        both = lambda names: [f"{s}.{h}" for s in names for h in range(2)]
        pe_names = [f"{x}@{d}" for d in range(2) for x in both(stages) + tail]
        act_names = [f"{x}@{d}" for d in range(2) for x in both([s for s in stages if s in by_act]) + ["sq", "root"] * with_y]
        dve_names = [f"{x}@{d}" for d in range(2) for x in
                     both(["B", "Kh", "Tt1"] + [f"X{b}" for b in (*LEVELS, 32)] + ["Y"] * with_y) + (["cen", "gn"] if with_y else [])
                     + both(["S"])]
        pe_o, act_o, dve_o = Order(pe_s, pe_names), Order(act_s, act_names), Order(dve_s, dve_names)
        spots = {x: j % 4 for j, x in enumerate(stages)}

        def ps(stage, h):
            return bank[2 * spots[stage] + h]

        sets = [("strict_up", "incl_up", "up1", "low", "up32"), ("strict_low", "incl_low", "low1", "up", "low32")]
        half = lambda x, h: x[:, H * h:H * h + H, :]
        nload = 1 + 2 * len(inputs)

        with nc.Block() as block:
            @block.sync
            def _(sp):
                sp.wait_ge(cleared, 1)

                def load(d, chunk, used):
                    at_o, at_v = chunk
                    NO, NV = P * 2 * C, P * C
                    kr = g["kr_dram"][d][:, ds(at_o, NO)].rearrange("i (p b t) -> p i b t", p=P, b=2)
                    bk = g["bk_dram"][d][:, ds(at_o, NO)].rearrange("i (p b t) -> p i b t", p=P, b=2)
                    vv = g["v_dram"][:, ds(at_v, NV)].rearrange("i (p t) -> p i t", p=P)
                    if used is not None:
                        sp.wait_ge(pe_s, used)
                    sp.dma_start(KR[d][:, :, :, :].rearrange("p i b t -> p i (b t)"), kr.rearrange("p i b t -> p i (b t)")).then_inc(loaded[d], 16)
                    for hh in range(2):
                        q = slice(64 * hh, 64 * hh + 64)
                        src = {"K": kr[q, :, 0, :], "B": bk[q, :, 0, :], "Kh": bk[q, :, 1, :], "V": vv[q, :, :]}
                        if with_y:
                            src["R"] = kr[q, :, 1, :]
                        for x in inputs:
                            sp.dma_start(bd[d][x][q, :, q], src[x]).then_inc(loaded[d], 16)

                for d in range(2):
                    c = first if d == 0 else first + n - 1
                    load(d, (c * P * 2 * C, c * P * C), None)
                with sp.Fori(0, n - 1) as i:
                    for d in range(2):
                        if d == 0:
                            at = sp.snap(i * (P * 2 * C) + (first + 1) * P * 2 * C), sp.snap(i * (P * C) + (first + 1) * P * C)
                        else:
                            top = first + n - 2
                            at = sp.snap(i * (-P * 2 * C) + top * P * 2 * C), sp.snap(i * (-P * C) + top * P * C)
                        used = sp.snap(i * len(pe_names) + pe_o.at[f"S.1@{d}"])
                        load(d, at, used)

            @block.tensor
            def _(pe):
                pe.wait_ge(cleared, 1)
                with pe.Fori(0, n) as i:
                    for d in range(2):
                        ins = bd[d]
                        at = lambda o, name: i * len(o.names) + o.at[f"{name}@{d}"]
                        act_at = lambda name: at(act_o, name)
                        dve_at = lambda name: at(dve_o, name)
                        I_ = g["ident"]

                        def free(stage, h):
                            j = stages.index(stage)
                            if j < 4:
                                return
                            old = stages[j - 4]
                            if old in by_act:
                                pe.wait_ge(act_s, act_at(f"{old}.{h}"))
                            else:
                                pe.wait_ge(dve_s, dve_at(f"{old}.{h}"))

                        def products(stage, h, terms):
                            out = ps(stage, h)
                            for q in range(H):
                                p = H * h + q
                                for j, (lhs, rhs) in enumerate(terms):
                                    last = pe.matmul(out[:, q, :], lhs(p), rhs(p), start=(j == 0), stop=(j == len(terms) - 1))
                            pe_o.done(f"{stage}.{h}@{d}", last)

                        def turns(stage, h, src):
                            out = ps(stage, h)
                            for q in range(H):
                                last = pe.transpose(out[:, q, :], src[:, H * h + q, :], I_)
                            pe_o.done(f"{stage}.{h}@{d}", last)

                        m = lambda x: (lambda p: x[:, p, :])
                        pe.wait_ge(loaded[d], (i + 1) * 16 * nload)
                        if d == 1:
                            pe.wait_ge(dve_s, i * len(dve_names) + dve_o.at["S.1@0"])
                            pe.wait_ge(act_s, i * len(act_names) + len(act_names) // 2)
                        else:
                            pe.wait_ge(dve_s, i * len(dve_names))
                            pe.wait_ge(act_s, i * len(act_names))
                        for h in range(2):
                            products("B", h, [(m(ins["B"]), lambda p: KR[d][:, p, :, :].rearrange("p b t -> p (b t)"))])
                        for h in range(2):
                            products("Kh", h, [(m(ins["Kh"]), lambda p: KR[d][:, p, :, :].rearrange("p b t -> p (b t)"))])
                        for stage, x in (("Bt", "B"), ("Kt", "Kh"), ("Vt", "V")):
                            for h in range(2):
                                free(stage, h)
                                turns(stage, h, ins[x])
                        for h in range(2):
                            free("T1", h)
                            pe.wait_ge(dve_s, dve_at(f"Tt1.{h}"))
                            turns("T1", h, W["Tt"])
                        for b in (*LEVELS, 32):
                            for h in range(2):
                                free(f"G{b}", h)
                                if b == 2:
                                    pe.wait_ge(act_s, act_at(f"T1.{h}"))
                                else:
                                    pe.wait_ge(dve_s, dve_at(f"X{b // 2}.{h}"))
                                products(f"G{b}", h, [(m(W["M"]), m(W["T"]))])
                            for h in range(2):
                                free(f"X{b}", h)
                                pe.wait_ge(act_s, act_at(f"G{b}.{h}"))
                                if b < 32:
                                    products(f"X{b}", h, [(m(W["Tt"]), m(W["G"]))])
                                else:
                                    products(f"X{b}", h, [(m(W["G"]), m(W["Tt"]))])
                            if b < 32:
                                for h in range(2):
                                    free(f"Tt{b}", h)
                                    pe.wait_ge(dve_s, dve_at(f"X{b}.{h}"))
                                    turns(f"Tt{b}", h, W["T"])
                        for h in range(2):
                            free("X", h)
                            products("X", h, [(m(ins["K"]), m(S[d])), (m(W["Aak"]), m(W["Vt"]))])
                        for h in range(2):
                            free("U", h)
                            pe.wait_ge(dve_s, dve_at(f"X32.{h}"))
                            pe.wait_ge(act_s, act_at(f"X.{h}"))
                            products("U", h, [(m(W["Tt"]), m(W["G"]))])
                        if with_y:
                            for h in range(2):
                                free("Y", h)
                                pe.wait_ge(act_s, act_at(f"U.{h}"))
                                products("Y", h, [(m(S[d]), m(ins["R"])), (m(W["U"]), m(W["Arb"])), (m(W["Vt"]), m(W["Ark"]))])
                        for h in range(2):
                            free("S", h)
                            pe.wait_ge(act_s, act_at(f"U.{h}"))
                            products("S", h, [(m(W["Bt"]), m(W["U"])), (m(W["Kt"]), m(W["Vt"]))])
                        if with_y:
                            pe.wait_ge(dve_s, dve_at("Y.1"))
                            out = ps("U", 0)[:, :, :].rearrange("p a b -> p (a b)")
                            pe_o.done(f"mean@{d}", pe.matmul(out, g["mean_w"], Y[:, :, :].rearrange("p a b -> p (a b)"), start=True, stop=True))
                            pe.wait_ge(act_s, act_at("sq"))
                            pe_o.done(f"var@{d}", pe.matmul(out, g["mean_w"], Yq[:, :, :].rearrange("p a b -> p (a b)"), start=True, stop=True))

            @block.scalar
            def _(act):
                with act.Fori(0, n) as i:
                    for d in range(2):
                        pe_at = lambda name: i * len(pe_names) + pe_o.at[f"{name}@{d}"]

                        def copy(stage, h, dst, scale=1.0):
                            act.wait_ge(pe_s, pe_at(f"{stage}.{h}"))
                            act_o.done(f"{stage}.{h}@{d}", act.activation(half(dst, h), ps(stage, h)[:, :, :], ACT.Copy, scale=scale))

                        for stage, dst in (("Bt", "Bt"), ("Kt", "Kt"), ("Vt", "Vt"), ("T1", "T")):
                            for h in range(2):
                                copy(stage, h, W[dst])
                        for b in (*LEVELS, 32):
                            for h in range(2):
                                copy(f"G{b}", h, W["G"], -1.0)
                            if b < 32:
                                for h in range(2):
                                    copy(f"Tt{b}", h, W["Tt"])
                        for h in range(2):
                            copy("X", h, W["G"])
                        for h in range(2):
                            copy("U", h, W["U"], -1.0)
                        if with_y:
                            act.wait_ge(dve_s, i * len(dve_names) + dve_o.at[f"cen@{d}"])
                            act_o.done(f"sq@{d}", act.activation(Yq[:, :, :], Yc[:, :, :], ACT.Square))
                            act.wait_ge(pe_s, pe_at("var"))
                            act_o.done(f"root@{d}", act.activation(Rs[:, :, :].rearrange("p a b -> p (a b)"),
                                                                   ps("U", 0)[:, :, :].rearrange("p a b -> p (a b)"), ACT.Sqrt, bias=g["gn_eps"]))

            @block.vector
            def _(dve):
                for d in range(2):
                    for x in inputs:
                        dve.memset(bd[d][x][:, :, :], 0.0)
                dve.drain().then_inc(cleared, 1)
                with dve.Fori(0, n) as i:
                    for d in range(2):
                        strict, incl, lvl1, lvl, last_lvl = sets[d]
                        pe_at = lambda name: i * len(pe_names) + pe_o.at[f"{name}@{d}"]
                        chunk = dve.snap(i + first) if d == 0 else dve.snap(i * -1 + (first + n - 1))
                        col = None
                        if with_y:
                            col = dve.snap(i * C) if d == 0 else dve.snap(i * -C + (n - 1) * C)
                        mask = lambda nm: g["mask"](nm).unsqueeze(1).to_broadcast([P, H, P])
                        wide = lambda nm: g["mask"](nm).rearrange("p (a t) -> p a t", a=2).unsqueeze(1).to_broadcast([P, H, 2, C])
                        spread = lambda x: x.unsqueeze(2).to_broadcast([P, H, 2, C])
                        four = lambda x: x.rearrange("p h (a t) -> p h a t", a=2)
                        dve.tensor_copy(PC[:, d, :], g["decay_end"][:, d, ds(chunk, 1), :].rearrange("p a i -> p (a i)"))
                        for stage, first_m, second_m in (("B", "M", "Arb"), ("Kh", "Aak", "Ark")):
                            for h in range(2):
                                dve.wait_ge(pe_s, pe_at(f"{stage}.{h}"))
                                src = ps(stage, h)
                                ins_ = dve.tensor_tensor(four(half(W[first_m], h)), spread(src[:, :, 0:C]), wide(strict), ALU.mult)
                                if with_y:
                                    ins_ = dve.tensor_tensor(four(half(W[second_m], h)), spread(src[:, :, C:P]), wide(incl), ALU.mult)
                                dve_o.done(f"{stage}.{h}@{d}", ins_)
                        dve.drain()
                        for h in range(2):
                            dve.tensor_tensor(half(W["Tt"], h), half(W["M"], h), mask(lvl1), ALU.mult)
                            dve.drain()
                            dve_o.done(f"Tt1.{h}@{d}", dve.scalar_tensor_tensor(
                                out=half(W["Tt"], h), in0=half(W["Tt"], h), scalar=-1.0, in1=mask("ident"), op0=ALU.mult, op1=ALU.add))
                        for b in (*LEVELS, 32):
                            dst = W["T"] if b < 32 else W["Tt"]
                            for h in range(2):
                                dve.wait_ge(pe_s, pe_at(f"X{b}.{h}"))
                                dve.sem_inc(x_seen, 1)
                                mk = mask(f"{lvl}{b}" if b < 32 else last_lvl).bitcast(U32)
                                dve_o.done(f"X{b}.{h}@{d}", dve.copy_predicated(half(dst, h), mk, ps(f"X{b}", h)[:, :, :]))
                        if with_y:
                            for h in range(2):
                                dve.wait_ge(pe_s, pe_at(f"Y.{h}"))
                                for hh in range(2):
                                    q = slice(64 * hh, 64 * hh + 64)
                                    last = dve.tensor_copy(Y[q, H * h:H * h + H, :], ps("Y", h)[q, :, q])
                                dve_o.done(f"Y.{h}@{d}", last)
                            dve.wait_ge(pe_s, pe_at("mean"))
                            dve_o.done(f"cen@{d}", dve.tensor_tensor(Yc[:, :, :], Y[:, :, :], ps("U", 0)[:, :, :].rearrange("p a b -> p (a b)").rearrange("p (i t) -> p i t", t=C), ALU.subtract))
                            dve.wait_ge(act_s, i * len(act_names) + act_o.at[f"root@{d}"])
                            dve.reciprocal(Rs[:, :, :], Rs[:, :, :])
                            dve.drain()
                            dve_o.done(f"gn@{d}", dve.tensor_tensor(yn[d][:, :, ds(col, C)], Yc[:, :, :], Rs[:, :, :], ALU.mult))
                        for h in range(2):
                            dve.wait_ge(pe_s, pe_at(f"S.{h}"))
                            dve.tensor_tensor(half(S[d], h), half(S[d], h), ps("S", h)[:, :, :], ALU.add)
                            dve.drain()
                            dve_o.done(f"S.{h}@{d}", dve.tensor_tensor(half(S[d], h), half(S[d], h), PC[:, d, H * h:H * h + H].unsqueeze(2).to_broadcast([P, H, P]), ALU.mult))


def read_out(nc, g, I, yn):
    with ExitStack() as ctx:
        sb = lambda n, s, d=F32: ctx.enter_context(nc.sbuf_tensor(n, s, d))
        sem = lambda n: ctx.enter_context(nc.semaphore(n))
        g2, b2 = sb("ro_g2", [P, D]), sb("ro_b2", [P, KT])
        ps = [ctx.enter_context(nc.psum_tensor(f"ro_ps{k}", [P, SEQ], F32)) for k in range(KT)]
        loaded, gate = sem("ro_loaded"), sem("ro_gate")
        chan = g["chan"]
        with nc.Block() as block:
            @block.sync
            def _(sp):
                sp.dma_start(g2[:, :], I["g2"]).then_inc(loaded, 16)

            @block.tensor
            def _(pe):
                pe.wait_ge(loaded, 16)
                for i in range(KT):
                    pe.matmul(ps[i][:, :], g2[:, i * P:i * P + P], g["xg"][:, :], start=True, stop=True).then_inc(gate, 1)

            @block.vector
            def _(dve):
                dve.tensor_scalar(b2[:, :], chan[:, 33:41], 2.0, None, ALU.mult)
                y = yn[0]
                dve.tensor_tensor(y[:, :, :], y[:, :, :], yn[1][:, :, :], ALU.add)
                dve.drain()
                for i in range(KT):
                    dve.tensor_scalar(y[:, i, :], y[:, i, :], chan[:, 25 + i:26 + i], b2[:, i:i + 1], ALU.mult, ALU.add)
                dve.drain()
                dve.tensor_tensor(y[:, :, :], y[:, :, :], g["bonus"][:, :, :], ALU.add)
                dve.drain()
                for i in range(KT):
                    dve.wait_ge(gate, i + 1)
                    dve.tensor_tensor(y[:, i, :], y[:, i, :], ps[i][:, :], ALU.mult)


def pooling(nc, g, I, py):
    NT = SEQ // P
    with ExitStack() as ctx:
        sb = lambda n, s, d=F32: ctx.enter_context(nc.sbuf_tensor(n, s, d))
        sem = lambda n: ctx.enter_context(nc.semaphore(n))
        w, pw = sb("pl_w", [P, KT, 512]), sb("pl_pw", [P, 4, P])
        u = sb("pl_u", [P, NT, 512])
        box = sb("pl_box", [P, 2, NT, SEQ])
        diff = sb("pl_diff", [P, 2, SEQ])
        ps = [ctx.enter_context(nc.psum_tensor(f"pl_ps{k}", [P, SEQ], F32)) for k in range(8)]
        loaded, boxed = sem("pl_loaded"), [sem("pl_box0"), sem("pl_box1")]
        u_ps, u_sb, d_ps, d_sb, y_ps = sem("pl_u_ps"), sem("pl_u_sb"), sem("pl_d_ps"), sem("pl_d_sb"), sem("pl_y_ps")
        with nc.Block() as block:
            @block.sync
            def _(sp):
                sp.dma_start(w[:, :, :], I["w_pool"]).then_inc(loaded, 16)
                sp.dma_start(pw[:, :, :], I["pool_w"]).then_inc(loaded, 16)
                for j in range(4):
                    if j >= 2:
                        sp.wait_ge(d_ps, j - 1)
                    sp.dma_start(box[:, j % 2, :, :], I["pool_box"][j]).then_inc(boxed[j % 2], 16)

            @block.tensor
            def _(pe):
                pe.wait_ge(loaded, 32)
                for t in range(NT):
                    for k in range(KT):
                        last = pe.matmul(ps[t][:, :], g["hT"][:, k, CTX + t * P:CTX + t * P + P], w[:, k, :], start=(k == 0), stop=(k == KT - 1))
                    last.then_inc(u_ps, 1)
                pe.wait_ge(u_sb, NT)
                for j in range(4):
                    pe.wait_ge(boxed[j % 2], 16 * (j // 2 + 1))
                    for t in range(NT):
                        last = pe.matmul(ps[4 + j % 2][:, :], u[:, t, j * P:j * P + P], box[:, j % 2, t, :], start=(t == 0), stop=(t == NT - 1))
                    last.then_inc(d_ps, 1)
                    pe.wait_ge(d_sb, j + 1)
                    pe.matmul(ps[j][:, :], pw[:, j, :], diff[:, j % 2, :], start=True, stop=True).then_inc(y_ps, 1)

            @block.vector
            def _(dve):
                for t in range(NT):
                    dve.wait_ge(u_ps, t + 1)
                    dve.tensor_copy(u[:, t, :], ps[t][:, :]).then_inc(u_sb, 1)
                for j in range(4):
                    dve.wait_ge(d_ps, j + 1)
                    if j >= 2:
                        dve.wait_ge(y_ps, j - 1)
                    dve.tensor_copy(diff[:, j % 2, :], ps[4 + j % 2][:, :]).then_inc(d_sb, 1)

            @block.scalar
            def _(act):
                for j in range(4):
                    act.wait_ge(y_ps, j + 1)
                    act.activation(py[:, j, :], ps[j][:, :], ACT.Copy, scale=g["chan"][:, 41 + j:42 + j])


MG = 2 * KT + 4 + KT


def merge(nc, g, I, py, ry, merged):
    with ExitStack() as ctx:
        sb = lambda n, s, d=F32: ctx.enter_context(nc.sbuf_tensor(n, s, d))
        sem = lambda n: ctx.enter_context(nc.semaphore(n))
        w = sb("mg_w", [P, 2, MG, P])
        sig = sb("mg_sig", [P, 2, 2, SEQ])
        ps = [[ctx.enter_context(nc.psum_tensor(f"mg_ps{u}{k}", [P, SEQ], F32)) for k in range(4)] for u in range(2)]
        loaded = [sem("mg_loaded0"), sem("mg_loaded1")]
        pe_s, act_s, dve_s = sem("mg_pe"), sem("mg_act"), sem("mg_dve")
        pe_o = Order(pe_s, ["gp", "gr", "pp", "rp"])
        act_o = Order(act_s, ["gp", "gr"])
        dve_o = Order(dve_s, ["pp", "rp", "out"])
        hT = g["hT"]
        NW = P * MG * P
        with nc.Block() as block:
            @block.sync
            def _(sp):
                for u in range(2):
                    sp.dma_start(w[:, u, :, :], I["w_merge"][u].rearrange("p (m n) -> p m n", m=MG)).then_inc(loaded[u], 16)
                with sp.Fori(0, KT // 2 - 1) as i:
                    for u in range(2):
                        at = sp.snap(i * 2 * NW + (u + 2) * NW)
                        sp.wait_ge(pe_s, i * 8 + 4 * u + 4)
                        sp.dma_start(w[:, u, :, :], flat(I["w_merge"], at, NW).rearrange("(p m n) -> p m n", p=P, m=MG)).then_inc(loaded[u], 16)

            @block.tensor
            def _(pe):
                with pe.Fori(0, KT // 2) as i:
                    for u in range(2):
                        m = i * 2 + u
                        pe.wait_ge(loaded[u], (i + 1) * 16)
                        pe.wait_ge(dve_s, i * 6)
                        for name, w0, n, src in (("gp", 0, KT, None), ("gr", KT, KT, None), ("pp", 2 * KT, 4, py), ("rp", 2 * KT + 4, KT, ry)):
                            for k in range(n):
                                rhs = hT[:, k, CTX:TOK] if src is None else src[:, k, :]
                                last = pe.matmul(ps[u]["gp gr pp rp".split().index(name)][:, :], w[:, u, w0 + k, :], rhs, start=(k == 0), stop=(k == n - 1))
                            pe_o.done(name, last)

            @block.scalar
            def _(act):
                with act.Fori(0, KT // 2) as i:
                    for u in range(2):
                        m = i * 2 + u
                        for k, name in enumerate(("gp", "gr")):
                            act.wait_ge(pe_s, m * 4 + k + 1)
                            if k == 0:
                                act.wait_ge(dve_s, i * 6)
                            act_o.done(name, act.activation(sig[:, u, k, :], ps[u][k][:, :], ACT.Sigmoid))

            @block.vector
            def _(dve):
                with dve.Fori(0, KT // 2) as i:
                    for u in range(2):
                        m = i * 2 + u
                        mr = dve.snap(i * 2 + u)
                        for k, name in enumerate(("pp", "rp")):
                            dve.wait_ge(act_s, m * 2 + k + 1)
                            dve.wait_ge(pe_s, m * 4 + 3 + k)
                            dve_o.done(name, dve.tensor_tensor(sig[:, u, k, :], sig[:, u, k, :], ps[u][2 + k][:, :], ALU.mult))
                        dve.drain()
                        dve_o.done("out", dve.tensor_tensor(merged[:, ds(mr, 1), :], sig[:, u, 0:1, :], sig[:, u, 1:2, :], ALU.add))


def project_out(nc, g, I, merged, x1, logits):
    NT = SEQ // P
    with ExitStack() as ctx:
        sb = lambda n, s, d=F32: ctx.enter_context(nc.sbuf_tensor(n, s, d))
        sem = lambda n: ctx.enter_context(nc.semaphore(n))
        w = sb("po_w", [P, KT, D])
        rows = sb("po_rows", [P, 3, D])
        gains = sb("po_gains", [P, 2, D])
        rw, rb = sb("po_rw", [P, KT, 36]), sb("po_rb", [1, 36])
        sq = sb("po_sq", [P, D])
        f = sb("po_f", [P, 2, D])
        fT = sb("po_fT", [P, 2, KT, P])
        st = sb("po_st", [P, NT, 8])
        ps = [ctx.enter_context(nc.psum_tensor(f"po_ps{k}", [P, D], F32)) for k in range(2)]
        pt = ctx.enter_context(nc.psum_tensor("po_pt", [P, KT, P], F32))
        pl = ctx.enter_context(nc.psum_tensor("po_pl", [P, NT, P], F32))
        loaded, xload = sem("po_loaded"), sem("po_x")
        rows_ready = sem("po_rows_ready")
        pe_m, pe_t, pe_l = sem("po_product"), sem("po_turned"), sem("po_logits")
        act_sum, act_root, act_fT = sem("po_sum"), sem("po_root"), sem("po_fT_ready")
        dve_mean, dve_x, dve_f = sem("po_mean"), sem("po_x1"), sem("po_f_ready")
        fst = [sem("po_fst0"), sem("po_fst1")]
        with nc.Block() as block:
            @block.sync
            def _(sp):
                sp.dma_start(w[:, :, :], I["w_out"]).then_inc(loaded, 16)
                sp.dma_start(rw[:, :, :], I["router_w"]).then_inc(loaded, 16)
                sp.dma_start(rb[:, :], I["router_b"]).then_inc(loaded, 16)
                sp.dma_start(rows[:, :, :], g["mod_rows"][:, 0:3 * D].rearrange("p (a n) -> p a n", a=3)).then_inc(loaded, 16)
                for j in range(2):
                    sp.dma_start(gains[:, j, :], I["gains"][j:j + 1, :].to_broadcast([P, D])).then_inc(loaded, 16)
                for t in range(NT):
                    sp.dma_start(x1[:, t, :], I["x"][t * P:t * P + P, :]).then_inc(xload, 16)
                for t in range(NT):
                    sp.wait_ge(dve_f, t + 1)
                    sp.dma_start(g["f_dram"][t * P:t * P + P, :], f[:, t % 2, :]).then_inc(fst[t % 2], 16)
                for u in range(2):
                    sp.wait_ge(fst[u], NT // 2 * 16)

            @block.tensor
            def _(pe):
                pe.wait_ge(loaded, 96)

                def product(t):
                    if t >= 2:
                        pe.wait_ge(dve_x, t - 1)
                    for h in range(2):
                        for k in range(KT):
                            last = pe.matmul(ps[t % 2][:, h * 512:h * 512 + 512], merged[:, k, t * P:t * P + P], w[:, k, h * 512:h * 512 + 512], start=(k == 0), stop=(k == KT - 1))
                    last.then_inc(pe_m, 1)

                def turn(t):
                    pe.wait_ge(dve_f, t + 1)
                    if t:
                        pe.wait_ge(act_fT, t)
                    for k in range(KT):
                        last = pe.transpose(pt[:, k, :], f[:, t % 2, k * P:k * P + P], g["ident"])
                    last.then_inc(pe_t, 1)

                def route(t):
                    pe.wait_ge(act_fT, t + 1)
                    for k in range(KT):
                        pe.matmul(pl[:, t, 0:36], fT[:, t % 2, k, :], rw[:, k, :], start=(k == 0), stop=False)
                    pe.matmul(pl[:, t, 0:36], g["mask"]("ones")[0:1, :], rb[:, :], start=False, stop=True).then_inc(pe_l, 1)

                product(0)
                for t in range(NT):
                    if t + 1 < NT:
                        product(t + 1)
                    turn(t)
                    route(t)

            @block.scalar
            def _(act):
                for t in range(NT):
                    act.wait_ge(pe_m, t + 1)
                    act.activation(sq[:, :], ps[t % 2][:, :], ACT.Square, accum_out=st[:, t, 0:1])
                    act.drain().then_inc(act_sum, 1)
                    act.wait_ge(dve_mean, 2 * t + 1)
                    act.activation(st[:, t, 2:3], st[:, t, 1:2], ACT.Sqrt).then_inc(act_root, 1)
                    act.wait_ge(dve_x, t + 1)
                    act.activation(sq[:, :], x1[:, t, :], ACT.Square, accum_out=st[:, t, 4:5])
                    act.drain().then_inc(act_sum, 1)
                    act.wait_ge(dve_mean, 2 * t + 2)
                    act.activation(st[:, t, 6:7], st[:, t, 5:6], ACT.Sqrt).then_inc(act_root, 1)
                    act.wait_ge(pe_t, t + 1)
                    if t >= 2:
                        act.wait_ge(pe_l, t - 1)
                    act.activation(fT[:, t % 2, :, :], pt[:, :, :], ACT.Copy).then_inc(act_fT, 1)

            @block.vector
            def _(dve):
                dve.wait_ge(loaded, 96)
                dve.tensor_tensor(rows[:, 0, :], rows[:, 0, :], gains[:, 0, :], ALU.mult)
                dve.scalar_tensor_tensor(out=rows[:, 2, :], in0=rows[:, 2, :], scalar=1.0, in1=gains[:, 1, :], op0=ALU.add, op1=ALU.mult)
                dve.wait_ge(xload, NT * 16)
                dve.drain()
                for t in range(NT):
                    dve.wait_ge(act_sum, 2 * t + 1)
                    dve.tensor_scalar(st[:, t, 1:2], st[:, t, 0:1], 1.0 / D, RMS_EPS, ALU.mult, ALU.add).then_inc(dve_mean, 1)
                    dve.wait_ge(act_root, 2 * t + 1)
                    dve.reciprocal(st[:, t, 3:4], st[:, t, 2:3])
                    dve.drain()
                    if t >= 2:
                        dve.wait_ge(pe_t, t - 1)
                        dve.wait_ge(fst[t % 2], 16 * (t // 2))
                    ft = f[:, t % 2, :]
                    dve.scalar_tensor_tensor(out=ft, in0=ps[t % 2][:, :], scalar=st[:, t, 3:4], in1=rows[:, 0, :], op0=ALU.mult, op1=ALU.mult)
                    dve.drain()
                    dve.tensor_tensor(x1[:, t, :], x1[:, t, :], ft, ALU.add).then_inc(dve_x, 1)
                    dve.wait_ge(act_sum, 2 * t + 2)
                    dve.tensor_scalar(st[:, t, 5:6], st[:, t, 4:5], 1.0 / D, RMS_EPS, ALU.mult, ALU.add).then_inc(dve_mean, 1)
                    dve.wait_ge(act_root, 2 * t + 2)
                    dve.reciprocal(st[:, t, 7:8], st[:, t, 6:7])
                    dve.drain()
                    dve.scalar_tensor_tensor(out=ft, in0=x1[:, t, :], scalar=st[:, t, 7:8], in1=rows[:, 2, :], op0=ALU.mult, op1=ALU.mult)
                    dve.drain()
                    dve.tensor_tensor(ft, ft, rows[:, 1, :], ALU.add).then_inc(dve_f, 1)
                dve.wait_ge(pe_l, NT)
                dve.tensor_copy(logits[:, :, :], pl[:, :, 0:36])


SLOTS = P
SPILL = 7
TILES = NE + SPILL
EXPERT_W = KT * 2 * FE + 2 * D


def route(nc, g, logits, R):
    NT = SEQ // P
    with ExitStack() as ctx:
        sb = lambda n, s, d=F32: ctx.enter_context(nc.sbuf_tensor(n, s, d))
        sem = lambda n: ctx.enter_context(nc.semaphore(n))
        t4 = lambda n: sb(n, [P, NT, 4])
        t8 = lambda n: sb(n, [P, NT, 8])
        t32 = lambda n: sb(n, [P, NT, NE])
        m1, s1 = sb("rt_m1", [P, NT, 1]), sb("rt_s1", [P, NT, 1])
        eg, tg, gh = t4("rt_eg"), t4("rt_tg"), t4("rt_gh")
        sel, te, oh1, oh2, msk = t8("rt_sel"), t8("rt_te"), t8("rt_oh1"), t8("rt_oh2"), t8("rt_msk")
        e32, O1, O2, both, pre, tmp = (t32(f"rt_x{j}") for j in range(6))
        ma, mb, e2, w1 = (sb(f"rt_m{j}", [P, NT, 1]) for j in "abcd")
        rev = sb("rt_rev", [P, 8])
        base, cnt, over, tmpc, incl = (sb(f"rt_c{j}", [P, NE]) for j in range(5))
        zero = sb("rt_zero", [P, TILES])
        zero_rows = sb("rt_zero_rows", [P, D])
        ovq = sb("rt_ovq", [P, SPILL])
        tokid = sb("rt_tokid", [P, NT])
        table = sb("rt_table", [TILES, P])
        ps = ctx.enter_context(nc.psum_tensor("rt_ps", [P, NT + 1, NE], F32))
        pt = ctx.enter_context(nc.psum_tensor("rt_pt", [P, TILES], F32))
        ex, ex_done, cst, both_ready, pref = sem("rt_exp_in"), sem("rt_exp"), sem("rt_cst"), sem("rt_both"), sem("rt_prefix")
        zeroed, slots_ready, scattered, tab, turned = sem("rt_zeroed"), sem("rt_slots"), sem("rt_scattered"), sem("rt_tab"), sem("rt_turned")
        rows_cleared = sem("rt_rows_cleared")
        X = AX.X
        with nc.Block() as block:
            @block.sync
            def _(sp):
                sp.wait_ge(cst, 1)
                for q in range(SPILL):
                    sp.dma_start(g["y_dram"][(NE + q) * SLOTS:(NE + q + 1) * SLOTS, :], zero_rows[:, :]).then_inc(rows_cleared, 16)
                sp.wait_ge(rows_cleared, SPILL * 16)

            @block.gpsimd
            def _(pool):
                pool.iota(rev[:, :], [[-1, 8]], base=8, channel_multiplier=0, allow_small_or_imprecise_dtypes=True)
                pool.iota(base[:, :], [[SLOTS, NE]], base=0, channel_multiplier=0, allow_small_or_imprecise_dtypes=True)
                pool.iota(tokid[:, :], [[P, NT]], base=0, channel_multiplier=1, allow_small_or_imprecise_dtypes=True)
                pool.memset(zero[:, :], 0.0)
                pool.memset(zero_rows[:, :], 0.0)
                pool.drain().then_inc(cst, 1)
                pool.wait_ge(cst, 1)
                pool.dma_start(g["slot_tok"].rearrange("(p n) a -> p (n a)", p=P), zero[:, :]).then_inc(zeroed, 16)
                pool.wait_ge(zeroed, 16)
                pool.wait_ge(slots_ready, 1)
                for t in range(NT):
                    for j in range(2):
                        pool.indirect_dma_start(out=g["slot_tok"], out_offset=bass.IndirectOffsetOnAxis(ap=R["slot"][:, j, t:t + 1], axis=0),
                                                in_=tokid[:, t:t + 1], in_offset=None).then_inc(scattered, 16)
                pool.wait_ge(scattered, 2 * NT * 16)
                pool.dma_start(table[:, :], g["slot_tok"].rearrange("(t s) a -> t (s a)", t=TILES)).then_inc(tab, 16)

            @block.scalar
            def _(act):
                act.wait_ge(ex, 1)
                act.activation(eg[:, :, :], tg[:, :, :], ACT.Exp).then_inc(ex_done, 1)
                act.wait_ge(ex, 2)
                act.activation(e2[:, :, :], mb[:, :, :], ACT.Exp).then_inc(ex_done, 1)

            @block.tensor
            def _(pe):
                pe.wait_ge(both_ready, 1)
                for t in range(NT + 1):
                    for q in range(t):
                        last = pe.matmul(ps[:, t, :], g["mask"]("ones"), both[:, q, :], start=(q == 0), stop=(t == NT and q == t - 1))
                    if t < NT:
                        last = pe.matmul(ps[:, t, :], g["mask"]("before"), both[:, t, :], start=(t == 0), stop=True)
                last.then_inc(pref, 1)
                pe.wait_ge(tab, 16)
                pe.transpose(pt[:, :], table[:, :], g["ident"][0:TILES, 0:TILES]).then_inc(turned, 1)

            @block.vector
            def _(dve):
                def tt(o, a, b, op):
                    dve.tensor_tensor(o, a, b, op)
                    dve.drain()

                def ts(o, a, s0, s1_, op0, op1=ALU.bypass):
                    dve.tensor_scalar(o, a, s0, s1_, op0, op1)
                    dve.drain()

                def red(o, a, op):
                    dve.tensor_reduce(o, a, X, op)
                    dve.drain()

                def first_hot(out, score, best, n, tmp_):
                    red(best, score, ALU.max)
                    tt(tmp_, score, best.to_broadcast([P, NT, n]), ALU.is_equal)
                    tt(tmp_, tmp_, rev[:, 8 - n:8].unsqueeze(1).to_broadcast([P, NT, n]), ALU.mult)
                    red(s1[:, :, :], tmp_, ALU.max)
                    tt(out, tmp_, s1[:, :, :].to_broadcast([P, NT, n]), ALU.is_equal)

                gl = logits[:, :, 0:4]
                el = logits[:, :, 4:36]
                dve.wait_ge(cst, 1)
                first_hot(gh[:, :, :], gl, m1[:, :, :], 4, tg[:, :, :])
                tt(tg[:, :, :], gl, m1[:, :, :].to_broadcast([P, NT, 4]), ALU.subtract)
                dve.drain().then_inc(ex, 1)
                for q in range(4):
                    src = el[:, :, 8 * q:8 * q + 8]
                    if q == 0:
                        tt(sel[:, :, :], src, gh[:, :, 0:1].to_broadcast([P, NT, 8]), ALU.mult)
                    else:
                        tt(te[:, :, :], src, gh[:, :, q:q + 1].to_broadcast([P, NT, 8]), ALU.mult)
                        tt(sel[:, :, :], sel[:, :, :], te[:, :, :], ALU.add)
                first_hot(oh1[:, :, :], sel[:, :, :], ma[:, :, :], 8, te[:, :, :])
                dve.scalar_tensor_tensor(out=msk[:, :, :], in0=oh1[:, :, :], scalar=-3.0e38, in1=sel[:, :, :], op0=ALU.mult, op1=ALU.add)
                dve.drain()
                first_hot(oh2[:, :, :], msk[:, :, :], mb[:, :, :], 8, te[:, :, :])
                tt(mb[:, :, :], mb[:, :, :], ma[:, :, :], ALU.subtract)
                dve.drain().then_inc(ex, 1)
                for o, oh in ((O1, oh1), (O2, oh2)):
                    for q in range(4):
                        dve.tensor_tensor(o[:, :, 8 * q:8 * q + 8], oh[:, :, :], gh[:, :, q:q + 1].to_broadcast([P, NT, 8]), ALU.mult)
                dve.drain()
                tt(both[:, :, :], O1[:, :, :], O2[:, :, :], ALU.add)
                dve.drain().then_inc(both_ready, 1)
                dve.wait_ge(ex_done, 2)
                red(m1[:, :, :], eg[:, :, :], ALU.add)
                dve.reciprocal(m1[:, :, :], m1[:, :, :])
                ts(w1[:, :, :], e2[:, :, :], 1.0, None, ALU.add)
                dve.reciprocal(w1[:, :, :], w1[:, :, :])
                dve.drain()
                gate = lambda j: R["gate"][:, j, :].unsqueeze(2)
                tt(gate(0), m1[:, :, :], w1[:, :, :], ALU.mult)
                tt(gate(1), gate(0), e2[:, :, :], ALU.mult)
                dve.wait_ge(pref, 1)
                dve.tensor_copy(pre[:, :, :], ps[:, 0:NT, :])
                dve.tensor_copy(cnt[:, :], ps[:, NT, :])
                dve.drain()
                ts(over[:, :], cnt[:, :], float(SLOTS), None, ALU.is_gt)
                for j in (2, 3):
                    dve.scalar_tensor_tensor(out=over[:, :], in0=cnt[:, :], scalar=float(j * SLOTS), in1=over[:, :], op0=ALU.is_gt, op1=ALU.add)
                    dve.drain()
                ts(tmpc[:, :], over[:, :], 0.0, 1.0, ALU.mult, ALU.add)
                dve.tensor_tensor_scan(incl[:, :], tmpc[:, :], over[:, :], 0.0, ALU.mult, ALU.add)
                dve.drain()
                for q in range(SPILL):
                    dve.tensor_scalar(tmpc[:, :], incl[:, :], float(q), None, ALU.is_le)
                    dve.drain()
                    dve.tensor_reduce(ovq[:, q:q + 1], tmpc[:, :], X, ALU.add)
                    dve.drain()
                ts(ovq[:, :], ovq[:, :], float(NE - 1), None, ALU.min)
                dve.tensor_copy(R["spill_expert"][:, :], ovq[:, :])
                dve.tensor_copy(R["spill_tiles"][:, :], incl[:, NE - 1:NE])
                tt(tmpc[:, :], incl[:, :], over[:, :], ALU.subtract)
                ts(tmpc[:, :], tmpc[:, :], float(SLOTS), float((NE - 1) * SLOTS), ALU.mult, ALU.add)
                tt(tmpc[:, :], tmpc[:, :], base[:, :], ALU.subtract)
                ts(tmp[:, :, :], pre[:, :, :], float(SLOTS), None, ALU.is_ge)
                tt(tmp[:, :, :], tmp[:, :, :], tmpc[:, :].unsqueeze(1).to_broadcast([P, NT, NE]), ALU.mult)
                tt(pre[:, :, :], pre[:, :, :], tmp[:, :, :], ALU.add)
                tt(pre[:, :, :], pre[:, :, :], base[:, :].unsqueeze(1).to_broadcast([P, NT, NE]), ALU.add)
                for j, o in enumerate((O1, O2)):
                    tt(o[:, :, :], o[:, :, :], pre[:, :, :], ALU.mult)
                    red(s1[:, :, :], o[:, :, :], ALU.add)
                    dve.tensor_copy(R["slot"][:, j, :], s1[:, :, :].rearrange("p t a -> p (t a)"))
                    dve.drain()
                dve.drain().then_inc(slots_ready, 1)
                dve.wait_ge(turned, 1)
                dve.tensor_copy(R["tok"][:, :], pt[:, :])


def experts(nc, g, I, R):
    with ExitStack() as ctx:
        sb = lambda n, s, d=F32: ctx.enter_context(nc.sbuf_tensor(n, s, d))
        sem = lambda n: ctx.enter_context(nc.semaphore(n))
        w = sb("ex_w", [P, 2, EXPERT_W])
        idx = sb("ex_idx", [P, 2, 1], U32)
        xe = sb("ex_x", [P, 2, D])
        xT = sb("ex_xT", [P, 2, KT, P])
        sg = sb("ex_sig", [P, 2, FE])
        h = sb("ex_h", [P, 2, FE])
        hT = sb("ex_hT", [P, 2, 2, P])
        y = sb("ex_y", [P, 2, D])
        p_x = ctx.enter_context(nc.psum_tensor("ex_px", [P, KT, P], F32))
        p_gu = [ctx.enter_context(nc.psum_tensor(f"ex_pgu{u}", [P, 2 * FE], F32)) for u in range(2)]
        p_h = [ctx.enter_context(nc.psum_tensor(f"ex_ph{u}", [P, 2, P], F32)) for u in range(2)]
        p_y = ctx.enter_context(nc.psum_tensor("ex_py", [P, D], F32))
        NWE = P * EXPERT_W
        gu = lambda u: w[:, u, 0:KT * 2 * FE].rearrange("p (k n) -> p k n", k=KT)
        dn = lambda u: w[:, u, KT * 2 * FE:].rearrange("p (k n) -> p k n", k=2)

        def run(tag, pairs, spill):
            wl, gath, yst = [sem(f"{tag}_w{u}") for u in range(2)], [sem(f"{tag}_g{u}") for u in range(2)], [sem(f"{tag}_y{u}") for u in range(2)]
            s = {n: sem(f"{tag}_{n}") for n in ("turned", "xT", "gu", "sig", "h", "hturned", "hT", "down", "y", "idx", "seen", "seen2", "stored")}
            U = 1 if spill else 2
            with nc.Block() as block:
                def loop(eng, body):
                    if not spill:
                        with eng.Fori(0, pairs) as i:
                            for u in range(2):
                                body(i, u, i * 2 + u)
                    else:
                        count = eng.value_load(R["spill_tiles"][0:1, 0:1], min_val=0, max_val=SPILL)
                        with eng.Fori(0, SPILL) as i:
                            with eng.If(count > i):
                                body(i, 0, i)

                @block.sync
                def _(sp):
                    def body(i, u, t):
                        if spill:
                            e = sp.value_load(R["spill_expert"][0:1, ds(i, 1)], min_val=0, max_val=NE - 1)
                            at = sp.snap(e * NWE)
                            at_y = sp.snap(i * (SLOTS * D) + NE * SLOTS * D)
                            sp.wait_ge(s["down"], i)
                        else:
                            at = sp.snap(i * 2 * NWE + u * NWE)
                            at_y = sp.snap(i * 2 * SLOTS * D + u * SLOTS * D)
                            sp.wait_ge(s["down"], i * 2 + u - 1 if u else i * 2)
                        return at, at_y

                    def load(u, at):
                        sp.dma_start(w[:, u, :], flat(I["w_experts"], at, NWE).rearrange("(p n) -> p n", p=P)).then_inc(wl[u], 16)

                    def store(u, at_y):
                        sp.dma_start(flat(g["y_dram"], at_y, SLOTS * D).rearrange("(p n) -> p n", p=P), y[:, u, :]).then_inc(yst[u], 16)

                    if spill:
                        def one(i, u, t):
                            at, at_y = body(i, u, t)
                            load(0, at)
                            sp.wait_ge(s["y"], i + 1)
                            store(0, at_y)
                            sp.wait_ge(yst[0], i * 16 + 16)
                            sp.sem_inc(s["stored"], 1)
                        loop(sp, one)
                    else:
                        for u in range(2):
                            load(u, u * NWE)
                        with sp.Fori(0, pairs - 1) as i:
                            for u in range(2):
                                at = sp.snap(i * 2 * NWE + (u + 2) * NWE)
                                at_y = sp.snap(i * 2 * SLOTS * D + u * SLOTS * D)
                                sp.wait_ge(s["down"], i * 2 + u + 1)
                                load(u, at)
                                sp.wait_ge(s["y"], i * 2 + u + 1)
                                store(u, at_y)
                        for u in range(2):
                            t = 2 * pairs - 2 + u
                            sp.wait_ge(s["y"], t + 1)
                            store(u, t * SLOTS * D)
                        for u in range(2):
                            sp.wait_ge(yst[u], pairs * 16)

                @block.gpsimd
                def _(pool):
                    def body(i, u, t):
                        tile = pool.snap(i + NE) if spill else pool.snap(i * 2 + u)
                        if spill:
                            pool.wait_ge(s["turned"], i)
                        else:
                            pool.wait_ge(s["turned"], i * 2)
                        pool.sem_inc(s["seen"], 1)
                        pool.tensor_copy(idx[:, u, :], R["tok"][:, ds(tile, 1)]).then_inc(s["idx"], 1)
                        pool.wait_ge(s["idx"], i * U + u + 1)
                        pool.sem_inc(s["seen2"], 1)
                        pool.indirect_dma_start(out=xe[:, u, :], out_offset=None, in_=g["f_dram"],
                                                in_offset=bass.IndirectOffsetOnAxis(ap=idx[:, u, 0:1], axis=0)).then_inc(gath[u], 16)
                    loop(pool, body)

                @block.tensor
                def _(pe):
                    def turn(i, u, t):
                        pe.wait_ge(gath[u], (i + 1) * 16)
                        pe.wait_ge(s["xT"], t)
                        for k in range(KT):
                            last = pe.transpose(p_x[:, k, :], xe[:, u, k * P:k * P + P], g["ident"])
                        last.then_inc(s["turned"], 1)

                    def tile(i, u, t, nxt):
                        pe.wait_ge(wl[u], (i + 1) * 16)
                        pe.wait_ge(s["xT"], t + 1)
                        if spill:
                            pe.wait_ge(s["h"], t)
                        else:
                            pe.wait_ge(s["h"], i * 2)
                        for k in range(KT):
                            last = pe.matmul(p_gu[u][:, :], xT[:, u, k, :], gu(u)[:, k, :], start=(k == 0), stop=(k == KT - 1))
                        last.then_inc(s["gu"], 1)
                        if nxt is not None:
                            turn(*nxt)
                        pe.wait_ge(s["h"], t + 1)
                        for k in range(2):
                            last = pe.transpose(p_h[u][:, k, :], h[:, u, k * P:k * P + P], g["ident"])
                        last.then_inc(s["hturned"], 1)
                        pe.wait_ge(s["hT"], t + 1)
                        pe.wait_ge(s["y"], t)
                        for q in range(2):
                            for k in range(2):
                                last = pe.matmul(p_y[:, q * 512:q * 512 + 512], hT[:, u, k, :], dn(u)[:, k, q * 512:q * 512 + 512], start=(k == 0), stop=(k == 1))
                        last.then_inc(s["down"], 1)

                    if spill:
                        def one(i, u, t):
                            turn(i, 0, i)
                            tile(i, 0, i, None)
                        loop(pe, one)
                    else:
                        turn(0, 0, 0)
                        with pe.Fori(0, pairs - 1) as i:
                            tile(i, 0, i * 2, (i, 1, i * 2 + 1))
                            tile(i, 1, i * 2 + 1, (i + 1, 0, i * 2 + 2))
                        i = pairs - 1
                        tile(i, 0, i * 2, (i, 1, i * 2 + 1))
                        tile(i, 1, i * 2 + 1, None)

                @block.scalar
                def _(act):
                    def body(i, u, t):
                        act.wait_ge(s["turned"], t + 1)
                        act.wait_ge(s["gu"], i if spill else i * 2)
                        act.activation(xT[:, u, :, :], p_x[:, :, :], ACT.Copy).then_inc(s["xT"], 1)
                        act.wait_ge(s["gu"], t + 1)
                        act.wait_ge(s["h"], i if spill else i * 2)
                        act.activation(sg[:, u, :], p_gu[u][:, 0:FE], ACT.Sigmoid).then_inc(s["sig"], 1)
                        act.wait_ge(s["down"], t + 1)
                        act.wait_ge(yst[u], i * 16)
                        act.activation(y[:, u, :], p_y[:, :], ACT.Copy).then_inc(s["y"], 1)

                    if spill:
                        loop(act, body)
                        return

                    def xt(i, u, t, guard):
                        act.wait_ge(s["turned"], t + 1)
                        if guard is not None:
                            act.wait_ge(s["gu"], guard)
                        act.activation(xT[:, u, :, :], p_x[:, :, :], ACT.Copy).then_inc(s["xT"], 1)

                    def rest(i, u, t, nxt):
                        act.wait_ge(s["gu"], t + 1)
                        act.wait_ge(s["h"], i * 2)
                        act.activation(sg[:, u, :], p_gu[u][:, 0:FE], ACT.Sigmoid).then_inc(s["sig"], 1)
                        if nxt is not None:
                            xt(*nxt)
                        act.wait_ge(s["down"], t + 1)
                        act.wait_ge(yst[u], i * 16)
                        act.activation(y[:, u, :], p_y[:, :], ACT.Copy).then_inc(s["y"], 1)

                    xt(0, 0, 0, None)
                    with act.Fori(0, pairs - 1) as i:
                        rest(i, 0, i * 2, (i, 1, i * 2 + 1, i * 2))
                        rest(i, 1, i * 2 + 1, (i + 1, 0, i * 2 + 2, i * 2 + 1))
                    i = pairs - 1
                    rest(i, 0, i * 2, (i, 1, i * 2 + 1, i * 2))
                    rest(i, 1, i * 2 + 1, None)

                @block.vector
                def _(dve):
                    def body(i, u, t):
                        dve.wait_ge(s["sig"], t + 1)
                        dve.wait_ge(s["hturned"], i if spill else i * 2)
                        dve.tensor_tensor(sg[:, u, :], sg[:, u, :], p_gu[u][:, 0:FE], ALU.mult)
                        dve.drain()
                        dve.tensor_tensor(h[:, u, :], sg[:, u, :], p_gu[u][:, FE:2 * FE], ALU.mult).then_inc(s["h"], 1)
                        dve.wait_ge(s["hturned"], t + 1)
                        dve.wait_ge(s["down"], i if spill else i * 2)
                        dve.tensor_copy(hT[:, u, :, :], p_h[u][:, :, :]).then_inc(s["hT"], 1)
                    loop(dve, body)

        run("ex", NE // 2, False)
        run("sp", None, True)


def combine(nc, g, I, R, x1, out):
    NT = SEQ // P
    with ExitStack() as ctx:
        sb = lambda n, s, d=F32: ctx.enter_context(nc.sbuf_tensor(n, s, d))
        sem = lambda n: ctx.enter_context(nc.semaphore(n))
        rows = sb("cb_rows", [P, NT, 2, D])
        gt, gain = sb("cb_gt", [P, D]), sb("cb_gain", [P, D])
        acc = sb("cb_acc", [P, NT, D])
        sq = sb("cb_sq", [P, D])
        st = sb("cb_st", [P, NT, 4])
        loaded, gath = sem("cb_loaded"), [sem(f"cb_g{t}") for t in range(NT)]
        acc_s, sum_s, mean_s, root_s, out_s, stored = sem("cb_acc_s"), sem("cb_sum"), sem("cb_mean"), sem("cb_root"), sem("cb_out"), sem("cb_stored")
        with nc.Block() as block:
            @block.gpsimd
            def _(pool):
                for t in range(NT):
                    for j in range(2):
                        pool.indirect_dma_start(out=rows[:, t, j, :], out_offset=None, in_=g["y_dram"],
                                                in_offset=bass.IndirectOffsetOnAxis(ap=R["slot"][:, j, t:t + 1], axis=0)).then_inc(gath[t], 16)

            @block.sync
            def _(sp):
                sp.dma_start(gt[:, :], g["mod_rows"][:, 3 * D:4 * D]).then_inc(loaded, 16)
                sp.dma_start(gain[:, :], I["gains"][2:3, :].to_broadcast([P, D])).then_inc(loaded, 16)
                for t in range(NT):
                    sp.wait_ge(out_s, t + 1)
                    sp.dma_start(out[0, t * P:t * P + P, :], acc[:, t, :]).then_inc(stored, 16)
                sp.wait_ge(stored, NT * 16)

            @block.scalar
            def _(act):
                for t in range(NT):
                    act.wait_ge(acc_s, t + 1)
                    act.activation(sq[:, :], acc[:, t, :], ACT.Square, accum_out=st[:, t, 0:1])
                    act.drain().then_inc(sum_s, 1)
                    act.wait_ge(mean_s, t + 1)
                    act.activation(st[:, t, 2:3], st[:, t, 1:2], ACT.Sqrt).then_inc(root_s, 1)

            @block.vector
            def _(dve):
                dve.wait_ge(loaded, 32)
                dve.tensor_tensor(gt[:, :], gt[:, :], gain[:, :], ALU.mult)
                for t in range(NT):
                    dve.wait_ge(gath[t], 32)
                    dve.tensor_scalar(rows[:, t, 0, :], rows[:, t, 0, :], R["gate"][:, 0, t:t + 1], None, ALU.mult)
                    dve.drain()
                    dve.scalar_tensor_tensor(out=acc[:, t, :], in0=rows[:, t, 1, :], scalar=R["gate"][:, 1, t:t + 1], in1=rows[:, t, 0, :], op0=ALU.mult, op1=ALU.add).then_inc(acc_s, 1)
                for t in range(NT):
                    dve.wait_ge(sum_s, t + 1)
                    dve.tensor_scalar(st[:, t, 1:2], st[:, t, 0:1], 1.0 / D, RMS_EPS, ALU.mult, ALU.add).then_inc(mean_s, 1)
                    dve.wait_ge(root_s, t + 1)
                    dve.reciprocal(st[:, t, 3:4], st[:, t, 2:3])
                    dve.drain()
                    dve.scalar_tensor_tensor(out=acc[:, t, :], in0=acc[:, t, :], scalar=st[:, t, 3:4], in1=gt[:, :], op0=ALU.mult, op1=ALU.mult)
                    dve.drain()
                    dve.tensor_tensor(acc[:, t, :], acc[:, t, :], x1[:, t, :], ALU.add).then_inc(out_s, 1)


def layout(a):
    a = {k: np.asarray(v) for k, v in a.items()}
    L = {k: (v[0] if k not in ("x", "ctx", "c", "c_ctx") else v) for k, v in a.items()}
    out = {}
    cols = lambda v: v.reshape(-1, P).T
    out["x"], out["ctx"] = a["x"][0], a["ctx"][0]
    out["cvecs"] = np.stack([cols(a["c"][0]), cols(a["c_ctx"])], 1)
    out["ada_b"] = L["ada_b"][None]
    out["ada_w"] = L["ada_w"].reshape(KT, P, ADA_N, 512).transpose(2, 1, 0, 3)
    out["masks"] = mask_table()
    conv = L["conv_w"]
    chan = np.zeros((P, 64), np.float32)
    chan[:, 0:8] = cols(L["norm_gains"][0])
    for j in range(3):
        chan[:, 16 + 3 * j:19 + 3 * j] = conv[:, 3 * D + j * P:3 * D + (j + 1) * P].T
    chan[:, 25:33], chan[:, 33:41] = cols(L["lnx_w"]), cols(L["lnx_b"])
    chan[:, 41:45] = cols(L["pool_scale"])
    out["chan"] = chan
    win = L["w_in"]
    tiles = lambda w: w.reshape(KT, P, -1, P).transpose(2, 1, 0, 3)
    c0 = 512
    out["w_lr"] = tiles(win[:, c0 + 3 * D:c0 + 3 * D + 3 * P]).transpose(1, 0, 2, 3)
    r, k, v = (tiles(win[:, c0 + j * D:c0 + (j + 1) * D]) for j in range(3))
    w2 = L["w2"].reshape(P, KT, P).transpose(1, 0, 2)[:, :, None]
    a2 = L["a2"].reshape(P, KT, P).transpose(1, 0, 2)[:, :, None]
    out["w_prep"] = np.concatenate([r, k, v, w2, a2], 2).reshape(KT, P, PREPW)
    par = [conv[q, j * D:(j + 1) * D] for j in range(3) for q in range(3)]
    par += [L["w0"][0], L["w0"][1], L["a0"][0], L["a0"][1], L["k_k"], L["k_a"], L["r_k"].reshape(-1)]
    out["p_prep"] = np.stack([q.reshape(KT, P) for q in par], 2)
    out["g2"] = L["g2"]
    out["w_pool"] = win[:, 0:512].reshape(KT, P, 512).transpose(1, 0, 2)
    out["pool_w"] = L["pool_w"].transpose(1, 0, 2)
    out["pool_box"] = pool_table()
    gates = tiles(win[:, 512 + 3456:])
    pp, rp = (w.reshape(-1, P, KT, P).transpose(2, 1, 0, 3) for w in (L["pool_proj"], L["rwkv_proj"]))
    out["w_merge"] = np.concatenate([gates[0:KT], gates[KT:], pp, rp], 2).reshape(KT, P, MG * P)
    out["w_out"] = L["w_out"].reshape(KT, P, D).transpose(1, 0, 2)
    out["router_w"] = np.concatenate([L["router_group_w"], L["router_expert_w"]], 1).reshape(KT, P, 36).transpose(1, 0, 2)
    out["router_b"] = np.concatenate([L["router_group_b"], L["router_expert_b"]])[None]
    out["gains"] = L["norm_gains"][1:4]
    gu = np.concatenate([L["expert_w_gate"], L["expert_w_up"]], 2).reshape(NE, KT, P, 2 * FE).transpose(0, 2, 1, 3).reshape(NE, P, -1)
    dn = L["expert_w_down"].reshape(NE, 2, P, D).transpose(0, 2, 1, 3).reshape(NE, P, -1)
    out["w_experts"] = np.concatenate([gu, dn], 2)
    return {k: np.ascontiguousarray(v) for k, v in out.items()}


def program(nc, I, out):
    with ExitStack() as ctx:
        sb = lambda n, s, d=F32: ctx.enter_context(nc.sbuf_tensor(n, s, d))
        dram = lambda n, s, d=F32: nc.dram_tensor(n, s, d, kind="Internal").ap()
        g = {"masks": sb("masks_sb", [P, NM, P]), "chan": sb("chan_sb", [P, 64]), "mod": sb("mod_cols", [P, 2 * KT, 2])}
        g["mask"] = lambda n: g["masks"][:, MASKS.index(n), :]
        g["ident"] = g["mask"]("ident")
        g["mod_rows"] = dram("mod_rows_dram", [P, 4 * D])
        g["v_dram"] = dram("v_chunks", [KT, CHUNKS * P * C])
        g["kr_dram"] = dram("kr_chunks", [2, KT, CHUNKS * P * 2 * C])
        g["bk_dram"] = dram("bk_chunks", [2, KT, CHUNKS * P * 2 * C])
        g["hT"] = sb("hT", [P, KT, TOK])
        g["xg"] = sb("xg_sb", [P, SEQ])
        g["bonus"] = sb("bonus_sb", [P, KT, SEQ])
        g["decay_end"] = sb("decay_end", [P, 2, CHUNKS, KT])
        g["small"] = sb("small_sb", [P, 4])
        g["gn_eps"] = g["small"][:, 0:1]
        mean_w = sb("mean_w", [P, P])
        g["mean_w"] = mean_w[:, :]
        modulation(nc, g, I)
        norm_and_turn(nc, g, I)
        with ExitStack() as inner:
            g["xw"] = inner.enter_context(nc.sbuf_tensor("xw_sb", [P, 2, TOK], F32))
            g["xa"] = inner.enter_context(nc.sbuf_tensor("xa_sb", [P, 2, TOK], F32))
            low_rank_inputs(nc, g, I)
            prepare(nc, g, I)
        x1 = g["hT"][:, :, :].rearrange("p k t -> p (k t)")[:, 0:SEQ * KT].rearrange("p (t e) -> p t e", e=D)
        logits = sb("logits", [P, SEQ // P, 36])
        g["f_dram"] = dram("f_rows", [SEQ, D])
        g["slot_tok"] = dram("slot_tok", [TILES * SLOTS, 1])
        g["y_dram"] = dram("y_rows", [TILES * SLOTS, D])
        with ExitStack() as mixers:
            msb = lambda n, s: mixers.enter_context(nc.sbuf_tensor(n, s, F32))
            yn = [msb(f"y_normed{d}", [P, KT, SEQ]) for d in range(2)]
            with ExitStack() as inner:
                S = [inner.enter_context(nc.sbuf_tensor(f"state{d}", [P, KT, P], F32)) for d in range(2)]
                with nc.Block() as block:
                    @block.vector
                    def _(dve):
                        for d in range(2):
                            dve.memset(S[d][:, :, :], 0.0)
                        dve.memset(g["small"][:, 0:1], GN_EPS)
                        dve.tensor_scalar(g["mean_w"], g["mask"]("heads"), 1.0 / HD, None, ALU.mult)
                recurrence(nc, g, 0, S, yn)
                recurrence(nc, g, 1, S, yn)
            read_out(nc, g, I, yn)
            py = msb("pool_y", [P, 4, SEQ])
            pooling(nc, g, I, py)
            merge(nc, g, I, py, yn[0], yn[1])
            project_out(nc, g, I, yn[1], x1, logits)
        R = {"slot": sb("slot", [P, 2, SEQ // P], U32), "gate": sb("gate", [P, 2, SEQ // P]), "tok": sb("tok", [P, TILES], U32),
             "spill_expert": sb("spill_expert", [P, SPILL], I32), "spill_tiles": sb("spill_tiles", [P, 1], I32)}
        route(nc, g, logits, R)
        experts(nc, g, I, R)
        combine(nc, g, I, R, x1, out)


def kernel(**inputs):
    import concourse.bacc as bacc
    from concourse.bass_utils import run_bass_kernel_spmd

    nc = bacc.Bacc("TRN2", target_bir_lowering=False, num_devices=1)
    arrays = {f"in_{k}": v for k, v in layout(inputs).items()}
    aps = {k[3:]: nc.dram_tensor(k, v.shape, mybir.dt.from_np(v.dtype), kind="ExternalInput").ap() for k, v in arrays.items()}
    out = nc.dram_tensor("out", (1, SEQ, D), F32, kind="ExternalOutput").ap()
    program(nc, aps, out)
    r = run_bass_kernel_spmd(nc, [arrays], core_ids=[0])
    return r.results[0]["out"]
```

```python
from contextlib import ExitStack

import concourse.bass as bass
import numpy as np
from concourse import mybir

F32 = mybir.dt.float32
U32 = mybir.dt.uint32
I32 = mybir.dt.int32
ALU = mybir.AluOpType
ACT = mybir.ActivationFunctionType
AX = mybir.AxisListType
ds = bass.ds

P = 128
D = 1024
KT = D // P
SEQ, CTX = 512, 256
TOK = CTX + SEQ
HD = 64
C = 64
CTX_CHUNKS, LAT_CHUNKS = CTX // C, SEQ // C
CHUNKS = CTX_CHUNKS + LAT_CHUNKS
GRID_W = 64
WINDOWS = (2, 4, 8, 16)
NG, EPG, NE = 4, 8, 32
FE = 256
GN_EPS, RMS_EPS = 64e-5, 1e-6
DECAY = float(np.exp(-0.5))
ADA_N = 6 * D // 512
NPAR = 16
(P_CR, P_CK, P_CV, P_W0, P_A0, P_KK, P_KA, P_RK) = (0, 3, 6, 9, 11, 13, 14, 15)
PREPW = (3 * KT + 2) * P
LEVELS = (2, 4, 8, 16)

MASKS = ["ident", "heads", "strict_up", "strict_low", "incl_up", "incl_low"]
MASKS += ["before", "ones"]
MASKS += [f"up{b}" for b in (1, 2, 4, 8, 16, 32)] + [f"low{b}" for b in (1, 2, 4, 8, 16, 32)]
NM = len(MASKS)


def mask_table():
    r, c = np.arange(P)[:, None], np.arange(P)[None, :]
    same = (r // HD) == (c // HD)
    t = {"ident": r == c, "heads": same, "strict_up": same & (r < c), "strict_low": same & (r > c),
         "incl_up": same & (r <= c), "incl_low": same & (r >= c),
         "before": r < c, "ones": r + c >= 0}
    for b in (1, 2, 4, 8, 16, 32):
        low = (r // (2 * b) == c // (2 * b)) & (r // b % 2 == 1) & (c // b % 2 == 0)
        t[f"low{b}"], t[f"up{b}"] = low, low.T
    return np.ascontiguousarray(np.stack([t[m] for m in MASKS], 1).astype(np.float32))


def pool_table():
    rows = SEQ // GRID_W

    def mean(n, win):
        lo = win // 2
        hi = win - lo - 1
        m = np.zeros((n, n))
        for t in range(n):
            a, b = max(t - lo, 0), min(t + hi + 1, n)
            m[a:b, t] = 1.0 / (b - a)
        return m

    out = [np.kron(mean(rows, w), mean(GRID_W, w)) - np.eye(SEQ) for w in WINDOWS]
    return np.ascontiguousarray(np.stack(out).reshape(4, SEQ // P, P, SEQ).transpose(0, 2, 1, 3).astype(np.float32))


def flat(ap, at, n):
    names = "abcdefg"[:len(ap.shape)]
    return ap.rearrange(f"{' '.join(names)} -> ({' '.join(names)})")[ds(at, n)]


class Order:

    def __init__(self, sem, names):
        self.sem, self.names = sem, names
        self.at = {n: k + 1 + len(names) for k, n in enumerate(names)}
        self.next = 0

    def start(self, engine):
        engine.sem_inc(self.sem, len(self.names))

    def done(self, name, ins):
        assert self.names[self.next % len(self.names)] == name, (name, self.names[self.next % len(self.names)])
        self.next += 1
        ins.then_inc(self.sem, 1)

    def value(self, name, i=0, back=0):
        return i * len(self.names) + (self.at[name] - back * len(self.names))


def modulation(nc, g, I):
    with ExitStack() as ctx:
        sb = lambda n, s, d=F32: ctx.enter_context(nc.sbuf_tensor(n, s, d))
        sem = lambda n: ctx.enter_context(nc.semaphore(n))
        cvec = sb("cvec", [P, 2, KT])
        sig = sb("csig", [P, 2, KT])
        silu = sb("csilu", [P, 2, KT])
        lhs = sb("clhs", [P, 2, KT, P])
        ones = sb("ones_row", [1, P])
        bias = sb("ada_bias", [1, 6 * D])
        w = sb("ada_tile", [P, 2, KT, 512])
        first = sb("mod_first", [P, 2 * D])
        rest = sb("mod_rest", [P, 2, 512])
        gains = sb("mod_gains", [P, 4, D])
        ps = [ctx.enter_context(nc.psum_tensor(f"mod_ps{k}", [P, 512], F32)) for k in range(2)]
        pt = [ctx.enter_context(nc.psum_tensor(f"mod_pt{k}", [P, 4, P], F32)) for k in range(4)]
        small, wload, silu_ready, lhs_ready = sem("small"), [sem("wload0"), sem("wload1")], sem("silu"), sem("lhs")
        block_done, evac, turned, rest_out, mod_ready = sem("block_done"), sem("evac"), sem("turned"), [sem("ro0"), sem("ro1")], sem("mod_ready")
        NF = 2 * D // 512
        with nc.Block() as block:
            @block.sync
            def _(sp):
                sp.dma_start(cvec[:, :, :], I["cvecs"]).then_inc(small, 16)
                sp.dma_start(bias[:, :], I["ada_b"]).then_inc(small, 16)
                sp.dma_start(g["masks"][:, :, :], I["masks"]).then_inc(small, 16)
                sp.dma_start(g["chan"][:, :], I["chan"]).then_inc(small, 16)
                with sp.Fori(0, ADA_N // 2) as i:
                    for u in range(2):
                        at = sp.snap(i * 2 * P * KT * 512 + u * P * KT * 512)
                        sp.wait_ge(block_done, i * 2)
                        sp.dma_start(w[:, u, :, :], flat(I["ada_w"], at, P * KT * 512).rearrange("(p k n) -> p k n", p=P, k=KT)).then_inc(wload[u], 16)

            @block.scalar
            def _(act):
                act.wait_ge(small, 64)
                act.activation(sig[:, :, :], cvec[:, :, :], ACT.Sigmoid).then_inc(silu_ready, 1)

            @block.vector
            def _(dve):
                dve.memset(ones[:, :], 1.0)
                dve.wait_ge(silu_ready, 1)
                dve.tensor_tensor(silu[:, :, :], sig[:, :, :], cvec[:, :, :], ALU.mult)
                dve.drain()
                for h in range(2):
                    dve.tensor_copy(lhs[:, 0, :, h * 64:h * 64 + 64], silu[:, h, :].unsqueeze(2).to_broadcast([P, KT, 64]))
                dve.tensor_copy(lhs[:, 1, :, :], silu[:, 0, :].unsqueeze(2).to_broadcast([P, KT, P]))
                dve.drain().then_inc(lhs_ready, 1)
                for n in range(NF):
                    dve.wait_ge(block_done, n + 1)
                    dve.tensor_copy(first[:, n * 512:n * 512 + 512], ps[n % 2][:, :]).then_inc(evac, 1)
                with dve.Fori(0, (ADA_N - NF) // 2) as i:
                    for u in range(2):
                        dve.wait_ge(block_done, i * 2 + NF + u + 1)
                        dve.wait_ge(rest_out[u], i * 16)
                        dve.tensor_copy(rest[:, u, :], ps[u][:, :]).then_inc(evac, 1)
                for t in range(4):
                    dve.wait_ge(turned, t + 1)
                    dve.tensor_copy(g["mod"][:, t * 4:t * 4 + 4, :], pt[t][:, :, 0::64])
                dve.drain()
                sc, gain = g["mod"][:, KT:2 * KT, :], g["chan"][:, 0:KT].unsqueeze(2).to_broadcast([P, KT, 2])
                dve.scalar_tensor_tensor(out=sc, in0=sc, scalar=1.0, in1=gain, op0=ALU.add, op1=ALU.mult).then_inc(mod_ready, 1)

            @block.tensor
            def _(pe):
                pe.wait_ge(small, 64)
                pe.wait_ge(lhs_ready, 1)

                def one(n, u, which, i=None):
                    pe.wait_ge(wload[u], ((n // 2) + 1) * 16 if i is None else (i + NF // 2 + 1) * 16)
                    for k in range(KT):
                        pe.matmul(ps[u][:, :], lhs[:, which, k, :], w[:, u, k, :], start=(k == 0), stop=False)
                    at = n * 512 if i is None else pe.snap(i * 1024 + (NF + u) * 512)
                    pe.matmul(ps[u][:, :], ones[:, :], bias[:, ds(at, 512)], start=False, stop=True).then_inc(block_done, 1)

                for n in range(NF):
                    if n >= 2:
                        pe.wait_ge(evac, n - 1)
                    one(n, n % 2, 0)
                with pe.Fori(0, (ADA_N - NF) // 2) as i:
                    for u in range(2):
                        pe.wait_ge(evac, i * 2 + NF + u - 1)
                        one(None, u, 1, i)
                pe.wait_ge(evac, NF)
                for t in range(4):
                    for k in range(4):
                        n = (t * 4 + k) * P
                        last = pe.transpose(pt[t][:, k, :], first[:, n:n + P], g["ident"])
                    last.then_inc(turned, 1)

            @block.gpsimd
            def _(pool):
                with pool.Fori(0, (ADA_N - NF) // 2) as i:
                    for u in range(2):
                        blk = pool.snap(i * 1024 + u * 512)
                        pool.wait_ge(evac, i * 2 + NF + u + 1)
                        pool.dma_start(g["mod_rows"][:, ds(blk, 512)], rest[:, u, :]).then_inc(rest_out[u], 16)
                for u in range(2):
                    pool.wait_ge(rest_out[u], (ADA_N - NF) // 2 * 16)


def norm_and_turn(nc, g, I):
    with ExitStack() as ctx:
        sb = lambda n, s, d=F32: ctx.enter_context(nc.sbuf_tensor(n, s, d))
        sem = lambda n: ctx.enter_context(nc.semaphore(n))
        NT = TOK // P
        xs = sb("x_tiles", [P, NT, D])
        xn = sb("x_normed", [P, 2, D])
        sq = sb("x_sq", [P, D])
        st = sb("x_stat", [P, 4, NT])
        tmp = sb("x_tmp", [P, KT, P])
        pt = [ctx.enter_context(nc.psum_tensor(f"x_pt{k}", [P, KT, P], F32)) for k in range(2)]
        loaded = [sem(f"x_loaded{t}") for t in range(NT)]
        summed, root, normed, turned, evac = sem("summed"), sem("root"), sem("normed"), sem("x_turned"), sem("x_evac")
        meaned = sem("meaned")
        with nc.Block() as block:
            @block.sync
            def _(sp):
                for t in range(NT):
                    src = I["ctx"][t * P:t * P + P, :] if t < CTX // P else I["x"][(t - 2) * P:(t - 1) * P, :]
                    sp.dma_start(xs[:, t, :], src).then_inc(loaded[t], 16)

            @block.scalar
            def _(act):
                for t in range(NT):
                    act.wait_ge(loaded[t], 16)
                    act.activation(sq[:, :], xs[:, t, :], ACT.Square, accum_out=st[:, 0, t:t + 1])
                    act.drain().then_inc(summed, 1)
                act.wait_ge(meaned, 1)
                act.activation(st[:, 2, :], st[:, 1, :], ACT.Sqrt).then_inc(root, 1)

            @block.vector
            def _(dve):
                dve.wait_ge(summed, NT)
                dve.tensor_scalar(st[:, 1, :], st[:, 0, :], 1.0 / D, RMS_EPS, ALU.mult, ALU.add).then_inc(meaned, 1)
                dve.wait_ge(root, 1)
                dve.reciprocal(st[:, 3, :], st[:, 2, :])
                dve.drain()
                for t in range(NT + 1):
                    if t < NT:
                        if t >= 2:
                            dve.wait_ge(turned, t - 1)
                        dve.tensor_scalar(xn[:, t % 2, :], xs[:, t, :], st[:, 3, t:t + 1], None, ALU.mult).then_inc(normed, 1)
                    if t >= 1:
                        s = t - 1
                        which = 1 if s < CTX // P else 0
                        scale = g["mod"][:, KT:2 * KT, which:which + 1].to_broadcast([P, KT, P])
                        shift = g["mod"][:, 0:KT, which:which + 1].to_broadcast([P, KT, P])
                        dve.wait_ge(turned, s + 1)
                        dve.tensor_tensor(tmp[:, :, :], pt[s % 2][:, :, :], scale, ALU.mult).then_inc(evac, 1)
                        dve.drain()
                        dve.tensor_tensor(g["hT"][:, :, s * P:s * P + P], tmp[:, :, :], shift, ALU.add)
                        dve.drain()

            @block.tensor
            def _(pe):
                for t in range(NT):
                    pe.wait_ge(normed, t + 1)
                    if t >= 2:
                        pe.wait_ge(evac, t - 1)
                    for k in range(KT):
                        last = pe.transpose(pt[t % 2][:, k, :], xn[:, t % 2, k * P:k * P + P], g["ident"])
                    last.then_inc(turned, 1)


def low_rank_inputs(nc, g, I):
    with ExitStack() as ctx:
        sb = lambda n, s, d=F32: ctx.enter_context(nc.sbuf_tensor(n, s, d))
        sem = lambda n: ctx.enter_context(nc.semaphore(n))
        w = sb("lr_w", [P, 3, KT, P])
        y = sb("lr_y", [P, 3, TOK])
        ps = [[ctx.enter_context(nc.psum_tensor(f"lr_ps{j}{k}", [P, 512], F32)) for k in range(2)] for j in range(3)]
        wl, mm, cv = sem("lr_loaded"), sem("lr_mm"), sem("lr_conv")
        hT, xw, xa, xg, chan = g["hT"], g["xw"], g["xa"], g["xg"], g["chan"]
        with nc.Block() as block:
            @block.sync
            def _(sp):
                sp.dma_start(w[:, :, :, :], I["w_lr"]).then_inc(wl, 16)

            @block.tensor
            def _(pe):
                pe.wait_ge(wl, 16)
                for j in range(3):
                    for part, (a, n) in enumerate(((CTX, SEQ), (0, CTX))):
                        if j == 2 and part == 1:
                            continue
                        for k in range(KT):
                            last = pe.matmul(ps[j][part][:, 0:n], w[:, j, k, :], hT[:, k, a:a + n], start=(k == 0), stop=(k == KT - 1))
                    last.then_inc(mm, 1)

            @block.vector
            def _(dve):
                for z in (xw, xa):
                    dve.memset(z[:, :, :], 0.0)
                dve.drain()
                for j in range(3):
                    dve.wait_ge(mm, j + 1)
                    tap = lambda q: chan[:, 16 + 3 * j + q:17 + 3 * j + q]
                    for part, (a, n) in enumerate(((CTX, SEQ), (0, CTX))):
                        if j == 2 and part == 1:
                            continue
                        s = ps[j][part]
                        dve.tensor_scalar(y[:, j, a:a + n], s[:, 0:n], tap(1), None, ALU.mult)
                        dve.drain()
                        dve.scalar_tensor_tensor(out=y[:, j, a + 1:a + n], in0=s[:, 0:n - 1], scalar=tap(0), in1=y[:, j, a + 1:a + n], op0=ALU.mult, op1=ALU.add)
                        dve.drain()
                        dve.scalar_tensor_tensor(out=y[:, j, a:a + n - 1], in0=s[:, 1:n], scalar=tap(2), in1=y[:, j, a:a + n - 1], op0=ALU.mult, op1=ALU.add)
                        dve.drain()
                    dve.drain().then_inc(cv, 1)
                for d in range(2):
                    h = slice(64 * d, 64 * d + 64)
                    dve.tensor_copy(xa[h, d, :], y[h, 1, :])

            @block.scalar
            def _(act):
                act.wait_ge(cv, 1)
                for d in range(2):
                    h = slice(64 * d, 64 * d + 64)
                    act.activation(xw[h, d, :], y[h, 0, :], ACT.Tanh)
                act.wait_ge(cv, 3)
                act.activation(xg[:, :], y[:, 2, CTX:TOK], ACT.Sigmoid)


def prepare(nc, g, I):
    with ExitStack() as ctx:
        sb = lambda n, s, d=F32: ctx.enter_context(nc.sbuf_tensor(n, s, d))
        sem = lambda n: ctx.enter_context(nc.semaphore(n))
        w = sb("pr_w", [P, 2, PREPW])
        par = sb("pr_par", [P, 2, NPAR])
        rk = sb("pr_rk", [P, P])
        r, k, v = sb("pr_r", [P, TOK]), sb("pr_k", [P, TOK]), sb("pr_v", [P, TOK])
        kraw, ksq, kk = sb("pr_kraw", [P, TOK]), sb("pr_ksq", [P, TOK]), sb("pr_kk", [P, TOK])
        norm, rnorm = sb("pr_norm", [P, TOK]), sb("pr_rnorm", [P, TOK])
        s_dec, rate = sb("pr_s", [P, 2, TOK]), sb("pr_rate", [P, 2, TOK])
        reset = sb("pr_reset", [P, 2, CHUNKS, C])
        cum, cumx = sb("pr_cum", [P, 2, TOK]), sb("pr_cumx", [P, 2, TOK])
        e_in, e_out, e_prev = (sb(f"pr_e{j}", [P, TOK]) for j in range(3))
        kd, bb = sb("pr_kd", [P, 2, TOK]), sb("pr_bb", [P, TOK])
        k_ka, k_rest = sb("pr_kka", [P, TOK]), sb("pr_krest", [P, TOK])
        rkd = sb("pr_rkd", [P, SEQ])
        KR = sb("pr_KR", [P, 2, CHUNKS, 2, C])
        BK = sb("pr_BK", [P, 2, CHUNKS, 2, C])
        one_less = sb("pr_1ka", [P, 1])
        bank = [ctx.enter_context(nc.psum_tensor(f"pr_ps{j}", [P, 512], F32)) for j in range(8)]
        B_R, B_K, B_V, B_KC, B_VC = bank[0:5]
        PAIR = [(bank[5], bank[6]), (B_R, bank[7])]
        B_BONUS = bank[7]
        wload = [sem("pr_wl0"), sem("pr_wl1")]
        pe_s, act_s, dve_s, pool_s = sem("pr_pe"), sem("pr_act"), sem("pr_dve"), sem("pr_pool")
        stored = [sem("pr_st0"), sem("pr_st1")]
        vstored = sem("pr_vst")
        hT, heads = g["hT"], g["mask"]("heads")
        pe_o = Order(pe_s, ["k", "r", "v", "a0", "a1", "w0", "w1", "norm", "bonus"])
        act_o = Order(act_s, ["tap_k", "tap_r", "ksq", "tap_v", "sig_a0", "sig_a1", "sig_w0", "sig_w1", "exp0", "rnorm", "exp1"])
        dve_o = Order(dve_s, ["conv_k", "kraw", "conv_r", "conv_v", "kds", "cum0", "cum1", "guard", "kk", "dec0", "dec1", "bonus"])
        pool_o = Order(pool_s, ["kd0", "kd1"])
        lat = slice(CTX, TOK)
        parts = ((CTX, SEQ), (0, CTX))
        low_rank = (("a0", 1, g["xa"], 0), ("a1", 1, g["xa"], 1), ("w0", 0, g["xw"], 0), ("w1", 0, g["xw"], 1))
        mixed = {"k": (1, k, B_K, B_KC, P_CK), "r": (0, r, B_R, None, P_CR), "v": (2, v, B_V, B_VC, P_CV)}

        def body(u):
            return w[:, u, :].rearrange("p (j n) -> p j n", n=P), lambda q: par[:, u, q:q + 1]

        with nc.Block() as block:
            @block.sync
            def _(sp):
                for u in range(2):
                    sp.dma_start(w[:, u, :], I["w_prep"][u]).then_inc(wload[u], 16)
                    sp.dma_start(par[:, u, :], I["p_prep"][u]).then_inc(wload[u], 16)
                sp.sem_inc(vstored, 16)
                for d in range(2):
                    sp.sem_inc(stored[d], 32)

                NV, NO = CHUNKS * P * C, CHUNKS * P * 2 * C

                def store(m, at, at_v):
                    sp.wait_ge(dve_s, dve_o.value("conv_v", m))
                    sp.dma_start(flat(g["v_dram"], at_v, NV).rearrange("(c p t) -> p c t", c=CHUNKS, p=P),
                                 v[:, :].rearrange("p (c t) -> p c t", t=C)).then_inc(vstored, 16)

                def store_operands(m, at):
                    for d in range(2):
                        sp.wait_ge(dve_s, dve_o.value(f"dec{d}", m))
                        for dst, src in ((g["kr_dram"], KR), (g["bk_dram"], BK)):
                            sp.dma_start(flat(dst[d], at, NO).rearrange("(c p t) -> p c t", c=CHUNKS, p=P),
                                         src[:, d, :, :, :].rearrange("p c b t -> p c (b t)")).then_inc(stored[d], 16)

                with sp.Fori(0, KT // 2 - 1) as i:
                    for u in range(2):
                        m = i * 2 + u
                        at, at_v = sp.snap(i * 2 * NO + u * NO), sp.snap(i * 2 * NV + u * NV)
                        nxt_w = sp.snap(i * 2 * P * PREPW + (u + 2) * P * PREPW)
                        nxt_p = sp.snap(i * 2 * P * NPAR + (u + 2) * P * NPAR)
                        store(m, at, at_v)
                        sp.wait_ge(pe_s, pe_o.value("bonus", m))
                        sp.dma_start(w[:, u, :], flat(I["w_prep"], nxt_w, P * PREPW).rearrange("(p n) -> p n", p=P)).then_inc(wload[u], 16)
                        sp.dma_start(par[:, u, :], flat(I["p_prep"], nxt_p, P * NPAR).rearrange("(p n) -> p n", p=P)).then_inc(wload[u], 16)
                        store_operands(m, at)
                for m in (KT - 2, KT - 1):
                    store(m, m * NO, m * NV)
                    store_operands(m, m * NO)
                for d in range(2):
                    sp.wait_ge(stored[d], (KT + 1) * 32)
                sp.wait_ge(vstored, (KT + 1) * 16)

            @block.tensor
            def _(pe):
                pe_o.start(pe)
                with pe.Fori(0, KT // 2) as i:
                    for u in range(2):
                        wv, pr = body(u)
                        m = i * 2 + u
                        pe.wait_ge(wload[u], (i + 1) * 32)
                        for name in ("k", "r", "v"):
                            j, _y, lat_bank, ctx_bank, _q = mixed[name]
                            if name == "r":
                                pe.wait_ge(act_s, act_o.value("sig_w1", m, 1))
                            else:
                                pe.wait_ge(dve_s, dve_o.value(f"conv_{name}", m, 1))
                            for kt in range(KT):
                                last = pe.matmul(lat_bank[:, :], wv[:, j * KT + kt, :], hT[:, kt, lat], start=(kt == 0), stop=(kt == KT - 1))
                            if ctx_bank is not None:
                                for kt in range(KT):
                                    last = pe.matmul(ctx_bank[:, 0:CTX], wv[:, j * KT + kt, :], hT[:, kt, 0:CTX], start=(kt == 0), stop=(kt == KT - 1))
                            pe_o.done(name, last)
                        for q, (name, maps, src, d) in enumerate(low_rank):
                            if q == 0:
                                pe.wait_ge(dve_s, dve_o.value("guard", m, 1))
                            elif q == 1:
                                pe.wait_ge(dve_s, dve_o.value("conv_r", m))
                            else:
                                pe.wait_ge(act_s, act_o.value(("sig_a0", "sig_a1")[q - 2], m))
                            for part, (a, n) in enumerate(parts):
                                last = pe.matmul(PAIR[q % 2][part][:, 0:n], wv[:, 3 * KT + maps, :], src[:, d, a:a + n], start=True, stop=True)
                            pe_o.done(name, last)
                        pe.wait_ge(act_s, act_o.value("sig_w0", m))
                        for part, (a, n) in enumerate(parts):
                            last = pe.matmul(PAIR[0][part][:, 0:n], heads, ksq[:, a:a + n], start=True, stop=True)
                        pe_o.done("norm", last)
                        pe.wait_ge(act_s, act_o.value("sig_w1", m))
                        pe.wait_ge(dve_s, dve_o.value("kds", m))
                        pe_o.done("bonus", pe.matmul(B_BONUS[:, :], rk[:, :], rkd[:, :], start=True, stop=True))

            @block.scalar
            def _(act):
                act_o.start(act)
                with act.Fori(0, KT // 2) as i:
                    for u in range(2):
                        wv, pr = body(u)
                        m = i * 2 + u
                        act.wait_ge(wload[u], (i + 1) * 32)
                        for name, used in (("k", "kraw"), ("r", "dec1"), ("v", "bonus")):
                            _j, y, b, bc, q = mixed[name]
                            act.wait_ge(dve_s, dve_o.value(used, m, 1))
                            if name == "v":
                                act.wait_ge(vstored, (m + 1) * 16)
                            act.wait_ge(pe_s, pe_o.value(name, m))
                            last = act.activation(y[:, lat], b[:, :], ACT.Copy, scale=pr(q + 1))
                            if bc is not None:
                                last = act.activation(y[:, 0:CTX], bc[:, 0:CTX], ACT.Copy, scale=pr(q + 1))
                            act_o.done(f"tap_{name}", last)
                            if name == "r":
                                act.wait_ge(dve_s, dve_o.value("kraw", m))
                                act_o.done("ksq", act.activation(ksq[:, :], kraw[:, :], ACT.Square))
                        for q, (name, _maps, _src, d) in enumerate(low_rank):
                            y, p0 = (rate, P_A0 + d) if name[0] == "a" else (s_dec, P_W0 + d)
                            act.wait_ge(pe_s, pe_o.value(name, m))
                            for part, (a, n) in enumerate(parts):
                                last = act.activation(y[:, d, a:a + n], PAIR[q % 2][part][:, 0:n], ACT.Sigmoid, bias=pr(p0))
                            act_o.done(f"sig_{name}", last)
                        for d in range(2):
                            act.wait_ge(dve_s, dve_o.value(f"cum{d}", m))
                            if d:
                                act.wait_ge(dve_s, dve_o.value("dec0", m))
                            act.activation(e_in[:, :], cum[:, d, :], ACT.Exp, scale=-DECAY)
                            act.activation(e_out[:, :], cum[:, d, :], ACT.Exp, scale=DECAY)
                            act_o.done(f"exp{d}", act.activation(e_prev[:, :], cumx[:, d, :], ACT.Exp, scale=-DECAY))
                            if d == 0:
                                act.wait_ge(dve_s, dve_o.value("guard", m))
                                act.activation(norm[:, :], norm[:, :], ACT.Ln)
                                act.drain()
                                act_o.done("rnorm", act.activation(rnorm[:, :], norm[:, :], ACT.Exp, scale=-0.5))

            @block.gpsimd
            def _(pool):
                pool_o.start(pool)
                with pool.Fori(0, KT // 2) as i:
                    for u in range(2):
                        m = i * 2 + u
                        pool.wait_ge(dve_s, dve_o.value("kraw", m))
                        for d in range(2):
                            pool.wait_ge(act_s, act_o.value(f"sig_a{d}", m))
                            pool.tensor_tensor(kd[:, d, :], rate[:, d, :], k_ka[:, :], ALU.mult)
                            pool.drain()
                            pool_o.done(f"kd{d}", pool.tensor_tensor(kd[:, d, :], kd[:, d, :], k_rest[:, :], ALU.add))

            @block.vector
            def _(dve):
                dve_o.start(dve)
                dve.memset(reset[:, :, :, :], 1.0)
                dve.memset(KR[:, :, 0:CTX_CHUNKS, 1, :], 0.0)
                dve.drain()
                dve.memset(reset[:, 0, :, 0:1], 0.0)
                dve.memset(reset[:, 1, :, C - 1:C], 0.0)
                dve.drain()
                with dve.Fori(0, KT // 2) as i:
                    for u in range(2):
                        wv, pr = body(u)
                        m = i * 2 + u
                        mreg = dve.snap(i * 2 + u)
                        dve.wait_ge(wload[u], (i + 1) * 32)
                        dve.tensor_scalar(one_less[:, :], pr(P_KA), -1.0, 1.0, ALU.mult, ALU.add)
                        for name in ("k", "r", "v"):
                            _j, y, b, bc, q = mixed[name]
                            dve.wait_ge(act_s, act_o.value(f"tap_{name}", m))
                            todo = [(b, CTX, SEQ)] + ([(bc, 0, CTX)] if bc is not None else [])
                            for tap in (0, 2):
                                for s, a, n in todo:
                                    dst = y[:, a + 1:a + n] if tap == 0 else y[:, a:a + n - 1]
                                    src = s[:, 0:n - 1] if tap == 0 else s[:, 1:n]
                                    last = dve.scalar_tensor_tensor(out=dst, in0=src, scalar=pr(q + tap), in1=dst, op0=ALU.mult, op1=ALU.add)
                                if tap == 0:
                                    dve.drain()
                            dve_o.done(f"conv_{name}", last)
                            if name == "k":
                                dve.drain()
                                dve.tensor_scalar(k_ka[:, :], k[:, :], pr(P_KA), None, ALU.mult)
                                dve.tensor_scalar(k_rest[:, :], k[:, :], one_less[:, 0:1], None, ALU.mult)
                                dve.tensor_scalar(rk[:, :], heads, pr(P_RK), None, ALU.mult)
                                dve_o.done("kraw", dve.tensor_scalar(kraw[:, :], k[:, :], pr(P_KK), None, ALU.mult))
                        dve.wait_ge(pool_s, pool_o.value("kd1", m))
                        dve.tensor_tensor(rkd[:, :], kd[:, 0, lat], kd[:, 1, lat], ALU.add)
                        dve.drain()
                        dve_o.done("kds", dve.tensor_tensor(rkd[:, :], rkd[:, :], r[:, lat], ALU.mult))
                        for d in range(2):
                            f = slice(None, None, 1 if d == 0 else -1)
                            rs = reset[:, d, :, :].rearrange("p c t -> p (c t)")
                            dve.wait_ge(act_s, act_o.value(f"sig_w{d}", m))
                            dve.tensor_tensor_scan(cum[:, d, f], rs[:, f], s_dec[:, d, f], 0.0, ALU.mult, ALU.add)
                            dve.drain()
                            dve_o.done(f"cum{d}", dve.tensor_tensor(cumx[:, d, :], cum[:, d, :], s_dec[:, d, :], ALU.subtract))
                        dve.wait_ge(pe_s, pe_o.value("norm", m))
                        for part, (a, n) in enumerate(parts):
                            last = dve.tensor_scalar(norm[:, a:a + n], PAIR[0][part][:, 0:n], 1e-24, None, ALU.max)
                        dve_o.done("guard", last)
                        dve.wait_ge(act_s, act_o.value("rnorm", m))
                        dve_o.done("kk", dve.tensor_tensor(kk[:, :], kraw[:, :], rnorm[:, :], ALU.mult))
                        for d in range(2):
                            chunks = lambda x: x.rearrange("p (c t) -> p c t", t=C)
                            dve.drain()
                            dve.tensor_tensor(bb[:, :], kk[:, :], rate[:, d, :], ALU.mult)
                            dve.wait_ge(act_s, act_o.value(f"exp{d}", m))
                            dve.wait_ge(stored[d], (m + 1) * 32)
                            dve.tensor_tensor(KR[:, d, :, 0, :], chunks(kk[:, :]), chunks(e_prev[:, :]), ALU.mult)
                            dve.tensor_tensor(KR[:, d, CTX_CHUNKS:, 1, :], chunks(r[:, lat]), chunks(e_in[:, lat]), ALU.mult)
                            dve.tensor_copy(g["decay_end"][:, d, :, ds(mreg, 1)], chunks(e_in[:, :])[:, :, (C - 1) * (1 - d):(C - 1) * (1 - d) + 1])
                            dve.drain()
                            dve.tensor_tensor(BK[:, d, :, 0, :], chunks(bb[:, :]), chunks(e_out[:, :]), ALU.mult)
                            dve_o.done(f"dec{d}", dve.tensor_tensor(BK[:, d, :, 1, :], chunks(kd[:, d, :]), chunks(e_out[:, :]), ALU.mult))
                        dve.wait_ge(pe_s, pe_o.value("bonus", m))
                        dve_o.done("bonus", dve.tensor_tensor(g["bonus"][:, ds(mreg, 1), :], B_BONUS[:, :].unsqueeze(1), v[:, lat].unsqueeze(1), ALU.mult))


def recurrence(nc, g, part, S):
    n = (CTX_CHUNKS, LAT_CHUNKS)[part]
    first = (0, CTX_CHUNKS)[part]
    with_y = part == 1
    H = KT // 2
    with ExitStack() as ctx:
        sb = lambda nm, s, d=F32: ctx.enter_context(nc.sbuf_tensor(f"{nm}_{part}", s, d))
        sem = lambda nm: ctx.enter_context(nc.semaphore(f"{nm}_{part}"))
        KR = [sb(f"rc_KR{d}", [P, KT, 2, C]) for d in range(2)]
        early, late = ["B", "Kh", "V"], ["K"] + ["R"] * with_y
        bd = [{x: sb(f"rc_{x}bd{d}", [P, KT, P]) for x in early + late} for d in range(2)]
        mats = ["M", "Aak", "Bt", "Kt", "Vt", "T", "Tt", "G"] + ["Arb", "Ark"] * with_y
        W = [{x: sb(f"rc_{x}{d}", [P, KT, P]) for x in mats} for d in range(2)]
        for w in W:
            w["U"] = w["M"]
        PC = sb("rc_PC", [P, 2, KT])
        yc = [sb(f"rc_y{d}", [P, KT, C]) for d in range(2)] if with_y else None
        bank = [ctx.enter_context(nc.psum_tensor(f"rc_ps{j}_{part}", [P, H, P], F32)) for j in range(8)]
        loaded_early, loaded_late = [sem("rc_early0"), sem("rc_early1")], [sem("rc_late0"), sem("rc_late1")]
        pe_s, act_s, dve_s = sem("rc_pe"), sem("rc_act"), sem("rc_dve")
        cleared, x_seen = sem("rc_cleared"), sem("rc_x_seen")
        y_stored = [sem("rc_y_stored0"), sem("rc_y_stored1")]

        stages = ["B", "Kh", "Bt", "Kt", "Vt", "T1"]
        for b in LEVELS:
            stages += [f"G{b}", f"X{b}", f"Tt{b}"]
        stages += ["G32", "X32", "X", "U"] + ["Y"] * with_y + ["S"]
        by_act = {"Bt", "Kt", "Vt", "T1", "X", "U"} | {f"G{b}" for b in (*LEVELS, 32)} | {f"Tt{b}" for b in LEVELS}
        halves = lambda names: [f"{s}.{h}@{d}" for s in names for d in range(2) for h in range(2)]
        pe_o = Order(pe_s, halves(stages))
        act_o = Order(act_s, halves([s for s in stages if s in by_act]))
        dve_o = Order(dve_s, halves(["B", "Kh", "Tt1"] + [s for s in stages[6:] if s not in by_act]))
        sets = [("strict_up", "incl_up", "up1", "low", "up32"), ("strict_low", "incl_low", "low1", "up", "low32")]
        half = lambda x, h: x[:, H * h:H * h + H, :]

        def ps(stage, d, h):
            return bank[4 * d + 2 * (stages.index(stage) % 2) + h]

        with nc.Block() as block:
            @block.sync
            def _(sp):
                NO, NV, NY = P * 2 * C, P * C, P * KT * C
                for d in range(2):
                    if with_y:
                        sp.sem_inc(y_stored[d], 16)
                sp.wait_ge(cleared, 1)

                def place(d, q, at_o, at_v):
                    kr = g["kr_dram"][d][:, ds(at_o, NO)].rearrange("i (p b t) -> p i b t", p=P, b=2)
                    bk = g["bk_dram"][d][:, ds(at_o, NO)].rearrange("i (p b t) -> p i b t", p=P, b=2)
                    vv = g["v_dram"][:, ds(at_v, NV)].rearrange("i (p t) -> p i t", p=P)
                    return {"KR": kr, "K": kr[q, :, 0, :], "R": kr[q, :, 1, :], "B": bk[q, :, 0, :], "Kh": bk[q, :, 1, :], "V": vv[q, :, :]}

                def load(d, names, sem_, at_o, at_v):
                    if "B" in names:
                        sp.dma_start(KR[d][:, :, :, :].rearrange("p i b t -> p i (b t)"),
                                     place(d, slice(0, P), at_o, at_v)["KR"].rearrange("p i b t -> p i (b t)")).then_inc(sem_, 16)
                    for hh in range(2):
                        q = slice(64 * hh, 64 * hh + 64)
                        for x in names:
                            sp.dma_start(bd[d][x][q, :, q], place(d, q, at_o, at_v)[x]).then_inc(sem_, 16)

                def store(d, at_y):
                    sp.dma_start(g["y_chunks"][d:d + 1, ds(at_y, NY)].rearrange("a (p n) -> (a p) n", p=P),
                                 yc[d][:, :, :].rearrange("p i t -> p (i t)")).then_inc(y_stored[d], 16)

                for d in range(2):
                    c = first if d == 0 else first + n - 1
                    load(d, early, loaded_early[d], c * NO, c * NV)
                for d in range(2):
                    c = first if d == 0 else first + n - 1
                    load(d, late, loaded_late[d], c * NO, c * NV)
                with sp.Fori(0, n - 1) as i:
                    sign = (1, -1)
                    nxt = (first + 1, first + n - 2)
                    at_o = [sp.snap(i * (sign[d] * NO) + nxt[d] * NO) for d in range(2)]
                    at_v = [sp.snap(i * (sign[d] * NV) + nxt[d] * NV) for d in range(2)]
                    turned = [sp.snap(pe_o.value(f"Vt.1@{d}", i)) for d in range(2)]
                    used = [sp.snap(pe_o.value(f"{'Y' if with_y else 'X'}.1@{d}", i)) for d in range(2)]
                    if with_y:
                        at_y = [sp.snap(i * NY), sp.snap(i * -NY + (n - 1) * NY)]
                        y_ready = [sp.snap(dve_o.value(f"Y.1@{d}", i)) for d in range(2)]
                    for d in range(2):
                        sp.wait_ge(pe_s, turned[d])
                        load(d, early, loaded_early[d], at_o[d], at_v[d])
                    for d in range(2):
                        sp.wait_ge(pe_s, used[d])
                        load(d, late, loaded_late[d], at_o[d], at_v[d])
                    if with_y:
                        for d in range(2):
                            sp.wait_ge(dve_s, y_ready[d])
                            store(d, at_y[d])
                if with_y:
                    for d in range(2):
                        sp.wait_ge(dve_s, dve_o.value(f"Y.1@{d}", n - 1))
                        store(d, (n - 1) * NY if d == 0 else 0)
                    for d in range(2):
                        sp.wait_ge(y_stored[d], (n + 1) * 16)

            @block.tensor
            def _(pe):
                pe_o.start(pe)
                pe.wait_ge(cleared, 1)
                with pe.Fori(0, n) as i:
                    I_ = g["ident"]

                    def free(stage, d, h):
                        j = stages.index(stage)
                        same = [k for k in range(len(stages)) if k % 2 == j % 2]
                        old, back = (stages[j - 2], 0) if j >= 2 else (stages[same[-1]], 1)
                        o = act_o if old in by_act else dve_o
                        pe.wait_ge(o.sem, o.value(f"{old}.{h}@{d}", i, back))

                    def products(stage, d, h, terms):
                        out = ps(stage, d, h)
                        for q in range(H):
                            p = H * h + q
                            for j, (lhs, rhs) in enumerate(terms):
                                last = pe.matmul(out[:, q, :], lhs(p), rhs(p), start=(j == 0), stop=(j == len(terms) - 1))
                        pe_o.done(f"{stage}.{h}@{d}", last)

                    def turns(stage, d, h, src):
                        out = ps(stage, d, h)
                        for q in range(H):
                            last = pe.transpose(out[:, q, :], src[:, H * h + q, :], I_)
                        pe_o.done(f"{stage}.{h}@{d}", last)

                    def on_act(name, d, h):
                        pe.wait_ge(act_s, act_o.value(f"{name}.{h}@{d}", i))

                    def on_dve(name, d, h):
                        pe.wait_ge(dve_s, dve_o.value(f"{name}.{h}@{d}", i))

                    m = lambda x: (lambda p: x[:, p, :])
                    dh = [(d, h) for d in range(2) for h in range(2)]
                    for stage in ("B", "Kh"):
                        for d, h in dh:
                            if stage == "B" and h == 0:
                                pe.wait_ge(loaded_early[d], (i + 1) * 16 * (1 + 2 * len(early)))
                            free(stage, d, h)
                            products(stage, d, h, [(m(bd[d][stage]), lambda p: KR[d][:, p, :, :].rearrange("p b t -> p (b t)"))])
                    for stage, x in (("Bt", "B"), ("Kt", "Kh"), ("Vt", "V")):
                        for d, h in dh:
                            free(stage, d, h)
                            turns(stage, d, h, bd[d][x])
                    for d, h in dh:
                        free("T1", d, h)
                        on_dve("Tt1", d, h)
                        turns("T1", d, h, W[d]["Tt"])
                    for b in (*LEVELS, 32):
                        for d, h in dh:
                            free(f"G{b}", d, h)
                            if b == 2:
                                on_act("T1", d, h)
                            else:
                                on_dve(f"X{b // 2}", d, h)
                            products(f"G{b}", d, h, [(m(W[d]["M"]), m(W[d]["T"]))])
                        for d, h in dh:
                            free(f"X{b}", d, h)
                            on_act(f"G{b}", d, h)
                            if b > 2:
                                on_act(f"Tt{b // 2}", d, h)
                            lhs, rhs = ("Tt", "G") if b < 32 else ("G", "Tt")
                            products(f"X{b}", d, h, [(m(W[d][lhs]), m(W[d][rhs]))])
                        if b < 32:
                            for d, h in dh:
                                free(f"Tt{b}", d, h)
                                on_dve(f"X{b}", d, h)
                                turns(f"Tt{b}", d, h, W[d]["T"])
                    for d, h in dh:
                        if h == 0:
                            pe.wait_ge(loaded_late[d], (i + 1) * 16 * 2 * len(late))
                        pe.wait_ge(dve_s, dve_o.value(f"S.{h}@{d}", i, 1))
                        free("X", d, h)
                        products("X", d, h, [(m(bd[d]["K"]), m(S[d])), (m(W[d]["Aak"]), m(W[d]["Vt"]))])
                    for d, h in dh:
                        free("U", d, h)
                        on_act("X", d, h)
                        products("U", d, h, [(m(W[d]["Tt"]), m(W[d]["G"]))])
                    if with_y:
                        for d, h in dh:
                            free("Y", d, h)
                            on_act("U", d, h)
                            products("Y", d, h, [(m(S[d]), m(bd[d]["R"])), (m(W[d]["U"]), m(W[d]["Arb"])), (m(W[d]["Vt"]), m(W[d]["Ark"]))])
                    for d, h in dh:
                        free("S", d, h)
                        on_act("U", d, h)
                        products("S", d, h, [(m(W[d]["Bt"]), m(W[d]["U"])), (m(W[d]["Kt"]), m(W[d]["Vt"]))])

            @block.scalar
            def _(act):
                act_o.start(act)
                with act.Fori(0, n) as i:
                    def copy(stage, dst, scale=1.0):
                        for d in range(2):
                            for h in range(2):
                                act.wait_ge(pe_s, pe_o.value(f"{stage}.{h}@{d}", i))
                                act_o.done(f"{stage}.{h}@{d}", act.activation(half(W[d][dst], h), ps(stage, d, h)[:, :, :], ACT.Copy, scale=scale))

                    for stage, dst in (("Bt", "Bt"), ("Kt", "Kt"), ("Vt", "Vt"), ("T1", "T")):
                        copy(stage, dst)
                    for b in (*LEVELS, 32):
                        copy(f"G{b}", "G", -1.0)
                        if b < 32:
                            copy(f"Tt{b}", "Tt")
                    copy("X", "G")
                    copy("U", "U", -1.0)

            @block.vector
            def _(dve):
                dve_o.start(dve)
                for d in range(2):
                    for x in early + late:
                        dve.memset(bd[d][x][:, :, :], 0.0)
                dve.drain().then_inc(cleared, 1)
                mask = lambda nm: g["mask"](nm).unsqueeze(1).to_broadcast([P, H, P])
                wide = lambda nm: g["mask"](nm).rearrange("p (a t) -> p a t", a=2).unsqueeze(1).to_broadcast([P, H, 2, C])
                spread = lambda x: x.unsqueeze(2).to_broadcast([P, H, 2, C])
                four = lambda x: x.rearrange("p h (a t) -> p h a t", a=2)
                dh = [(d, h) for d in range(2) for h in range(2)]
                with dve.Fori(0, n) as i:
                    dve.drain()
                    for d in range(2):
                        chunk = dve.snap(i + first) if d == 0 else dve.snap(i * -1 + (first + n - 1))
                        dve.tensor_copy(PC[:, d, :], g["decay_end"][:, d, ds(chunk, 1), :].rearrange("p a i -> p (a i)"))

                    def product(stage, d, h):
                        dve.wait_ge(pe_s, pe_o.value(f"{stage}.{h}@{d}", i))
                        return ps(stage, d, h)

                    for stage, first_m, second_m in (("B", "M", "Arb"), ("Kh", "Aak", "Ark")):
                        for d, h in dh:
                            strict, incl = sets[d][:2]
                            src = product(stage, d, h)
                            last = dve.tensor_tensor(four(half(W[d][first_m], h)), spread(src[:, :, 0:C]), wide(strict), ALU.mult)
                            if with_y:
                                last = dve.tensor_tensor(four(half(W[d][second_m], h)), spread(src[:, :, C:P]), wide(incl), ALU.mult)
                            dve_o.done(f"{stage}.{h}@{d}", last)
                    dve.drain()
                    for d, h in dh:
                        tt = half(W[d]["Tt"], h)
                        dve.tensor_tensor(tt, half(W[d]["M"], h), mask(sets[d][2]), ALU.mult)
                        dve.drain()
                        dve_o.done(f"Tt1.{h}@{d}", dve.scalar_tensor_tensor(out=tt, in0=tt, scalar=-1.0, in1=mask("ident"), op0=ALU.mult, op1=ALU.add))
                    for b in (*LEVELS, 32):
                        for d, h in dh:
                            src = product(f"X{b}", d, h)
                            dve.sem_inc(x_seen, 1)
                            mk = mask(f"{sets[d][3]}{b}" if b < 32 else sets[d][4]).bitcast(U32)
                            dve_o.done(f"X{b}.{h}@{d}", dve.copy_predicated(half(W[d]["T" if b < 32 else "Tt"], h), mk, src[:, :, :]))
                    if with_y:
                        for d, h in dh:
                            if h == 0:
                                dve.wait_ge(y_stored[d], (i + 1) * 16)
                            src = product("Y", d, h)
                            for hh in range(2):
                                q = slice(64 * hh, 64 * hh + 64)
                                last = dve.tensor_copy(yc[d][q, H * h:H * h + H, :], src[q, :, q])
                            dve_o.done(f"Y.{h}@{d}", last)
                    for d, h in dh:
                        src = product("S", d, h)
                        dve.tensor_tensor(half(S[d], h), half(S[d], h), src[:, :, :], ALU.add)
                        dve.drain()
                        dve_o.done(f"S.{h}@{d}", dve.tensor_tensor(half(S[d], h), half(S[d], h), PC[:, d, H * h:H * h + H].unsqueeze(2).to_broadcast([P, H, P]), ALU.mult))


def read_out(nc, g, I, ry):
    with ExitStack() as ctx:
        sb = lambda n, s, d=F32: ctx.enter_context(nc.sbuf_tensor(n, s, d))
        sem = lambda n: ctx.enter_context(nc.semaphore(n))
        g2, b2 = sb("ro_g2", [P, D]), sb("ro_b2", [P, KT])
        y = sb("ro_y", [P, 2, KT, SEQ])
        sq, rs = sb("ro_sq", [P, 2, SEQ]), sb("ro_rs", [P, 2, SEQ])
        gates = [ctx.enter_context(nc.psum_tensor(f"ro_gate{k}", [P, SEQ], F32)) for k in range(2)]
        means = [ctx.enter_context(nc.psum_tensor(f"ro_mean{k}", [P, SEQ], F32)) for k in range(3)]
        varis = [ctx.enter_context(nc.psum_tensor(f"ro_var{k}", [P, SEQ], F32)) for k in range(3)]
        loaded, y_loaded = sem("ro_loaded"), [sem(f"ro_y{k}") for k in range(2)]
        mean_s, cen_s, sq_s, var_s, rs_s, yn_s = sem("ro_means"), sem("ro_centred"), sem("ro_squared"), sem("ro_vars"), sem("ro_rstd"), sem("ro_normed")
        gate, gated = sem("ro_gates"), sem("ro_gated")
        chan = g["chan"]
        N = 2 * KT
        with nc.Block() as block:
            @block.sync
            def _(sp):
                sp.dma_start(g2[:, :], I["g2"]).then_inc(loaded, 16)
                for k in range(KT):
                    for d in range(2):
                        src = g["y_chunks"][d:d + 1, :].rearrange("a (c p i t) -> (a p) i c t", c=LAT_CHUNKS, p=P, i=KT)
                        sp.dma_start(y[:, d, k, :].rearrange("p (c t) -> p c t", t=C), src[:, k, :, :]).then_inc(y_loaded[k // (KT // 2)], 16)

            @block.tensor
            def _(pe):
                pe.wait_ge(loaded, 16)
                for j in range(N + 2):
                    if j < N:
                        if j % KT == 0:
                            pe.wait_ge(y_loaded[j // KT], KT * 16)
                        if j >= 3:
                            pe.wait_ge(cen_s, j - 2)
                        pe.matmul(means[j % 3][:, :], g["mean_w"], y[:, j % 2, j // 2, :], start=True, stop=True).then_inc(mean_s, 1)
                    if j >= 2:
                        t = j - 2
                        pe.wait_ge(sq_s, t + 1)
                        if t >= 3:
                            pe.wait_ge(rs_s, t - 2)
                        pe.matmul(varis[t % 3][:, :], g["mean_w"], sq[:, t % 2, :], start=True, stop=True).then_inc(var_s, 1)
                        if t % 2 == 1:
                            k = t // 2
                            if k >= 2:
                                pe.wait_ge(gated, k - 1)
                            pe.matmul(gates[k % 2][:, :], g2[:, k * P:k * P + P], g["xg"][:, :], start=True, stop=True).then_inc(gate, 1)

            @block.scalar
            def _(act):
                for j in range(N + 2):
                    if j < N:
                        act.wait_ge(cen_s, j + 1)
                        if j >= 2:
                            act.wait_ge(var_s, j - 1)
                        act.activation(sq[:, j % 2, :], y[:, j % 2, j // 2, :], ACT.Square).then_inc(sq_s, 1)
                    if j >= 2:
                        t = j - 2
                        act.wait_ge(var_s, t + 1)
                        if t >= 2:
                            act.wait_ge(yn_s, t - 1)
                        act.activation(rs[:, t % 2, :], varis[t % 3][:, :], ACT.Ln, bias=g["gn_eps"])
                        act.drain()
                        act.activation(rs[:, t % 2, :], rs[:, t % 2, :], ACT.Exp, scale=-0.5).then_inc(rs_s, 1)

            @block.vector
            def _(dve):
                dve.tensor_scalar(b2[:, :], chan[:, 33:41], 2.0, None, ALU.mult)
                for j in range(N + 4):
                    if j < N:
                        dve.wait_ge(mean_s, j + 1)
                        dve.tensor_tensor(y[:, j % 2, j // 2, :], y[:, j % 2, j // 2, :], means[j % 3][:, :], ALU.subtract).then_inc(cen_s, 1)
                    if j >= 3 and j - 3 < N:
                        t = j - 3
                        dve.wait_ge(rs_s, t + 1)
                        yt = y[:, t % 2, t // 2, :]
                        dve.tensor_tensor(yt, yt, rs[:, t % 2, :], ALU.mult).then_inc(yn_s, 1)
                        if t % 2 == 1:
                            k = t // 2
                            out = ry[:, k, :]
                            dve.drain()
                            dve.tensor_tensor(out, y[:, 0, k, :], y[:, 1, k, :], ALU.add)
                            dve.drain()
                            dve.tensor_scalar(out, out, chan[:, 25 + k:26 + k], b2[:, k:k + 1], ALU.mult, ALU.add)
                            dve.drain()
                            dve.tensor_tensor(out, out, g["bonus"][:, k, :], ALU.add)
                            dve.drain()
                            dve.wait_ge(gate, k + 1)
                            dve.tensor_tensor(out, out, gates[k % 2][:, :], ALU.mult).then_inc(gated, 1)


def pooling(nc, g, I, py):
    NT = SEQ // P
    with ExitStack() as ctx:
        sb = lambda n, s, d=F32: ctx.enter_context(nc.sbuf_tensor(n, s, d))
        sem = lambda n: ctx.enter_context(nc.semaphore(n))
        w, pw = sb("pl_w", [P, KT, 512]), sb("pl_pw", [P, 4, P])
        u = sb("pl_u", [P, NT, 512])
        box = sb("pl_box", [P, 2, NT, SEQ])
        diff = sb("pl_diff", [P, 2, SEQ])
        ps = [ctx.enter_context(nc.psum_tensor(f"pl_ps{k}", [P, SEQ], F32)) for k in range(8)]
        loaded, boxed = sem("pl_loaded"), [sem("pl_box0"), sem("pl_box1")]
        u_ps, u_sb, d_ps, d_sb, y_ps = sem("pl_u_ps"), sem("pl_u_sb"), sem("pl_d_ps"), sem("pl_d_sb"), sem("pl_y_ps")
        with nc.Block() as block:
            @block.sync
            def _(sp):
                sp.dma_start(w[:, :, :], I["w_pool"]).then_inc(loaded, 16)
                sp.dma_start(pw[:, :, :], I["pool_w"]).then_inc(loaded, 16)
                for j in range(4):
                    if j >= 2:
                        sp.wait_ge(d_ps, j - 1)
                    sp.dma_start(box[:, j % 2, :, :], I["pool_box"][j]).then_inc(boxed[j % 2], 16)

            @block.tensor
            def _(pe):
                pe.wait_ge(loaded, 32)
                for t in range(NT):
                    for k in range(KT):
                        last = pe.matmul(ps[t][:, :], g["hT"][:, k, CTX + t * P:CTX + t * P + P], w[:, k, :], start=(k == 0), stop=(k == KT - 1))
                    last.then_inc(u_ps, 1)
                pe.wait_ge(u_sb, NT)
                for j in range(4):
                    pe.wait_ge(boxed[j % 2], 16 * (j // 2 + 1))
                    for t in range(NT):
                        last = pe.matmul(ps[4 + j % 2][:, :], u[:, t, j * P:j * P + P], box[:, j % 2, t, :], start=(t == 0), stop=(t == NT - 1))
                    last.then_inc(d_ps, 1)
                    pe.wait_ge(d_sb, j + 1)
                    pe.matmul(ps[j][:, :], pw[:, j, :], diff[:, j % 2, :], start=True, stop=True).then_inc(y_ps, 1)

            @block.vector
            def _(dve):
                for t in range(NT):
                    dve.wait_ge(u_ps, t + 1)
                    dve.tensor_copy(u[:, t, :], ps[t][:, :]).then_inc(u_sb, 1)
                for j in range(4):
                    dve.wait_ge(d_ps, j + 1)
                    if j >= 2:
                        dve.wait_ge(y_ps, j - 1)
                    dve.tensor_copy(diff[:, j % 2, :], ps[4 + j % 2][:, :]).then_inc(d_sb, 1)

            @block.scalar
            def _(act):
                for j in range(4):
                    act.wait_ge(y_ps, j + 1)
                    act.activation(py[:, j, :], ps[j][:, :], ACT.Copy, scale=g["chan"][:, 41 + j:42 + j])


MG = 2 * KT + 4 + KT


def merge(nc, g, I, py, ry, merged):
    with ExitStack() as ctx:
        sb = lambda n, s, d=F32: ctx.enter_context(nc.sbuf_tensor(n, s, d))
        sem = lambda n: ctx.enter_context(nc.semaphore(n))
        w = sb("mg_w", [P, 2, MG, P])
        sig = sb("mg_sig", [P, 2, 2, SEQ])
        ps = [[ctx.enter_context(nc.psum_tensor(f"mg_ps{u}{k}", [P, SEQ], F32)) for k in range(4)] for u in range(2)]
        loaded = [sem("mg_loaded0"), sem("mg_loaded1")]
        pe_s, act_s, dve_s = sem("mg_pe"), sem("mg_act"), sem("mg_dve")
        pe_o = Order(pe_s, ["gp", "gr", "pp", "rp"])
        act_o = Order(act_s, ["gp", "gr"])
        dve_o = Order(dve_s, ["pp", "rp", "out"])
        hT = g["hT"]
        NW = P * MG * P
        with nc.Block() as block:
            @block.sync
            def _(sp):
                for u in range(2):
                    sp.dma_start(w[:, u, :, :], I["w_merge"][u].rearrange("p (m n) -> p m n", m=MG)).then_inc(loaded[u], 16)
                with sp.Fori(0, KT // 2 - 1) as i:
                    for u in range(2):
                        at = sp.snap(i * 2 * NW + (u + 2) * NW)
                        sp.wait_ge(pe_s, i * 8 + 4 * u + 4)
                        sp.dma_start(w[:, u, :, :], flat(I["w_merge"], at, NW).rearrange("(p m n) -> p m n", p=P, m=MG)).then_inc(loaded[u], 16)

            @block.tensor
            def _(pe):
                with pe.Fori(0, KT // 2) as i:
                    for u in range(2):
                        m = i * 2 + u
                        pe.wait_ge(loaded[u], (i + 1) * 16)
                        pe.wait_ge(dve_s, i * 6)
                        for name, w0, n, src in (("gp", 0, KT, None), ("gr", KT, KT, None), ("pp", 2 * KT, 4, py), ("rp", 2 * KT + 4, KT, ry)):
                            for k in range(n):
                                rhs = hT[:, k, CTX:TOK] if src is None else src[:, k, :]
                                last = pe.matmul(ps[u]["gp gr pp rp".split().index(name)][:, :], w[:, u, w0 + k, :], rhs, start=(k == 0), stop=(k == n - 1))
                            pe_o.done(name, last)

            @block.scalar
            def _(act):
                with act.Fori(0, KT // 2) as i:
                    for u in range(2):
                        m = i * 2 + u
                        for k, name in enumerate(("gp", "gr")):
                            act.wait_ge(pe_s, m * 4 + k + 1)
                            if k == 0:
                                act.wait_ge(dve_s, i * 6)
                            act_o.done(name, act.activation(sig[:, u, k, :], ps[u][k][:, :], ACT.Sigmoid))

            @block.vector
            def _(dve):
                with dve.Fori(0, KT // 2) as i:
                    for u in range(2):
                        m = i * 2 + u
                        mr = dve.snap(i * 2 + u)
                        for k, name in enumerate(("pp", "rp")):
                            dve.wait_ge(act_s, m * 2 + k + 1)
                            dve.wait_ge(pe_s, m * 4 + 3 + k)
                            dve_o.done(name, dve.tensor_tensor(sig[:, u, k, :], sig[:, u, k, :], ps[u][2 + k][:, :], ALU.mult))
                        dve.drain()
                        dve_o.done("out", dve.tensor_tensor(merged[:, ds(mr, 1), :], sig[:, u, 0:1, :], sig[:, u, 1:2, :], ALU.add))


def project_out(nc, g, I, merged, x1, logits):
    NT = SEQ // P
    with ExitStack() as ctx:
        sb = lambda n, s, d=F32: ctx.enter_context(nc.sbuf_tensor(n, s, d))
        sem = lambda n: ctx.enter_context(nc.semaphore(n))
        w = sb("po_w", [P, KT, D])
        rows = sb("po_rows", [P, 3, D])
        gains = sb("po_gains", [P, 2, D])
        rw, rb = sb("po_rw", [P, KT, 36]), sb("po_rb", [1, 36])
        sq = sb("po_sq", [P, D])
        f = sb("po_f", [P, 2, D])
        fT = sb("po_fT", [P, 2, KT, P])
        st = sb("po_st", [P, NT, 8])
        ps = [ctx.enter_context(nc.psum_tensor(f"po_ps{k}", [P, D], F32)) for k in range(2)]
        pt = ctx.enter_context(nc.psum_tensor("po_pt", [P, KT, P], F32))
        pl = ctx.enter_context(nc.psum_tensor("po_pl", [P, NT, P], F32))
        loaded, xload = sem("po_loaded"), sem("po_x")
        rows_ready = sem("po_rows_ready")
        pe_m, pe_t, pe_l = sem("po_product"), sem("po_turned"), sem("po_logits")
        act_sum, act_root, act_fT = sem("po_sum"), sem("po_root"), sem("po_fT_ready")
        dve_mean, dve_x, dve_f = sem("po_mean"), sem("po_x1"), sem("po_f_ready")
        fst = [sem("po_fst0"), sem("po_fst1")]
        with nc.Block() as block:
            @block.sync
            def _(sp):
                sp.dma_start(w[:, :, :], I["w_out"]).then_inc(loaded, 16)
                sp.dma_start(rw[:, :, :], I["router_w"]).then_inc(loaded, 16)
                sp.dma_start(rb[:, :], I["router_b"]).then_inc(loaded, 16)
                sp.dma_start(rows[:, :, :], g["mod_rows"][:, 0:3 * D].rearrange("p (a n) -> p a n", a=3)).then_inc(loaded, 16)
                for j in range(2):
                    sp.dma_start(gains[:, j, :], I["gains"][j:j + 1, :].to_broadcast([P, D])).then_inc(loaded, 16)
                for t in range(NT):
                    sp.dma_start(x1[:, t, :], I["x"][t * P:t * P + P, :]).then_inc(xload, 16)
                for t in range(NT):
                    sp.wait_ge(dve_f, t + 1)
                    sp.dma_start(g["f_dram"][t * P:t * P + P, :], f[:, t % 2, :]).then_inc(fst[t % 2], 16)
                for u in range(2):
                    sp.wait_ge(fst[u], NT // 2 * 16)

            @block.tensor
            def _(pe):
                pe.wait_ge(loaded, 96)

                def product(t):
                    if t >= 2:
                        pe.wait_ge(dve_x, t - 1)
                    for h in range(2):
                        for k in range(KT):
                            last = pe.matmul(ps[t % 2][:, h * 512:h * 512 + 512], merged[:, k, t * P:t * P + P], w[:, k, h * 512:h * 512 + 512], start=(k == 0), stop=(k == KT - 1))
                    last.then_inc(pe_m, 1)

                def turn(t):
                    pe.wait_ge(dve_f, t + 1)
                    if t:
                        pe.wait_ge(act_fT, t)
                    for k in range(KT):
                        last = pe.transpose(pt[:, k, :], f[:, t % 2, k * P:k * P + P], g["ident"])
                    last.then_inc(pe_t, 1)

                def route(t):
                    pe.wait_ge(act_fT, t + 1)
                    for k in range(KT):
                        pe.matmul(pl[:, t, 0:36], fT[:, t % 2, k, :], rw[:, k, :], start=(k == 0), stop=False)
                    pe.matmul(pl[:, t, 0:36], g["mask"]("ones")[0:1, :], rb[:, :], start=False, stop=True).then_inc(pe_l, 1)

                product(0)
                for t in range(NT):
                    if t + 1 < NT:
                        product(t + 1)
                    turn(t)
                    route(t)

            @block.scalar
            def _(act):
                for t in range(NT):
                    act.wait_ge(pe_m, t + 1)
                    act.activation(sq[:, :], ps[t % 2][:, :], ACT.Square, accum_out=st[:, t, 0:1])
                    act.drain().then_inc(act_sum, 1)
                    act.wait_ge(dve_mean, 2 * t + 1)
                    act.activation(st[:, t, 2:3], st[:, t, 1:2], ACT.Sqrt).then_inc(act_root, 1)
                    act.wait_ge(dve_x, t + 1)
                    act.activation(sq[:, :], x1[:, t, :], ACT.Square, accum_out=st[:, t, 4:5])
                    act.drain().then_inc(act_sum, 1)
                    act.wait_ge(dve_mean, 2 * t + 2)
                    act.activation(st[:, t, 6:7], st[:, t, 5:6], ACT.Sqrt).then_inc(act_root, 1)
                    act.wait_ge(pe_t, t + 1)
                    if t >= 2:
                        act.wait_ge(pe_l, t - 1)
                    act.activation(fT[:, t % 2, :, :], pt[:, :, :], ACT.Copy).then_inc(act_fT, 1)

            @block.vector
            def _(dve):
                dve.wait_ge(loaded, 96)
                dve.tensor_tensor(rows[:, 0, :], rows[:, 0, :], gains[:, 0, :], ALU.mult)
                dve.scalar_tensor_tensor(out=rows[:, 2, :], in0=rows[:, 2, :], scalar=1.0, in1=gains[:, 1, :], op0=ALU.add, op1=ALU.mult)
                dve.wait_ge(xload, NT * 16)
                dve.drain()
                for t in range(NT):
                    dve.wait_ge(act_sum, 2 * t + 1)
                    dve.tensor_scalar(st[:, t, 1:2], st[:, t, 0:1], 1.0 / D, RMS_EPS, ALU.mult, ALU.add).then_inc(dve_mean, 1)
                    dve.wait_ge(act_root, 2 * t + 1)
                    dve.reciprocal(st[:, t, 3:4], st[:, t, 2:3])
                    dve.drain()
                    if t >= 2:
                        dve.wait_ge(pe_t, t - 1)
                        dve.wait_ge(fst[t % 2], 16 * (t // 2))
                    ft = f[:, t % 2, :]
                    dve.scalar_tensor_tensor(out=ft, in0=ps[t % 2][:, :], scalar=st[:, t, 3:4], in1=rows[:, 0, :], op0=ALU.mult, op1=ALU.mult)
                    dve.drain()
                    dve.tensor_tensor(x1[:, t, :], x1[:, t, :], ft, ALU.add).then_inc(dve_x, 1)
                    dve.wait_ge(act_sum, 2 * t + 2)
                    dve.tensor_scalar(st[:, t, 5:6], st[:, t, 4:5], 1.0 / D, RMS_EPS, ALU.mult, ALU.add).then_inc(dve_mean, 1)
                    dve.wait_ge(act_root, 2 * t + 2)
                    dve.reciprocal(st[:, t, 7:8], st[:, t, 6:7])
                    dve.drain()
                    dve.scalar_tensor_tensor(out=ft, in0=x1[:, t, :], scalar=st[:, t, 7:8], in1=rows[:, 2, :], op0=ALU.mult, op1=ALU.mult)
                    dve.drain()
                    dve.tensor_tensor(ft, ft, rows[:, 1, :], ALU.add).then_inc(dve_f, 1)
                dve.wait_ge(pe_l, NT)
                dve.tensor_copy(logits[:, :, :], pl[:, :, 0:36])


SLOTS = P
SPILL = 7
TILES = NE + SPILL
EXPERT_W = KT * 2 * FE + 2 * D


def route(nc, g, logits, R):
    NT = SEQ // P
    with ExitStack() as ctx:
        sb = lambda n, s, d=F32: ctx.enter_context(nc.sbuf_tensor(n, s, d))
        sem = lambda n: ctx.enter_context(nc.semaphore(n))
        t4 = lambda n: sb(n, [P, NT, 4])
        t8 = lambda n: sb(n, [P, NT, 8])
        t32 = lambda n: sb(n, [P, NT, NE])
        m1, s1 = sb("rt_m1", [P, NT, 1]), sb("rt_s1", [P, NT, 1])
        eg, tg, gh = t4("rt_eg"), t4("rt_tg"), t4("rt_gh")
        sel, te, oh1, oh2, msk = t8("rt_sel"), t8("rt_te"), t8("rt_oh1"), t8("rt_oh2"), t8("rt_msk")
        e32, O1, O2, both, pre, tmp = (t32(f"rt_x{j}") for j in range(6))
        ma, mb, e2, w1 = (sb(f"rt_m{j}", [P, NT, 1]) for j in "abcd")
        rev = sb("rt_rev", [P, 8])
        base, cnt, over, tmpc, incl = (sb(f"rt_c{j}", [P, NE]) for j in range(5))
        zero = sb("rt_zero", [P, TILES])
        zero_rows = sb("rt_zero_rows", [P, D])
        ovq = sb("rt_ovq", [P, SPILL])
        tokid = sb("rt_tokid", [P, NT])
        table = sb("rt_table", [TILES, P])
        ps = ctx.enter_context(nc.psum_tensor("rt_ps", [P, NT + 1, NE], F32))
        pt = ctx.enter_context(nc.psum_tensor("rt_pt", [P, TILES], F32))
        ex, ex_done, cst, both_ready, pref = sem("rt_exp_in"), sem("rt_exp"), sem("rt_cst"), sem("rt_both"), sem("rt_prefix")
        zeroed, slots_ready, scattered, tab, turned = sem("rt_zeroed"), sem("rt_slots"), sem("rt_scattered"), sem("rt_tab"), sem("rt_turned")
        rows_cleared = sem("rt_rows_cleared")
        X = AX.X
        with nc.Block() as block:
            @block.sync
            def _(sp):
                sp.wait_ge(cst, 1)
                for q in range(SPILL):
                    sp.dma_start(g["y_dram"][(NE + q) * SLOTS:(NE + q + 1) * SLOTS, :], zero_rows[:, :]).then_inc(rows_cleared, 16)
                sp.wait_ge(rows_cleared, SPILL * 16)

            @block.gpsimd
            def _(pool):
                pool.iota(rev[:, :], [[-1, 8]], base=8, channel_multiplier=0, allow_small_or_imprecise_dtypes=True)
                pool.iota(base[:, :], [[SLOTS, NE]], base=0, channel_multiplier=0, allow_small_or_imprecise_dtypes=True)
                pool.iota(tokid[:, :], [[P, NT]], base=0, channel_multiplier=1, allow_small_or_imprecise_dtypes=True)
                pool.memset(zero[:, :], 0.0)
                pool.memset(zero_rows[:, :], 0.0)
                pool.drain().then_inc(cst, 1)
                pool.wait_ge(cst, 1)
                pool.dma_start(g["slot_tok"].rearrange("(p n) a -> p (n a)", p=P), zero[:, :]).then_inc(zeroed, 16)
                pool.wait_ge(zeroed, 16)
                pool.wait_ge(slots_ready, 1)
                for t in range(NT):
                    for j in range(2):
                        pool.indirect_dma_start(out=g["slot_tok"], out_offset=bass.IndirectOffsetOnAxis(ap=R["slot"][:, j, t:t + 1], axis=0),
                                                in_=tokid[:, t:t + 1], in_offset=None).then_inc(scattered, 16)
                pool.wait_ge(scattered, 2 * NT * 16)
                pool.dma_start(table[:, :], g["slot_tok"].rearrange("(t s) a -> t (s a)", t=TILES)).then_inc(tab, 16)

            @block.scalar
            def _(act):
                act.wait_ge(ex, 1)
                act.activation(eg[:, :, :], tg[:, :, :], ACT.Exp).then_inc(ex_done, 1)
                act.wait_ge(ex, 2)
                act.activation(e2[:, :, :], mb[:, :, :], ACT.Exp).then_inc(ex_done, 1)

            @block.tensor
            def _(pe):
                pe.wait_ge(both_ready, 1)
                for t in range(NT + 1):
                    for q in range(t):
                        last = pe.matmul(ps[:, t, :], g["mask"]("ones"), both[:, q, :], start=(q == 0), stop=(t == NT and q == t - 1))
                    if t < NT:
                        last = pe.matmul(ps[:, t, :], g["mask"]("before"), both[:, t, :], start=(t == 0), stop=True)
                last.then_inc(pref, 1)
                pe.wait_ge(tab, 16)
                pe.transpose(pt[:, :], table[:, :], g["ident"][0:TILES, 0:TILES]).then_inc(turned, 1)

            @block.vector
            def _(dve):
                def tt(o, a, b, op):
                    dve.tensor_tensor(o, a, b, op)
                    dve.drain()

                def ts(o, a, s0, s1_, op0, op1=ALU.bypass):
                    dve.tensor_scalar(o, a, s0, s1_, op0, op1)
                    dve.drain()

                def red(o, a, op):
                    dve.tensor_reduce(o, a, X, op)
                    dve.drain()

                def first_hot(out, score, best, n, tmp_):
                    red(best, score, ALU.max)
                    tt(tmp_, score, best.to_broadcast([P, NT, n]), ALU.is_equal)
                    tt(tmp_, tmp_, rev[:, 8 - n:8].unsqueeze(1).to_broadcast([P, NT, n]), ALU.mult)
                    red(s1[:, :, :], tmp_, ALU.max)
                    tt(out, tmp_, s1[:, :, :].to_broadcast([P, NT, n]), ALU.is_equal)

                gl = logits[:, :, 0:4]
                el = logits[:, :, 4:36]
                dve.wait_ge(cst, 1)
                first_hot(gh[:, :, :], gl, m1[:, :, :], 4, tg[:, :, :])
                tt(tg[:, :, :], gl, m1[:, :, :].to_broadcast([P, NT, 4]), ALU.subtract)
                dve.drain().then_inc(ex, 1)
                for q in range(4):
                    src = el[:, :, 8 * q:8 * q + 8]
                    if q == 0:
                        tt(sel[:, :, :], src, gh[:, :, 0:1].to_broadcast([P, NT, 8]), ALU.mult)
                    else:
                        tt(te[:, :, :], src, gh[:, :, q:q + 1].to_broadcast([P, NT, 8]), ALU.mult)
                        tt(sel[:, :, :], sel[:, :, :], te[:, :, :], ALU.add)
                first_hot(oh1[:, :, :], sel[:, :, :], ma[:, :, :], 8, te[:, :, :])
                dve.scalar_tensor_tensor(out=msk[:, :, :], in0=oh1[:, :, :], scalar=-3.0e38, in1=sel[:, :, :], op0=ALU.mult, op1=ALU.add)
                dve.drain()
                first_hot(oh2[:, :, :], msk[:, :, :], mb[:, :, :], 8, te[:, :, :])
                tt(mb[:, :, :], mb[:, :, :], ma[:, :, :], ALU.subtract)
                dve.drain().then_inc(ex, 1)
                for o, oh in ((O1, oh1), (O2, oh2)):
                    for q in range(4):
                        dve.tensor_tensor(o[:, :, 8 * q:8 * q + 8], oh[:, :, :], gh[:, :, q:q + 1].to_broadcast([P, NT, 8]), ALU.mult)
                dve.drain()
                tt(both[:, :, :], O1[:, :, :], O2[:, :, :], ALU.add)
                dve.drain().then_inc(both_ready, 1)
                dve.wait_ge(ex_done, 2)
                red(m1[:, :, :], eg[:, :, :], ALU.add)
                dve.reciprocal(m1[:, :, :], m1[:, :, :])
                ts(w1[:, :, :], e2[:, :, :], 1.0, None, ALU.add)
                dve.reciprocal(w1[:, :, :], w1[:, :, :])
                dve.drain()
                gate = lambda j: R["gate"][:, j, :].unsqueeze(2)
                tt(gate(0), m1[:, :, :], w1[:, :, :], ALU.mult)
                tt(gate(1), gate(0), e2[:, :, :], ALU.mult)
                dve.wait_ge(pref, 1)
                dve.tensor_copy(pre[:, :, :], ps[:, 0:NT, :])
                dve.tensor_copy(cnt[:, :], ps[:, NT, :])
                dve.drain()
                ts(over[:, :], cnt[:, :], float(SLOTS), None, ALU.is_gt)
                for j in (2, 3):
                    dve.scalar_tensor_tensor(out=over[:, :], in0=cnt[:, :], scalar=float(j * SLOTS), in1=over[:, :], op0=ALU.is_gt, op1=ALU.add)
                    dve.drain()
                ts(tmpc[:, :], over[:, :], 0.0, 1.0, ALU.mult, ALU.add)
                dve.tensor_tensor_scan(incl[:, :], tmpc[:, :], over[:, :], 0.0, ALU.mult, ALU.add)
                dve.drain()
                for q in range(SPILL):
                    dve.tensor_scalar(tmpc[:, :], incl[:, :], float(q), None, ALU.is_le)
                    dve.drain()
                    dve.tensor_reduce(ovq[:, q:q + 1], tmpc[:, :], X, ALU.add)
                    dve.drain()
                ts(ovq[:, :], ovq[:, :], float(NE - 1), None, ALU.min)
                dve.tensor_copy(R["spill_expert"][:, :], ovq[:, :])
                dve.tensor_copy(R["spill_tiles"][:, :], incl[:, NE - 1:NE])
                tt(tmpc[:, :], incl[:, :], over[:, :], ALU.subtract)
                ts(tmpc[:, :], tmpc[:, :], float(SLOTS), float((NE - 1) * SLOTS), ALU.mult, ALU.add)
                tt(tmpc[:, :], tmpc[:, :], base[:, :], ALU.subtract)
                ts(tmp[:, :, :], pre[:, :, :], float(SLOTS), None, ALU.is_ge)
                tt(tmp[:, :, :], tmp[:, :, :], tmpc[:, :].unsqueeze(1).to_broadcast([P, NT, NE]), ALU.mult)
                tt(pre[:, :, :], pre[:, :, :], tmp[:, :, :], ALU.add)
                tt(pre[:, :, :], pre[:, :, :], base[:, :].unsqueeze(1).to_broadcast([P, NT, NE]), ALU.add)
                for j, o in enumerate((O1, O2)):
                    tt(o[:, :, :], o[:, :, :], pre[:, :, :], ALU.mult)
                    red(s1[:, :, :], o[:, :, :], ALU.add)
                    dve.tensor_copy(R["slot"][:, j, :], s1[:, :, :].rearrange("p t a -> p (t a)"))
                    dve.drain()
                dve.drain().then_inc(slots_ready, 1)
                dve.wait_ge(turned, 1)
                dve.tensor_copy(R["tok"][:, :], pt[:, :])


def experts(nc, g, I, R):
    with ExitStack() as ctx:
        sb = lambda n, s, d=F32: ctx.enter_context(nc.sbuf_tensor(n, s, d))
        sem = lambda n: ctx.enter_context(nc.semaphore(n))
        w = sb("ex_w", [P, 2, EXPERT_W])
        idx = sb("ex_idx", [P, 2, 1], U32)
        xe = sb("ex_x", [P, 2, D])
        xT = sb("ex_xT", [P, 2, KT, P])
        sg = sb("ex_sig", [P, 2, FE])
        h = sb("ex_h", [P, 2, FE])
        hT = sb("ex_hT", [P, 2, 2, P])
        y = sb("ex_y", [P, 2, D])
        p_x = ctx.enter_context(nc.psum_tensor("ex_px", [P, KT, P], F32))
        p_gu = [ctx.enter_context(nc.psum_tensor(f"ex_pgu{u}", [P, 2 * FE], F32)) for u in range(2)]
        p_h = [ctx.enter_context(nc.psum_tensor(f"ex_ph{u}", [P, 2, P], F32)) for u in range(2)]
        p_y = ctx.enter_context(nc.psum_tensor("ex_py", [P, D], F32))
        NWE = P * EXPERT_W
        gu = lambda u: w[:, u, 0:KT * 2 * FE].rearrange("p (k n) -> p k n", k=KT)
        dn = lambda u: w[:, u, KT * 2 * FE:].rearrange("p (k n) -> p k n", k=2)

        def run(tag, pairs, spill):
            wl, gath, yst = [sem(f"{tag}_w{u}") for u in range(2)], [sem(f"{tag}_g{u}") for u in range(2)], [sem(f"{tag}_y{u}") for u in range(2)]
            s = {n: sem(f"{tag}_{n}") for n in ("turned", "xT", "gu", "sig", "h", "hturned", "hT", "down", "y", "idx", "seen", "seen2", "stored")}
            U = 1 if spill else 2
            with nc.Block() as block:
                def loop(eng, body):
                    if not spill:
                        with eng.Fori(0, pairs) as i:
                            for u in range(2):
                                body(i, u, i * 2 + u)
                    else:
                        count = eng.value_load(R["spill_tiles"][0:1, 0:1], min_val=0, max_val=SPILL)
                        with eng.Fori(0, SPILL) as i:
                            with eng.If(count > i):
                                body(i, 0, i)

                @block.sync
                def _(sp):
                    def body(i, u, t):
                        if spill:
                            e = sp.value_load(R["spill_expert"][0:1, ds(i, 1)], min_val=0, max_val=NE - 1)
                            at = sp.snap(e * NWE)
                            at_y = sp.snap(i * (SLOTS * D) + NE * SLOTS * D)
                            sp.wait_ge(s["down"], i)
                        else:
                            at = sp.snap(i * 2 * NWE + u * NWE)
                            at_y = sp.snap(i * 2 * SLOTS * D + u * SLOTS * D)
                            sp.wait_ge(s["down"], i * 2 + u - 1 if u else i * 2)
                        return at, at_y

                    def load(u, at):
                        sp.dma_start(w[:, u, :], flat(I["w_experts"], at, NWE).rearrange("(p n) -> p n", p=P)).then_inc(wl[u], 16)

                    def store(u, at_y):
                        sp.dma_start(flat(g["y_dram"], at_y, SLOTS * D).rearrange("(p n) -> p n", p=P), y[:, u, :]).then_inc(yst[u], 16)

                    if spill:
                        def one(i, u, t):
                            at, at_y = body(i, u, t)
                            load(0, at)
                            sp.wait_ge(s["y"], i + 1)
                            store(0, at_y)
                            sp.wait_ge(yst[0], i * 16 + 16)
                            sp.sem_inc(s["stored"], 1)
                        loop(sp, one)
                    else:
                        for u in range(2):
                            load(u, u * NWE)
                        with sp.Fori(0, pairs - 1) as i:
                            for u in range(2):
                                at = sp.snap(i * 2 * NWE + (u + 2) * NWE)
                                at_y = sp.snap(i * 2 * SLOTS * D + u * SLOTS * D)
                                sp.wait_ge(s["down"], i * 2 + u + 1)
                                load(u, at)
                                sp.wait_ge(s["y"], i * 2 + u + 1)
                                store(u, at_y)
                        for u in range(2):
                            t = 2 * pairs - 2 + u
                            sp.wait_ge(s["y"], t + 1)
                            store(u, t * SLOTS * D)
                        for u in range(2):
                            sp.wait_ge(yst[u], pairs * 16)

                @block.gpsimd
                def _(pool):
                    def body(i, u, t):
                        tile = pool.snap(i + NE) if spill else pool.snap(i * 2 + u)
                        if spill:
                            pool.wait_ge(s["turned"], i)
                        else:
                            pool.wait_ge(s["turned"], i * 2)
                        pool.sem_inc(s["seen"], 1)
                        pool.tensor_copy(idx[:, u, :], R["tok"][:, ds(tile, 1)]).then_inc(s["idx"], 1)
                        pool.wait_ge(s["idx"], i * U + u + 1)
                        pool.sem_inc(s["seen2"], 1)
                        pool.indirect_dma_start(out=xe[:, u, :], out_offset=None, in_=g["f_dram"],
                                                in_offset=bass.IndirectOffsetOnAxis(ap=idx[:, u, 0:1], axis=0)).then_inc(gath[u], 16)
                    loop(pool, body)

                @block.tensor
                def _(pe):
                    def turn(i, u, t):
                        pe.wait_ge(gath[u], (i + 1) * 16)
                        pe.wait_ge(s["xT"], t)
                        for k in range(KT):
                            last = pe.transpose(p_x[:, k, :], xe[:, u, k * P:k * P + P], g["ident"])
                        last.then_inc(s["turned"], 1)

                    def tile(i, u, t, nxt):
                        pe.wait_ge(wl[u], (i + 1) * 16)
                        pe.wait_ge(s["xT"], t + 1)
                        if spill:
                            pe.wait_ge(s["h"], t)
                        else:
                            pe.wait_ge(s["h"], i * 2)
                        for k in range(KT):
                            last = pe.matmul(p_gu[u][:, :], xT[:, u, k, :], gu(u)[:, k, :], start=(k == 0), stop=(k == KT - 1))
                        last.then_inc(s["gu"], 1)
                        if nxt is not None:
                            turn(*nxt)
                        pe.wait_ge(s["h"], t + 1)
                        for k in range(2):
                            last = pe.transpose(p_h[u][:, k, :], h[:, u, k * P:k * P + P], g["ident"])
                        last.then_inc(s["hturned"], 1)
                        pe.wait_ge(s["hT"], t + 1)
                        pe.wait_ge(s["y"], t)
                        for q in range(2):
                            for k in range(2):
                                last = pe.matmul(p_y[:, q * 512:q * 512 + 512], hT[:, u, k, :], dn(u)[:, k, q * 512:q * 512 + 512], start=(k == 0), stop=(k == 1))
                        last.then_inc(s["down"], 1)

                    if spill:
                        def one(i, u, t):
                            turn(i, 0, i)
                            tile(i, 0, i, None)
                        loop(pe, one)
                    else:
                        turn(0, 0, 0)
                        with pe.Fori(0, pairs - 1) as i:
                            tile(i, 0, i * 2, (i, 1, i * 2 + 1))
                            tile(i, 1, i * 2 + 1, (i + 1, 0, i * 2 + 2))
                        i = pairs - 1
                        tile(i, 0, i * 2, (i, 1, i * 2 + 1))
                        tile(i, 1, i * 2 + 1, None)

                @block.scalar
                def _(act):
                    def body(i, u, t):
                        act.wait_ge(s["turned"], t + 1)
                        act.wait_ge(s["gu"], i if spill else i * 2)
                        act.activation(xT[:, u, :, :], p_x[:, :, :], ACT.Copy).then_inc(s["xT"], 1)
                        act.wait_ge(s["gu"], t + 1)
                        act.wait_ge(s["h"], i if spill else i * 2)
                        act.activation(sg[:, u, :], p_gu[u][:, 0:FE], ACT.Sigmoid).then_inc(s["sig"], 1)
                        act.wait_ge(s["down"], t + 1)
                        act.wait_ge(yst[u], i * 16)
                        act.activation(y[:, u, :], p_y[:, :], ACT.Copy).then_inc(s["y"], 1)

                    if spill:
                        loop(act, body)
                        return

                    def xt(i, u, t, guard):
                        act.wait_ge(s["turned"], t + 1)
                        if guard is not None:
                            act.wait_ge(s["gu"], guard)
                        act.activation(xT[:, u, :, :], p_x[:, :, :], ACT.Copy).then_inc(s["xT"], 1)

                    def rest(i, u, t, nxt):
                        act.wait_ge(s["gu"], t + 1)
                        act.wait_ge(s["h"], i * 2)
                        act.activation(sg[:, u, :], p_gu[u][:, 0:FE], ACT.Sigmoid).then_inc(s["sig"], 1)
                        if nxt is not None:
                            xt(*nxt)
                        act.wait_ge(s["down"], t + 1)
                        act.wait_ge(yst[u], i * 16)
                        act.activation(y[:, u, :], p_y[:, :], ACT.Copy).then_inc(s["y"], 1)

                    xt(0, 0, 0, None)
                    with act.Fori(0, pairs - 1) as i:
                        rest(i, 0, i * 2, (i, 1, i * 2 + 1, i * 2))
                        rest(i, 1, i * 2 + 1, (i + 1, 0, i * 2 + 2, i * 2 + 1))
                    i = pairs - 1
                    rest(i, 0, i * 2, (i, 1, i * 2 + 1, i * 2))
                    rest(i, 1, i * 2 + 1, None)

                @block.vector
                def _(dve):
                    def body(i, u, t):
                        dve.wait_ge(s["sig"], t + 1)
                        dve.wait_ge(s["hturned"], i if spill else i * 2)
                        dve.tensor_tensor(sg[:, u, :], sg[:, u, :], p_gu[u][:, 0:FE], ALU.mult)
                        dve.drain()
                        dve.tensor_tensor(h[:, u, :], sg[:, u, :], p_gu[u][:, FE:2 * FE], ALU.mult).then_inc(s["h"], 1)
                        dve.wait_ge(s["hturned"], t + 1)
                        dve.wait_ge(s["down"], i if spill else i * 2)
                        dve.tensor_copy(hT[:, u, :, :], p_h[u][:, :, :]).then_inc(s["hT"], 1)
                    loop(dve, body)

        run("ex", NE // 2, False)
        run("sp", None, True)


def combine(nc, g, I, R, x1, out):
    NT = SEQ // P
    with ExitStack() as ctx:
        sb = lambda n, s, d=F32: ctx.enter_context(nc.sbuf_tensor(n, s, d))
        sem = lambda n: ctx.enter_context(nc.semaphore(n))
        rows = sb("cb_rows", [P, NT, 2, D])
        gt, gain = sb("cb_gt", [P, D]), sb("cb_gain", [P, D])
        acc = sb("cb_acc", [P, NT, D])
        sq = sb("cb_sq", [P, D])
        st = sb("cb_st", [P, NT, 4])
        loaded, gath = sem("cb_loaded"), [sem(f"cb_g{t}") for t in range(NT)]
        acc_s, sum_s, mean_s, root_s, out_s, stored = sem("cb_acc_s"), sem("cb_sum"), sem("cb_mean"), sem("cb_root"), sem("cb_out"), sem("cb_stored")
        with nc.Block() as block:
            @block.gpsimd
            def _(pool):
                for t in range(NT):
                    for j in range(2):
                        pool.indirect_dma_start(out=rows[:, t, j, :], out_offset=None, in_=g["y_dram"],
                                                in_offset=bass.IndirectOffsetOnAxis(ap=R["slot"][:, j, t:t + 1], axis=0)).then_inc(gath[t], 16)

            @block.sync
            def _(sp):
                sp.dma_start(gt[:, :], g["mod_rows"][:, 3 * D:4 * D]).then_inc(loaded, 16)
                sp.dma_start(gain[:, :], I["gains"][2:3, :].to_broadcast([P, D])).then_inc(loaded, 16)
                for t in range(NT):
                    sp.wait_ge(out_s, t + 1)
                    sp.dma_start(out[0, t * P:t * P + P, :], acc[:, t, :]).then_inc(stored, 16)
                sp.wait_ge(stored, NT * 16)

            @block.scalar
            def _(act):
                for t in range(NT):
                    act.wait_ge(acc_s, t + 1)
                    act.activation(sq[:, :], acc[:, t, :], ACT.Square, accum_out=st[:, t, 0:1])
                    act.drain().then_inc(sum_s, 1)
                    act.wait_ge(mean_s, t + 1)
                    act.activation(st[:, t, 2:3], st[:, t, 1:2], ACT.Sqrt).then_inc(root_s, 1)

            @block.vector
            def _(dve):
                dve.wait_ge(loaded, 32)
                dve.tensor_tensor(gt[:, :], gt[:, :], gain[:, :], ALU.mult)
                for t in range(NT):
                    dve.wait_ge(gath[t], 32)
                    dve.tensor_scalar(rows[:, t, 0, :], rows[:, t, 0, :], R["gate"][:, 0, t:t + 1], None, ALU.mult)
                    dve.drain()
                    dve.scalar_tensor_tensor(out=acc[:, t, :], in0=rows[:, t, 1, :], scalar=R["gate"][:, 1, t:t + 1], in1=rows[:, t, 0, :], op0=ALU.mult, op1=ALU.add).then_inc(acc_s, 1)
                for t in range(NT):
                    dve.wait_ge(sum_s, t + 1)
                    dve.tensor_scalar(st[:, t, 1:2], st[:, t, 0:1], 1.0 / D, RMS_EPS, ALU.mult, ALU.add).then_inc(mean_s, 1)
                    dve.wait_ge(root_s, t + 1)
                    dve.reciprocal(st[:, t, 3:4], st[:, t, 2:3])
                    dve.drain()
                    dve.scalar_tensor_tensor(out=acc[:, t, :], in0=acc[:, t, :], scalar=st[:, t, 3:4], in1=gt[:, :], op0=ALU.mult, op1=ALU.mult)
                    dve.drain()
                    dve.tensor_tensor(acc[:, t, :], acc[:, t, :], x1[:, t, :], ALU.add).then_inc(out_s, 1)


def layout(a):
    a = {k: np.asarray(v) for k, v in a.items()}
    L = {k: (v[0] if k not in ("x", "ctx", "c", "c_ctx") else v) for k, v in a.items()}
    out = {}
    cols = lambda v: v.reshape(-1, P).T
    out["x"], out["ctx"] = a["x"][0], a["ctx"][0]
    out["cvecs"] = np.stack([cols(a["c"][0]), cols(a["c_ctx"])], 1)
    out["ada_b"] = L["ada_b"][None]
    out["ada_w"] = L["ada_w"].reshape(KT, P, ADA_N, 512).transpose(2, 1, 0, 3)
    out["masks"] = mask_table()
    conv = L["conv_w"]
    chan = np.zeros((P, 64), np.float32)
    chan[:, 0:8] = cols(L["norm_gains"][0])
    for j in range(3):
        chan[:, 16 + 3 * j:19 + 3 * j] = conv[:, 3 * D + j * P:3 * D + (j + 1) * P].T
    chan[:, 25:33], chan[:, 33:41] = cols(L["lnx_w"]), cols(L["lnx_b"])
    chan[:, 41:45] = cols(L["pool_scale"])
    out["chan"] = chan
    win = L["w_in"]
    tiles = lambda w: w.reshape(KT, P, -1, P).transpose(2, 1, 0, 3)
    c0 = 512
    out["w_lr"] = tiles(win[:, c0 + 3 * D:c0 + 3 * D + 3 * P]).transpose(1, 0, 2, 3)
    r, k, v = (tiles(win[:, c0 + j * D:c0 + (j + 1) * D]) for j in range(3))
    w2 = L["w2"].reshape(P, KT, P).transpose(1, 0, 2)[:, :, None]
    a2 = L["a2"].reshape(P, KT, P).transpose(1, 0, 2)[:, :, None]
    out["w_prep"] = np.concatenate([r, k, v, w2, a2], 2).reshape(KT, P, PREPW)
    par = [conv[q, j * D:(j + 1) * D] for j in range(3) for q in range(3)]
    par += [L["w0"][0], L["w0"][1], L["a0"][0], L["a0"][1], L["k_k"], L["k_a"], L["r_k"].reshape(-1)]
    out["p_prep"] = np.stack([q.reshape(KT, P) for q in par], 2)
    out["g2"] = L["g2"]
    out["w_pool"] = win[:, 0:512].reshape(KT, P, 512).transpose(1, 0, 2)
    out["pool_w"] = L["pool_w"].transpose(1, 0, 2)
    out["pool_box"] = pool_table()
    gates = tiles(win[:, 512 + 3456:])
    pp, rp = (w.reshape(-1, P, KT, P).transpose(2, 1, 0, 3) for w in (L["pool_proj"], L["rwkv_proj"]))
    out["w_merge"] = np.concatenate([gates[0:KT], gates[KT:], pp, rp], 2).reshape(KT, P, MG * P)
    out["w_out"] = L["w_out"].reshape(KT, P, D).transpose(1, 0, 2)
    out["router_w"] = np.concatenate([L["router_group_w"], L["router_expert_w"]], 1).reshape(KT, P, 36).transpose(1, 0, 2)
    out["router_b"] = np.concatenate([L["router_group_b"], L["router_expert_b"]])[None]
    out["gains"] = L["norm_gains"][1:4]
    gu = np.concatenate([L["expert_w_gate"], L["expert_w_up"]], 2).reshape(NE, KT, P, 2 * FE).transpose(0, 2, 1, 3).reshape(NE, P, -1)
    dn = L["expert_w_down"].reshape(NE, 2, P, D).transpose(0, 2, 1, 3).reshape(NE, P, -1)
    out["w_experts"] = np.concatenate([gu, dn], 2)
    return {k: np.ascontiguousarray(v) for k, v in out.items()}


def program(nc, I, out):
    with ExitStack() as ctx:
        sb = lambda n, s, d=F32: ctx.enter_context(nc.sbuf_tensor(n, s, d))
        dram = lambda n, s, d=F32: nc.dram_tensor(n, s, d, kind="Internal").ap()
        g = {"masks": sb("masks_sb", [P, NM, P]), "chan": sb("chan_sb", [P, 64]), "mod": sb("mod_cols", [P, 2 * KT, 2])}
        g["mask"] = lambda n: g["masks"][:, MASKS.index(n), :]
        g["ident"] = g["mask"]("ident")
        g["mod_rows"] = dram("mod_rows_dram", [P, 4 * D])
        g["y_chunks"] = dram("y_chunks", [2, LAT_CHUNKS * P * KT * C])
        g["v_dram"] = dram("v_chunks", [KT, CHUNKS * P * C])
        g["kr_dram"] = dram("kr_chunks", [2, KT, CHUNKS * P * 2 * C])
        g["bk_dram"] = dram("bk_chunks", [2, KT, CHUNKS * P * 2 * C])
        g["hT"] = sb("hT", [P, KT, TOK])
        g["xg"] = sb("xg_sb", [P, SEQ])
        g["bonus"] = sb("bonus_sb", [P, KT, SEQ])
        g["decay_end"] = sb("decay_end", [P, 2, CHUNKS, KT])
        g["small"] = sb("small_sb", [P, 4])
        g["gn_eps"] = g["small"][:, 0:1]
        mean_w = sb("mean_w", [P, P])
        g["mean_w"] = mean_w[:, :]
        modulation(nc, g, I)
        norm_and_turn(nc, g, I)
        with ExitStack() as inner:
            g["xw"] = inner.enter_context(nc.sbuf_tensor("xw_sb", [P, 2, TOK], F32))
            g["xa"] = inner.enter_context(nc.sbuf_tensor("xa_sb", [P, 2, TOK], F32))
            low_rank_inputs(nc, g, I)
            prepare(nc, g, I)
        x1 = g["hT"][:, :, :].rearrange("p k t -> p (k t)")[:, 0:SEQ * KT].rearrange("p (t e) -> p t e", e=D)
        logits = sb("logits", [P, SEQ // P, 36])
        g["f_dram"] = dram("f_rows", [SEQ, D])
        g["slot_tok"] = dram("slot_tok", [TILES * SLOTS, 1])
        g["y_dram"] = dram("y_rows", [TILES * SLOTS, D])
        with ExitStack() as mixers:
            msb = lambda n, s: mixers.enter_context(nc.sbuf_tensor(n, s, F32))
            with ExitStack() as inner:
                S = [inner.enter_context(nc.sbuf_tensor(f"state{d}", [P, KT, P], F32)) for d in range(2)]
                with nc.Block() as block:
                    @block.vector
                    def _(dve):
                        for d in range(2):
                            dve.memset(S[d][:, :, :], 0.0)
                        dve.memset(g["small"][:, 0:1], GN_EPS)
                        dve.tensor_scalar(g["mean_w"], g["mask"]("heads"), 1.0 / HD, None, ALU.mult)
                recurrence(nc, g, 0, S)
                recurrence(nc, g, 1, S)
            ry, merged = msb("rwkv_y", [P, KT, SEQ]), msb("merged", [P, KT, SEQ])
            read_out(nc, g, I, ry)
            py = msb("pool_y", [P, 4, SEQ])
            pooling(nc, g, I, py)
            merge(nc, g, I, py, ry, merged)
            project_out(nc, g, I, merged, x1, logits)
        R = {"slot": sb("slot", [P, 2, SEQ // P], U32), "gate": sb("gate", [P, 2, SEQ // P]), "tok": sb("tok", [P, TILES], U32),
             "spill_expert": sb("spill_expert", [P, SPILL], I32), "spill_tiles": sb("spill_tiles", [P, 1], I32)}
        route(nc, g, logits, R)
        experts(nc, g, I, R)
        combine(nc, g, I, R, x1, out)


def kernel(**inputs):
    import concourse.bacc as bacc
    from concourse.bass_utils import run_bass_kernel_spmd

    nc = bacc.Bacc("TRN2", target_bir_lowering=False, num_devices=1)
    arrays = {f"in_{k}": v for k, v in layout(inputs).items()}
    aps = {k[3:]: nc.dram_tensor(k, v.shape, mybir.dt.from_np(v.dtype), kind="ExternalInput").ap() for k, v in arrays.items()}
    out = nc.dram_tensor("out", (1, SEQ, D), F32, kind="ExternalOutput").ap()
    program(nc, aps, out)
    r = run_bass_kernel_spmd(nc, [arrays], core_ids=[0])
    return r.results[0]["out"]
```

```python
from contextlib import ExitStack

import concourse.bass as bass
import numpy as np
from concourse import mybir

F32 = mybir.dt.float32
U32 = mybir.dt.uint32
I32 = mybir.dt.int32
ALU = mybir.AluOpType
ACT = mybir.ActivationFunctionType
AX = mybir.AxisListType
ds = bass.ds

P = 128
D = 1024
KT = D // P
SEQ, CTX = 512, 256
TOK = CTX + SEQ
HD = 64
C = 64
CTX_CHUNKS, LAT_CHUNKS = CTX // C, SEQ // C
CHUNKS = CTX_CHUNKS + LAT_CHUNKS
GRID_W = 64
WINDOWS = (2, 4, 8, 16)
NG, EPG, NE = 4, 8, 32
FE = 256
GN_EPS, RMS_EPS = 64e-5, 1e-6
DECAY = float(np.exp(-0.5))
ADA_N = 6 * D // 512
NPAR = 16
(P_CR, P_CK, P_CV, P_W0, P_A0, P_KK, P_KA, P_RK) = (0, 3, 6, 9, 11, 13, 14, 15)
PREPW = (3 * KT + 2) * P
LEVELS = (2, 4, 8, 16)

MASKS = ["ident", "heads", "up_both", "low_both"]
MASKS += ["before", "ones"]
MASKS += [f"up{b}" for b in (1, 2, 4, 8, 16, 32)] + [f"low{b}" for b in (1, 2, 4, 8, 16, 32)]
NM = len(MASKS)


def mask_table():
    r, c = np.arange(P)[:, None], np.arange(P)[None, :]
    same = (r // HD) == (c // HD)
    t = {"ident": r == c, "heads": same,
         "up_both": np.where(c < HD, r % HD < c % HD, r % HD <= c % HD),
         "low_both": np.where(c < HD, r % HD > c % HD, r % HD >= c % HD),
         "before": r < c, "ones": r + c >= 0}
    for b in (1, 2, 4, 8, 16, 32):
        low = (r // (2 * b) == c // (2 * b)) & (r // b % 2 == 1) & (c // b % 2 == 0)
        t[f"low{b}"], t[f"up{b}"] = low, low.T
    return np.ascontiguousarray(np.stack([t[m] for m in MASKS], 1).astype(np.float32))


def pool_table():
    rows = SEQ // GRID_W

    def mean(n, win):
        lo = win // 2
        hi = win - lo - 1
        m = np.zeros((n, n))
        for t in range(n):
            a, b = max(t - lo, 0), min(t + hi + 1, n)
            m[a:b, t] = 1.0 / (b - a)
        return m

    out = [np.kron(mean(rows, w), mean(GRID_W, w)) - np.eye(SEQ) for w in WINDOWS]
    return np.ascontiguousarray(np.stack(out).reshape(4, SEQ // P, P, SEQ).transpose(0, 2, 1, 3).astype(np.float32))


def flat(ap, at, n):
    names = "abcdefg"[:len(ap.shape)]
    return ap.rearrange(f"{' '.join(names)} -> ({' '.join(names)})")[ds(at, n)]


class Order:

    def __init__(self, sem, names):
        self.sem, self.names = sem, names
        self.at = {n: k + 1 + len(names) for k, n in enumerate(names)}
        self.next = 0

    def start(self, engine):
        engine.sem_inc(self.sem, len(self.names))

    def done(self, name, ins):
        assert self.names[self.next % len(self.names)] == name, (name, self.names[self.next % len(self.names)])
        self.next += 1
        ins.then_inc(self.sem, 1)

    def value(self, name, i=0, back=0):
        return i * len(self.names) + (self.at[name] - back * len(self.names))


def token_buffers(nc, ctx):
    NT = TOK // P
    sb = lambda n, s: ctx.enter_context(nc.sbuf_tensor(n, s, F32))
    return {"xs": sb("x_tiles", [P, NT, D]), "sq": sb("x_sq", [P, D]), "st": sb("x_stat", [P, 4, NT]),
            "loaded": [ctx.enter_context(nc.semaphore(f"x_loaded{t}")) for t in range(NT)]}


def modulation(nc, g, I, tb):
    with ExitStack() as ctx:
        sb = lambda n, s, d=F32: ctx.enter_context(nc.sbuf_tensor(n, s, d))
        sem = lambda n: ctx.enter_context(nc.semaphore(n))
        NF, NR = 2 * D // 512, 4 * D // 512
        cvec = sb("cvec", [P, 2, KT])
        sig = sb("csig", [P, 2, KT])
        silu = sb("csilu", [P, 2, KT])
        lhs = sb("clhs", [P, KT, P])
        ones = sb("ones_row", [1, P])
        bias = sb("ada_bias", [1, 6 * D])
        w_first, w_rest = sb("ada_first", [P, 2, KT, 512]), sb("ada_rest", [P, 2, KT, 512])
        first = sb("mod_first", [P, 2 * D])
        acc = sb("mod_acc", [P, NR, 512])
        rest = g["hT"][:, :, :].rearrange("p k t -> p (k t)")[:, 0:NR * 512].rearrange("p (n c) -> p n c", n=NR)
        ps = [ctx.enter_context(nc.psum_tensor(f"mod_ps{k}", [P, 512], F32)) for k in range(4)]
        pt = [ctx.enter_context(nc.psum_tensor(f"mod_pt{k}", [P, 4, P], F32)) for k in range(4)]
        small, silu_ready, lhs_ready = sem("small"), sem("silu"), sem("lhs")
        first_loaded, rest_loaded = [sem(f"ada_first{u}") for u in range(2)], [sem(f"ada_rest{u}") for u in range(2)]
        first_done, first_read, summed, rest_done, rest_read = sem("mod_first_done"), sem("mod_first_read"), sem("mod_summed"), sem("mod_rest_done"), sem("mod_rest_read")
        turned, stored = sem("turned"), sem("mod_stored")
        with nc.Block() as block:
            @block.sync
            def _(sp):
                sp.dma_start(cvec[:, :, :], I["cvecs"]).then_inc(small, 16)
                sp.dma_start(bias[:, :], I["ada_b"]).then_inc(small, 16)
                sp.dma_start(g["masks"][:, :, :], I["masks"]).then_inc(small, 16)
                sp.dma_start(g["chan"][:, :], I["chan"]).then_inc(small, 16)
                for n in range(NR):
                    if n < NF:
                        if n >= 2:
                            sp.wait_ge(first_done, n - 1)
                        sp.dma_start(w_first[:, n % 2, :, :], I["ada_w"][n]).then_inc(first_loaded[n % 2], 16)
                    if n >= 2:
                        sp.wait_ge(summed, n - 1)
                    sp.dma_start(w_rest[:, n % 2, :, :], I["ada_w"][NF + n]).then_inc(rest_loaded[n % 2], 16)
                for t in range(TOK // P):
                    src = I["ctx"][t * P:t * P + P, :] if t < CTX // P else I["x"][(t - 2) * P:(t - 1) * P, :]
                    sp.dma_start(tb["xs"][:, t, :], src).then_inc(tb["loaded"][t], 16)
                sp.wait_ge(rest_read, NR)
                sp.dma_start(g["mod_rows"], g["hT"][:, :, :].rearrange("p k t -> p (k t)")[:, 0:NR * 512]).then_inc(stored, 16)
                sp.wait_ge(stored, 16)

            @block.scalar
            def _(act):
                act.wait_ge(small, 64)
                act.activation(sig[:, :, :], cvec[:, :, :], ACT.Sigmoid).then_inc(silu_ready, 1)
                for n in range(NF):
                    act.wait_ge(first_done, n + 1)
                    act.activation(first[:, n * 512:n * 512 + 512], ps[n % 2][:, :], ACT.Copy).then_inc(first_read, 1)
                for n in range(NR):
                    act.wait_ge(rest_done, n + 1)
                    act.activation(rest[:, n, :], ps[2 + n % 2][:, :], ACT.Copy).then_inc(rest_read, 1)
                for t in range(TOK // P):
                    act.wait_ge(tb["loaded"][t], 16)
                    act.drain()
                    act.activation(tb["sq"][:, :], tb["xs"][:, t, :], ACT.Square, accum_out=tb["st"][:, 0, t:t + 1])

            @block.vector
            def _(dve):
                dve.memset(ones[:, :], 1.0)
                dve.wait_ge(silu_ready, 1)
                dve.tensor_tensor(silu[:, :, :], sig[:, :, :], cvec[:, :, :], ALU.mult)
                dve.drain()
                for h in range(2):
                    dve.tensor_copy(lhs[:, :, h * 64:h * 64 + 64], silu[:, h, :].unsqueeze(2).to_broadcast([P, KT, 64]))
                dve.drain().then_inc(lhs_ready, 1)
                for n in range(NR):
                    u = n % 2
                    dve.wait_ge(rest_loaded[u], (n // 2 + 1) * 16)
                    dve.tensor_scalar(acc[:, n, :], w_rest[:, u, 0, :], silu[:, 0, 0:1], None, ALU.mult)
                    for k in range(1, KT):
                        dve.drain()
                        last = dve.scalar_tensor_tensor(out=acc[:, n, :], in0=w_rest[:, u, k, :], scalar=silu[:, 0, k:k + 1], in1=acc[:, n, :], op0=ALU.mult, op1=ALU.add)
                    last.then_inc(summed, 1)
                for t in range(4):
                    dve.wait_ge(turned, t + 1)
                    dve.tensor_copy(g["mod"][:, t * 4:t * 4 + 4, :], pt[t][:, :, 0::64])
                dve.drain()
                sc, gain = g["mod"][:, KT:2 * KT, :], g["chan"][:, 0:KT].unsqueeze(2).to_broadcast([P, KT, 2])
                dve.scalar_tensor_tensor(out=sc, in0=sc, scalar=1.0, in1=gain, op0=ALU.add, op1=ALU.mult)

            @block.tensor
            def _(pe):
                pe.wait_ge(small, 64)
                pe.wait_ge(lhs_ready, 1)
                for n in range(NF):
                    pe.wait_ge(first_loaded[n % 2], (n // 2 + 1) * 16)
                    if n >= 2:
                        pe.wait_ge(first_read, n - 1)
                    for k in range(KT):
                        pe.matmul(ps[n % 2][:, :], lhs[:, k, :], w_first[:, n % 2, k, :], start=(k == 0), stop=False)
                    pe.matmul(ps[n % 2][:, :], ones[:, :], bias[:, n * 512:n * 512 + 512], start=False, stop=True).then_inc(first_done, 1)
                pe.wait_ge(first_read, NF)
                for t in range(4):
                    for k in range(4):
                        n = (t * 4 + k) * P
                        last = pe.transpose(pt[t][:, k, :], first[:, n:n + P], g["ident"])
                    last.then_inc(turned, 1)
                for n in range(NR):
                    if n >= 2:
                        pe.wait_ge(rest_read, n - 1)
                    pe.wait_ge(summed, n + 1)
                    pe.matmul(ps[2 + n % 2][:, :], g["mask"]("ones"), acc[:, n, :], start=True, stop=False)
                    pe.matmul(ps[2 + n % 2][:, :], ones[:, :], bias[:, (NF + n) * 512:(NF + n + 1) * 512], start=False, stop=True).then_inc(rest_done, 1)


def norm_and_turn(nc, g, I, tb):
    with ExitStack() as ctx:
        sb = lambda n, s, d=F32: ctx.enter_context(nc.sbuf_tensor(n, s, d))
        sem = lambda n: ctx.enter_context(nc.semaphore(n))
        NT = TOK // P
        xs, st = tb["xs"], tb["st"]
        xn = sb("x_normed", [P, 2, D])
        tmp = sb("x_tmp", [P, KT, P])
        pt = [ctx.enter_context(nc.psum_tensor(f"x_pt{k}", [P, KT, P], F32)) for k in range(2)]
        root, normed, turned, evac = sem("root"), sem("normed"), sem("x_turned"), sem("x_evac")
        meaned = sem("meaned")
        with nc.Block() as block:
            @block.scalar
            def _(act):
                act.wait_ge(meaned, 1)
                act.activation(st[:, 2, :], st[:, 1, :], ACT.Sqrt).then_inc(root, 1)

            @block.vector
            def _(dve):
                dve.tensor_scalar(st[:, 1, :], st[:, 0, :], 1.0 / D, RMS_EPS, ALU.mult, ALU.add).then_inc(meaned, 1)
                dve.wait_ge(root, 1)
                dve.reciprocal(st[:, 3, :], st[:, 2, :])
                dve.drain()
                for t in range(NT + 1):
                    if t < NT:
                        if t >= 2:
                            dve.wait_ge(turned, t - 1)
                        dve.tensor_scalar(xn[:, t % 2, :], xs[:, t, :], st[:, 3, t:t + 1], None, ALU.mult).then_inc(normed, 1)
                    if t >= 1:
                        s = t - 1
                        which = 1 if s < CTX // P else 0
                        scale = g["mod"][:, KT:2 * KT, which:which + 1].to_broadcast([P, KT, P])
                        shift = g["mod"][:, 0:KT, which:which + 1].to_broadcast([P, KT, P])
                        dve.wait_ge(turned, s + 1)
                        dve.tensor_tensor(tmp[:, :, :], pt[s % 2][:, :, :], scale, ALU.mult).then_inc(evac, 1)
                        dve.drain()
                        dve.tensor_tensor(g["hT"][:, :, s * P:s * P + P], tmp[:, :, :], shift, ALU.add)
                        dve.drain()

            @block.tensor
            def _(pe):
                for t in range(NT):
                    pe.wait_ge(normed, t + 1)
                    if t >= 2:
                        pe.wait_ge(evac, t - 1)
                    for k in range(KT):
                        last = pe.transpose(pt[t % 2][:, k, :], xn[:, t % 2, k * P:k * P + P], g["ident"])
                    last.then_inc(turned, 1)


def low_rank_inputs(nc, g, I):
    with ExitStack() as ctx:
        sb = lambda n, s, d=F32: ctx.enter_context(nc.sbuf_tensor(n, s, d))
        sem = lambda n: ctx.enter_context(nc.semaphore(n))
        w = sb("lr_w", [P, 3, KT, P])
        y = sb("lr_y", [P, 3, TOK])
        ps = [[ctx.enter_context(nc.psum_tensor(f"lr_ps{j}{k}", [P, 512], F32)) for k in range(2)] for j in range(3)]
        wl, mm, cv = sem("lr_loaded"), sem("lr_mm"), sem("lr_conv")
        zero, zero_set, cleared = sb("lr_zero", [P, D]), sem("lr_zero_set"), sem("lr_cleared")
        hT, xw, xa, xg, chan = g["hT"], g["xw"], g["xa"], g["xg"], g["chan"]
        with nc.Block() as block:
            @block.sync
            def _(sp):
                sp.dma_start(w[:, :, :, :], I["w_lr"]).then_inc(wl, 16)
                sp.wait_ge(zero_set, 1)
                sp.dma_start(g["slot_tok"].rearrange("(p n) a -> p (n a)", p=P), zero[:, 0:TILES]).then_inc(cleared, 16)
                for q in range(SPILL):
                    sp.dma_start(g["y_dram"][(NE + q) * SLOTS:(NE + q + 1) * SLOTS, :], zero[:, :]).then_inc(cleared, 16)
                sp.wait_ge(cleared, (SPILL + 1) * 16)

            @block.gpsimd
            def _(pool):
                pool.memset(zero[:, :], 0.0)
                pool.drain().then_inc(zero_set, 1)

            @block.tensor
            def _(pe):
                pe.wait_ge(wl, 16)
                for j in range(3):
                    for part, (a, n) in enumerate(((CTX, SEQ), (0, CTX))):
                        if j == 2 and part == 1:
                            continue
                        for k in range(KT):
                            last = pe.matmul(ps[j][part][:, 0:n], w[:, j, k, :], hT[:, k, a:a + n], start=(k == 0), stop=(k == KT - 1))
                    last.then_inc(mm, 1)

            @block.vector
            def _(dve):
                for z in (xw, xa):
                    dve.memset(z[:, :, :], 0.0)
                dve.drain()
                for j in range(3):
                    dve.wait_ge(mm, j + 1)
                    tap = lambda q: chan[:, 16 + 3 * j + q:17 + 3 * j + q]
                    for part, (a, n) in enumerate(((CTX, SEQ), (0, CTX))):
                        if j == 2 and part == 1:
                            continue
                        s = ps[j][part]
                        dve.tensor_scalar(y[:, j, a:a + n], s[:, 0:n], tap(1), None, ALU.mult)
                        dve.drain()
                        dve.scalar_tensor_tensor(out=y[:, j, a + 1:a + n], in0=s[:, 0:n - 1], scalar=tap(0), in1=y[:, j, a + 1:a + n], op0=ALU.mult, op1=ALU.add)
                        dve.drain()
                        dve.scalar_tensor_tensor(out=y[:, j, a:a + n - 1], in0=s[:, 1:n], scalar=tap(2), in1=y[:, j, a:a + n - 1], op0=ALU.mult, op1=ALU.add)
                        dve.drain()
                    dve.drain().then_inc(cv, 1)
                for d in range(2):
                    h = slice(64 * d, 64 * d + 64)
                    dve.tensor_copy(xa[h, d, :], y[h, 1, :])

            @block.scalar
            def _(act):
                act.wait_ge(cv, 1)
                for d in range(2):
                    h = slice(64 * d, 64 * d + 64)
                    act.activation(xw[h, d, :], y[h, 0, :], ACT.Tanh)
                act.wait_ge(cv, 3)
                act.activation(xg[:, :], y[:, 2, CTX:TOK], ACT.Sigmoid)


def prepare(nc, g, I):
    with ExitStack() as ctx:
        sb = lambda n, s, d=F32: ctx.enter_context(nc.sbuf_tensor(n, s, d))
        sem = lambda n: ctx.enter_context(nc.semaphore(n))
        w = sb("pr_w", [P, 2, PREPW])
        par = sb("pr_par", [P, 2, NPAR])
        rk = sb("pr_rk", [P, P])
        r, k, v = sb("pr_r", [P, TOK]), sb("pr_k", [P, TOK]), sb("pr_v", [P, TOK])
        kraw, ksq, kk = sb("pr_kraw", [P, TOK]), sb("pr_ksq", [P, TOK]), sb("pr_kk", [P, TOK])
        norm = sb("pr_norm", [P, TOK])
        s_dec, rates = sb("pr_s", [P, 2, TOK]), sb("pr_rate", [P, 2, 2, TOK])
        reset = sb("pr_reset", [P, 2, CHUNKS, C])
        cum, cumx = sb("pr_cum", [P, 2, TOK]), sb("pr_cumx", [P, 2, TOK])
        e_ins, e_outs, e_prevs = (sb(f"pr_e{j}", [P, 2, TOK]) for j in range(3))
        kd, bb = sb("pr_kd", [P, 2, TOK]), sb("pr_bb", [P, TOK])
        k_ka, k_rest = sb("pr_kka", [P, TOK]), sb("pr_krest", [P, TOK])
        rkd = sb("pr_rkd", [P, SEQ])
        KR = sb("pr_KR", [P, 2, CHUNKS, 2, C])
        BK = sb("pr_BK", [P, 2, CHUNKS, 2, C])
        one_less = sb("pr_1ka", [P, 1])
        bank = [ctx.enter_context(nc.psum_tensor(f"pr_ps{j}", [P, 512], F32)) for j in range(8)]
        B_R, B_K, B_V, B_KC, B_VC = bank[0:5]
        PAIR = [(bank[5], bank[6]), (B_R, bank[7])]
        B_BONUS = bank[7]
        wload = [sem("pr_wl0"), sem("pr_wl1")]
        pe_s, act_s, dve_s, pool_s = sem("pr_pe"), sem("pr_act"), sem("pr_dve"), sem("pr_pool")
        stored = [sem("pr_st0"), sem("pr_st1")]
        vstored = sem("pr_vst")
        hT, heads = g["hT"], g["mask"]("heads")
        pe_o = Order(pe_s, ["k", "a0", "a1", "r", "v", "w0", "w1", "norm", "bonus"])
        act_o = Order(act_s, ["tap_k", "sig_a0", "sig_a1", "tap_r", "ksq", "tap_v", "sig_w0", "sig_w1", "exp0", "rnorm", "exp1"])
        dve_o = Order(dve_s, ["conv_k", "kraw", "conv_r", "kds", "conv_v", "cum0", "cum1", "guard", "bonus", "kk", "dec0", "dec1"])
        pool_o = Order(pool_s, ["kd0", "kd1"])
        lat = slice(CTX, TOK)
        parts = ((CTX, SEQ), (0, CTX))
        low_rank = {"a0": (1, g["xa"], 0, PAIR[1]), "a1": (1, g["xa"], 1, PAIR[0]), "w0": (0, g["xw"], 0, PAIR[0]), "w1": (0, g["xw"], 1, PAIR[1])}
        mixed = {"k": (1, k, B_K, B_KC, P_CK), "r": (0, r, B_R, None, P_CR), "v": (2, v, B_V, B_VC, P_CV)}

        def body(u):
            return w[:, u, :].rearrange("p (j n) -> p j n", n=P), lambda q: par[:, u, q:q + 1]

        with nc.Block() as block:
            @block.sync
            def _(sp):
                for u in range(2):
                    sp.dma_start(w[:, u, :], I["w_prep"][u]).then_inc(wload[u], 16)
                    sp.dma_start(par[:, u, :], I["p_prep"][u]).then_inc(wload[u], 16)
                sp.sem_inc(vstored, 16)
                for d in range(2):
                    sp.sem_inc(stored[d], 32)

                NV, NO = CHUNKS * P * C, CHUNKS * P * 2 * C

                def store(m, at, at_v):
                    sp.wait_ge(dve_s, dve_o.value("conv_v", m))
                    sp.dma_start(flat(g["v_dram"], at_v, NV).rearrange("(c p t) -> p c t", c=CHUNKS, p=P),
                                 v[:, :].rearrange("p (c t) -> p c t", t=C)).then_inc(vstored, 16)

                def store_operands(m, at):
                    for d in range(2):
                        sp.wait_ge(dve_s, dve_o.value(f"dec{d}", m))
                        for dst, src in ((g["kr_dram"], KR), (g["bk_dram"], BK)):
                            sp.dma_start(flat(dst[d], at, NO).rearrange("(c p t) -> p c t", c=CHUNKS, p=P),
                                         src[:, d, :, :, :].rearrange("p c b t -> p c (b t)")).then_inc(stored[d], 16)

                with sp.Fori(0, KT // 2 - 1) as i:
                    for u in range(2):
                        m = i * 2 + u
                        at, at_v = sp.snap(i * 2 * NO + u * NO), sp.snap(i * 2 * NV + u * NV)
                        nxt_w = sp.snap(i * 2 * P * PREPW + (u + 2) * P * PREPW)
                        nxt_p = sp.snap(i * 2 * P * NPAR + (u + 2) * P * NPAR)
                        store(m, at, at_v)
                        sp.wait_ge(pe_s, pe_o.value("bonus", m))
                        sp.dma_start(w[:, u, :], flat(I["w_prep"], nxt_w, P * PREPW).rearrange("(p n) -> p n", p=P)).then_inc(wload[u], 16)
                        sp.dma_start(par[:, u, :], flat(I["p_prep"], nxt_p, P * NPAR).rearrange("(p n) -> p n", p=P)).then_inc(wload[u], 16)
                        store_operands(m, at)
                for m in (KT - 2, KT - 1):
                    store(m, m * NO, m * NV)
                    store_operands(m, m * NO)
                for d in range(2):
                    sp.wait_ge(stored[d], (KT + 1) * 32)
                sp.wait_ge(vstored, (KT + 1) * 16)

            @block.tensor
            def _(pe):
                pe_o.start(pe)
                with pe.Fori(0, KT // 2) as i:
                    for u in range(2):
                        wv, pr = body(u)
                        m = i * 2 + u
                        pe.wait_ge(wload[u], (i + 1) * 32)

                        def project(name):
                            j, _y, lat_bank, ctx_bank, _q = mixed[name]
                            for kt in range(KT):
                                last = pe.matmul(lat_bank[:, :], wv[:, j * KT + kt, :], hT[:, kt, lat], start=(kt == 0), stop=(kt == KT - 1))
                            if ctx_bank is not None:
                                for kt in range(KT):
                                    last = pe.matmul(ctx_bank[:, 0:CTX], wv[:, j * KT + kt, :], hT[:, kt, 0:CTX], start=(kt == 0), stop=(kt == KT - 1))
                            pe_o.done(name, last)

                        def low(name):
                            maps, src, d, pair = low_rank[name]
                            for part, (a, n) in enumerate(parts):
                                last = pe.matmul(pair[part][:, 0:n], wv[:, 3 * KT + maps, :], src[:, d, a:a + n], start=True, stop=True)
                            pe_o.done(name, last)

                        pe.wait_ge(dve_s, dve_o.value("conv_k", m, 1))
                        project("k")
                        pe.wait_ge(dve_s, dve_o.value("bonus", m, 1))
                        pe.wait_ge(act_s, act_o.value("sig_w1", m, 1))
                        low("a0")
                        low("a1")
                        pe.wait_ge(act_s, act_o.value("sig_a0", m))
                        project("r")
                        pe.wait_ge(dve_s, dve_o.value("conv_v", m, 1))
                        project("v")
                        pe.wait_ge(act_s, act_o.value("sig_a1", m))
                        low("w0")
                        pe.wait_ge(dve_s, dve_o.value("conv_r", m))
                        low("w1")
                        pe.wait_ge(act_s, act_o.value("sig_w0", m))
                        for part, (a, n) in enumerate(parts):
                            last = pe.matmul(PAIR[0][part][:, 0:n], heads, ksq[:, a:a + n], start=True, stop=True)
                        pe_o.done("norm", last)
                        pe.wait_ge(act_s, act_o.value("sig_w1", m))
                        pe.wait_ge(dve_s, dve_o.value("kds", m))
                        pe_o.done("bonus", pe.matmul(B_BONUS[:, :], rk[:, :], rkd[:, :], start=True, stop=True))

            @block.scalar
            def _(act):
                act_o.start(act)
                with act.Fori(0, KT // 2) as i:
                    for u in range(2):
                        wv, pr = body(u)
                        m = i * 2 + u
                        act.wait_ge(wload[u], (i + 1) * 32)

                        def tap(name, used):
                            _j, y, b, bc, q = mixed[name]
                            act.wait_ge(dve_s, dve_o.value(used, m, 1))
                            if name == "v":
                                act.wait_ge(vstored, (m + 1) * 16)
                            act.wait_ge(pe_s, pe_o.value(name, m))
                            last = act.activation(y[:, lat], b[:, :], ACT.Copy, scale=pr(q + 1))
                            if bc is not None:
                                last = act.activation(y[:, 0:CTX], bc[:, 0:CTX], ACT.Copy, scale=pr(q + 1))
                            act_o.done(f"tap_{name}", last)

                        def sig(name):
                            _maps, _src, d, pair = low_rank[name]
                            y, p0 = (rate, P_A0 + d) if name[0] == "a" else (s_dec, P_W0 + d)
                            act.wait_ge(pe_s, pe_o.value(name, m))
                            for part, (a, n) in enumerate(parts):
                                last = act.activation(y[:, d, a:a + n], pair[part][:, 0:n], ACT.Sigmoid, bias=pr(p0))
                            act_o.done(f"sig_{name}", last)

                        rate = rates[:, u, :, :]
                        tap("k", "kraw")
                        sig("a0")
                        sig("a1")
                        tap("r", "dec1")
                        act.wait_ge(dve_s, dve_o.value("kraw", m))
                        act_o.done("ksq", act.activation(ksq[:, :], kraw[:, :], ACT.Square))
                        tap("v", "bonus")
                        sig("w0")
                        sig("w1")
                        for d in range(2):
                            act.wait_ge(dve_s, dve_o.value(f"cum{d}", m))
                            e_in, e_out, e_prev = e_ins[:, d, :], e_outs[:, d, :], e_prevs[:, d, :]
                            act.activation(e_in[:, :], cum[:, d, :], ACT.Exp, scale=-DECAY)
                            act.activation(e_out[:, :], cum[:, d, :], ACT.Exp, scale=DECAY)
                            act_o.done(f"exp{d}", act.activation(e_prev[:, :], cumx[:, d, :], ACT.Exp, scale=-DECAY))
                            if d == 0:
                                act.wait_ge(dve_s, dve_o.value("guard", m))
                                act.activation(norm[:, :], norm[:, :], ACT.Ln)
                                act.drain()
                                act_o.done("rnorm", act.activation(norm[:, :], norm[:, :], ACT.Exp, scale=-0.5))

            @block.gpsimd
            def _(pool):
                pool_o.start(pool)
                with pool.Fori(0, KT // 2) as i:
                    for u in range(2):
                        m = i * 2 + u
                        rate = rates[:, u, :, :]
                        pool.wait_ge(dve_s, dve_o.value("kraw", m))
                        for d in range(2):
                            pool.wait_ge(act_s, act_o.value(f"sig_a{d}", m))
                            pool.tensor_tensor(kd[:, d, :], rate[:, d, :], k_ka[:, :], ALU.mult)
                            pool.drain()
                            pool_o.done(f"kd{d}", pool.tensor_tensor(kd[:, d, :], kd[:, d, :], k_rest[:, :], ALU.add))

            @block.vector
            def _(dve):
                dve_o.start(dve)
                dve.memset(reset[:, :, :, :], 1.0)
                dve.memset(KR[:, :, 0:CTX_CHUNKS, 1, :], 0.0)
                dve.drain()
                dve.memset(reset[:, 0, :, 0:1], 0.0)
                dve.memset(reset[:, 1, :, C - 1:C], 0.0)
                dve.drain()
                dve.memset(g["small"][:, 0:1], GN_EPS)
                dve.tensor_scalar(g["mean_w"], g["mask"]("heads"), 1.0 / HD, None, ALU.mult)
                with dve.Fori(0, KT // 2) as i:
                    for u in range(2):
                        wv, pr = body(u)
                        m = i * 2 + u
                        mreg = dve.snap(i * 2 + u)
                        rate = rates[:, u, :, :]
                        dve.wait_ge(wload[u], (i + 1) * 32)
                        dve.tensor_scalar(one_less[:, :], pr(P_KA), -1.0, 1.0, ALU.mult, ALU.add)
                        for name in ("k", "r", "v"):
                            _j, y, b, bc, q = mixed[name]
                            if name == "v":
                                dve.wait_ge(pool_s, pool_o.value("kd1", m))
                                dve.tensor_tensor(rkd[:, :], kd[:, 0, lat], kd[:, 1, lat], ALU.add)
                                dve.drain()
                                dve_o.done("kds", dve.tensor_tensor(rkd[:, :], rkd[:, :], r[:, lat], ALU.mult))
                            dve.wait_ge(act_s, act_o.value(f"tap_{name}", m))
                            todo = [(b, CTX, SEQ)] + ([(bc, 0, CTX)] if bc is not None else [])
                            for tap in (0, 2):
                                for s, a, n in todo:
                                    dst = y[:, a + 1:a + n] if tap == 0 else y[:, a:a + n - 1]
                                    src = s[:, 0:n - 1] if tap == 0 else s[:, 1:n]
                                    last = dve.scalar_tensor_tensor(out=dst, in0=src, scalar=pr(q + tap), in1=dst, op0=ALU.mult, op1=ALU.add)
                                if tap == 0:
                                    dve.drain()
                            dve_o.done(f"conv_{name}", last)
                            if name == "k":
                                dve.drain()
                                dve.tensor_scalar(k_ka[:, :], k[:, :], pr(P_KA), None, ALU.mult)
                                dve.tensor_scalar(k_rest[:, :], k[:, :], one_less[:, 0:1], None, ALU.mult)
                                dve.tensor_scalar(rk[:, :], heads, pr(P_RK), None, ALU.mult)
                                dve_o.done("kraw", dve.tensor_scalar(kraw[:, :], k[:, :], pr(P_KK), None, ALU.mult))
                        for d in range(2):
                            f = slice(None, None, 1 if d == 0 else -1)
                            rs = reset[:, d, :, :].rearrange("p c t -> p (c t)")
                            dve.wait_ge(act_s, act_o.value(f"sig_w{d}", m))
                            dve.tensor_tensor_scan(cum[:, d, f], rs[:, f], s_dec[:, d, f], 0.0, ALU.mult, ALU.add)
                            dve.drain()
                            dve_o.done(f"cum{d}", dve.tensor_tensor(cumx[:, d, :], cum[:, d, :], s_dec[:, d, :], ALU.subtract))
                        dve.wait_ge(pe_s, pe_o.value("norm", m))
                        for part, (a, n) in enumerate(parts):
                            last = dve.tensor_scalar(norm[:, a:a + n], PAIR[0][part][:, 0:n], 1e-24, None, ALU.max)
                        dve_o.done("guard", last)
                        dve.wait_ge(pe_s, pe_o.value("bonus", m))
                        dve_o.done("bonus", dve.tensor_tensor(g["bonus"][:, ds(mreg, 1), :], B_BONUS[:, :].unsqueeze(1), v[:, lat].unsqueeze(1), ALU.mult))
                        dve.wait_ge(act_s, act_o.value("rnorm", m))
                        dve_o.done("kk", dve.tensor_tensor(kk[:, :], kraw[:, :], norm[:, :], ALU.mult))
                        for d in range(2):
                            chunks = lambda x: x.rearrange("p (c t) -> p c t", t=C)
                            e_in, e_out, e_prev = e_ins[:, d, :], e_outs[:, d, :], e_prevs[:, d, :]
                            dve.drain()
                            dve.tensor_tensor(bb[:, :], kk[:, :], rate[:, d, :], ALU.mult)
                            dve.wait_ge(act_s, act_o.value(f"exp{d}", m))
                            dve.wait_ge(stored[d], (m + 1) * 32)
                            dve.tensor_tensor(KR[:, d, :, 0, :], chunks(kk[:, :]), chunks(e_prev[:, :]), ALU.mult)
                            dve.tensor_tensor(KR[:, d, CTX_CHUNKS:, 1, :], chunks(r[:, lat]), chunks(e_in[:, lat]), ALU.mult)
                            dve.tensor_copy(g["decay_end"][:, d, :, ds(mreg, 1)], chunks(e_in[:, :])[:, :, (C - 1) * (1 - d):(C - 1) * (1 - d) + 1])
                            dve.drain()
                            dve.tensor_tensor(BK[:, d, :, 0, :], chunks(bb[:, :]), chunks(e_out[:, :]), ALU.mult)
                            dve_o.done(f"dec{d}", dve.tensor_tensor(BK[:, d, :, 1, :], chunks(kd[:, d, :]), chunks(e_out[:, :]), ALU.mult))


def recurrence_buffers(nc, ctx):
    sb = lambda nm, s: ctx.enter_context(nc.sbuf_tensor(nm, s, F32))
    q = {nm: [sb(f"rc_{nm}{d}", s) for d in range(2)]
         for nm, s in (("KR", [P, KT, 2, C]), ("KRs", [P, KT, 2, C]), ("Arb", [P, KT, C]), ("yc", [P, KT, C]))}
    q["bd"] = [{x: sb(f"rc_{x}bd{d}", [P, KT, P]) for x in ("B", "Kh", "V")} for d in range(2)]
    q["W"] = [{x: sb(f"rc_{x}{d}", [P, KT, P]) for x in ("U", "Ak", "XT", "Bt", "Kt", "Vt", "T", "Tt", "G")} for d in range(2)]
    for w in q["W"]:
        w["M"] = w["U"]
    q["PC"] = sb("rc_PC", [P, 2, KT])
    return q


def recurrence(nc, g, part, S, q):
    n = (CTX_CHUNKS, LAT_CHUNKS)[part]
    first = (0, CTX_CHUNKS)[part]
    with_y = part == 1
    H = KT // 2
    with ExitStack() as ctx:
        sb = lambda nm, s, d=F32: ctx.enter_context(nc.sbuf_tensor(f"{nm}_{part}", s, d))
        sem = lambda nm: ctx.enter_context(nc.semaphore(f"{nm}_{part}"))
        KR, KRs, bd, W, Arb, PC, yc = (q[x] for x in ("KR", "KRs", "bd", "W", "Arb", "PC", "yc"))
        inputs = ["B", "Kh", "V"]
        bank = [ctx.enter_context(nc.psum_tensor(f"rc_ps{j}_{part}", [P, H, P], F32)) for j in range(8)]
        loaded = [sem("rc_loaded0"), sem("rc_loaded1")]
        pe_s, act_s, dve_s = sem("rc_pe"), sem("rc_act"), sem("rc_dve")
        cleared = sem("rc_cleared")
        y_stored = [sem("rc_y_stored0"), sem("rc_y_stored1")]

        stages = ["B", "Kh", "Bt", "Kt", "Vt", "T1"]
        for b in LEVELS:
            stages += [f"G{b}", f"X{b}", f"Tt{b}"]
        stages += ["G32", "X32", "SX", "Xt", "U"] + ["Y"] * with_y + ["S"]
        place = {x: j % 2 for j, x in enumerate(stages)}
        place.update(SX=0, Xt=1, U=1, Y=0, S=1)
        before = {x: stages[j - 2] for j, x in enumerate(stages)}
        before.update(SX="G32", Xt="X32", U="Xt", S="U", Y="SX", B="Y" if with_y else "SX", Kh="S")
        by_act = {"Bt", "Kt", "Vt", "T1", "SX", "Xt", "U"} | {f"G{b}" for b in (*LEVELS, 32)} | {f"Tt{b}" for b in LEVELS}
        halves = lambda names: [f"{s}.{h}@{d}" for s in names for d in range(2) for h in range(2)]
        pe_o = Order(pe_s, halves(stages))
        act_o = Order(act_s, halves(["M"] + [s for s in stages if s in by_act]))
        pool_s = sem("rc_pool")
        pool_o = Order(pool_s, ["KR.0", "KR.1", "I.0", "I.1"])
        dve_o = Order(dve_s, halves(["B", "Tt1", "Kh"] + [s for s in stages[6:] if s not in by_act]))
        sets = [("up1", "low", "up32"), ("low1", "up", "low32")]
        half = lambda x, h: x[:, H * h:H * h + H, :]

        def ps(stage, d, h):
            return bank[4 * d + 2 * place[stage] + h]

        with nc.Block() as block:
            @block.sync
            def _(sp):
                NO, NV, NY = P * 2 * C, P * C, P * KT * C
                for d in range(2):
                    if with_y:
                        sp.sem_inc(y_stored[d], 16)
                if part == 0:
                    sp.wait_ge(cleared, 2)

                def load(d, at_o, at_v):
                    kr = g["kr_dram"][d][:, ds(at_o, NO)].rearrange("i (p n) -> p i n", p=P)
                    bk = g["bk_dram"][d][:, ds(at_o, NO)].rearrange("i (p b t) -> p i b t", p=P, b=2)
                    vv = g["v_dram"][:, ds(at_v, NV)].rearrange("i (p t) -> p i t", p=P)
                    sp.dma_start(KR[d][:, :, :, :].rearrange("p i b t -> p i (b t)"), kr).then_inc(loaded[d], 16)
                    for hh in range(2):
                        q = slice(64 * hh, 64 * hh + 64)
                        for x, src in (("B", bk[q, :, 0, :]), ("Kh", bk[q, :, 1, :]), ("V", vv[q, :, :])):
                            sp.dma_start(bd[d][x][q, :, q], src).then_inc(loaded[d], 16)

                def store(d, at_y):
                    sp.dma_start(g["y_chunks"][d:d + 1, ds(at_y, NY)].rearrange("a (p n) -> (a p) n", p=P),
                                 yc[d][:, :, :].rearrange("p i t -> p (i t)")).then_inc(y_stored[d], 16)

                for d in range(2):
                    c = first if d == 0 else first + n - 1
                    load(d, c * NO, c * NV)
                with sp.Fori(0, n - 1) as i:
                    sign = (1, -1)
                    nxt = (first + 1, first + n - 2)
                    at_o = [sp.snap(i * (sign[d] * NO) + nxt[d] * NO) for d in range(2)]
                    at_v = [sp.snap(i * (sign[d] * NV) + nxt[d] * NV) for d in range(2)]
                    turned = [sp.snap(pe_o.value(f"Vt.1@{d}", i)) for d in range(2)]
                    if with_y:
                        at_y = [sp.snap(i * NY), sp.snap(i * -NY + (n - 1) * NY)]
                        y_ready = [sp.snap(dve_o.value(f"Y.1@{d}", i)) for d in range(2)]
                    for d in range(2):
                        sp.wait_ge(pe_s, turned[d])
                        load(d, at_o[d], at_v[d])
                    if with_y:
                        for d in range(2):
                            sp.wait_ge(dve_s, y_ready[d])
                            store(d, at_y[d])
                if with_y:
                    for d in range(2):
                        sp.wait_ge(dve_s, dve_o.value(f"Y.1@{d}", n - 1))
                        store(d, (n - 1) * NY if d == 0 else 0)
                    for d in range(2):
                        sp.wait_ge(y_stored[d], (n + 1) * 16)

            @block.tensor
            def _(pe):
                pe_o.start(pe)
                with pe.Fori(0, n) as i:
                    I_ = g["ident"]

                    def free(stage, d, h):
                        old, back = before[stage], 1 if stage in ("B", "Kh") else 0
                        o = act_o if old in by_act else dve_o
                        pe.wait_ge(o.sem, o.value(f"{old}.{h}@{d}", i, back))

                    def products(stage, d, h, terms):
                        out = ps(stage, d, h)
                        for q in range(H):
                            p = H * h + q
                            for j, (lhs, rhs) in enumerate(terms):
                                last = pe.matmul(out[:, q, :], lhs(p), rhs(p), start=(j == 0), stop=(j == len(terms) - 1))
                        pe_o.done(f"{stage}.{h}@{d}", last)

                    def turns(stage, d, h, src):
                        out = ps(stage, d, h)
                        for q in range(H):
                            last = pe.transpose(out[:, q, :], src[:, H * h + q, :], I_)
                        pe_o.done(f"{stage}.{h}@{d}", last)

                    def on_act(name, d, h):
                        pe.wait_ge(act_s, act_o.value(f"{name}.{h}@{d}", i))

                    def on_dve(name, d, h):
                        pe.wait_ge(dve_s, dve_o.value(f"{name}.{h}@{d}", i))

                    m = lambda x: (lambda p: x[:, p, :])
                    dh = [(d, h) for d in range(2) for h in range(2)]
                    for stage in ("B", "Kh"):
                        for d, h in dh:
                            if stage == "B" and h == 0:
                                pe.wait_ge(loaded[d], (i + 1) * 16 * (1 + 2 * len(inputs)))
                            free(stage, d, h)
                            products(stage, d, h, [(m(bd[d][stage]), lambda p: KR[d][:, p, :, :].rearrange("p b t -> p (b t)"))])
                    for stage, x in (("Bt", "B"), ("Kt", "Kh"), ("Vt", "V")):
                        for d, h in dh:
                            if stage == "Vt" and h == 0:
                                pe.wait_ge(pool_s, pool_o.value(f"KR.{d}", i))
                            free(stage, d, h)
                            turns(stage, d, h, bd[d][x])
                    for d, h in dh:
                        free("T1", d, h)
                        on_dve("Tt1", d, h)
                        turns("T1", d, h, W[d]["Tt"])
                    for b in (*LEVELS, 32):
                        for d, h in dh:
                            free(f"G{b}", d, h)
                            if b == 2:
                                on_act("T1", d, h)
                            else:
                                on_dve(f"X{b // 2}", d, h)
                            products(f"G{b}", d, h, [(m(W[d]["M"]), m(W[d]["T"]))])
                        for d, h in dh:
                            free(f"X{b}", d, h)
                            on_act(f"G{b}", d, h)
                            if b > 2:
                                on_act(f"Tt{b // 2}", d, h)
                            lhs, rhs = ("Tt", "G") if b < 32 else ("G", "Tt")
                            products(f"X{b}", d, h, [(m(W[d][lhs]), m(W[d][rhs]))])
                        if b < 32:
                            for d, h in dh:
                                free(f"Tt{b}", d, h)
                                on_dve(f"X{b}", d, h)
                                turns(f"Tt{b}", d, h, W[d]["T"])
                    for d, h in dh:
                        pe.wait_ge(dve_s, dve_o.value(f"S.{h}@{d}", i, 1))
                        free("SX", d, h)
                        products("SX", d, h, [(m(S[d]), lambda p: KRs[d][:, p, :, :].rearrange("p b t -> p (b t)")), (m(W[d]["Vt"]), m(W[d]["Ak"]))])
                    for d, h in dh:
                        free("Xt", d, h)
                        on_act("SX", d, h)
                        turns("Xt", d, h, W[d]["XT"])
                    for d, h in dh:
                        free("U", d, h)
                        products("U", d, h, [(m(W[d]["Tt"]), m(W[d]["G"]))])
                    if with_y:
                        for d, h in dh:
                            on_act("U", d, h)
                            for p in range(H * h, H * h + H):
                                last = pe.matmul(ps("Y", d, h)[:, p - H * h, 0:C], W[d]["U"][:, p, :], Arb[d][:, p, :], start=True, stop=True)
                            pe_o.done(f"Y.{h}@{d}", last)
                    for d, h in dh:
                        free("S", d, h)
                        products("S", d, h, [(m(W[d]["Bt"]), m(W[d]["U"])), (m(W[d]["Kt"]), m(W[d]["Vt"]))])

            @block.scalar
            def _(act):
                act_o.start(act)
                with act.Fori(0, n) as i:
                    for d in range(2):
                        for h in range(2):
                            act.wait_ge(pe_s, pe_o.value(f"B.{h}@{d}", i))
                            act_o.done(f"M.{h}@{d}", act.activation(
                                half(W[d]["M"], h).rearrange("p h (a t) -> p h a t", a=2),
                                ps("B", d, h)[:, :, 0:C].unsqueeze(2).to_broadcast([P, H, 2, C]), ACT.Copy, scale=-1.0))

                    def copy(stage, dst, scale=1.0):
                        for d in range(2):
                            for h in range(2):
                                act.wait_ge(pe_s, pe_o.value(f"{stage}.{h}@{d}", i))
                                act_o.done(f"{stage}.{h}@{d}", act.activation(half(W[d][dst], h), ps(stage, d, h)[:, :, :], ACT.Copy, scale=scale))

                    for stage, dst in (("Bt", "Bt"), ("Kt", "Kt"), ("Vt", "Vt"), ("T1", "T")):
                        copy(stage, dst)
                    for b in (*LEVELS, 32):
                        copy(f"G{b}", "G")
                        if b < 32:
                            copy(f"Tt{b}", "Tt")
                    for d in range(2):
                        for h in range(2):
                            if with_y and h == 0:
                                act.wait_ge(y_stored[d], (i + 1) * 16)
                            act.wait_ge(pe_s, pe_o.value(f"SX.{h}@{d}", i))
                            if with_y:
                                act.activation(half(yc[d], h), ps("SX", d, h)[:, :, C:P], ACT.Copy)
                            for hh in range(2):
                                q = slice(64 * hh, 64 * hh + 64)
                                last = act.activation(W[d]["XT"][q, H * h:H * h + H, q], ps("SX", d, h)[q, :, 0:C], ACT.Copy)
                            act_o.done(f"SX.{h}@{d}", last)
                    copy("Xt", "G")
                    copy("U", "U", -1.0)

            @block.gpsimd
            def _(pool):
                if part == 0:
                    for x in inputs:
                        pool.memset(bd[1][x][:, :, :], 0.0)
                    pool.drain().then_inc(cleared, 1)
                pool_o.start(pool)
                with pool.Fori(0, n) as i:
                    for d in range(2):
                        pool.wait_ge(pe_s, pe_o.value(f"SX.1@{d}", i, 1))
                        pool.wait_ge(loaded[d], (i + 1) * 16 * (1 + 2 * len(inputs)))
                        pool.sem_inc(g["noted"]["pool"], 1)
                        pool_o.done(f"KR.{d}", pool.tensor_copy(KRs[d][:, :, :, :], KR[d][:, :, :, :]))
                    for d in range(2):
                        pool.wait_ge(pe_s, pe_o.value(f"U.1@{d}", i, 1))
                        pool.sem_inc(g["noted"]["pool"], 1)
                        pool_o.done(f"I.{d}", pool.tensor_copy(W[d]["Tt"][:, :, :], g["ident"].unsqueeze(1).to_broadcast([P, KT, P])))

            @block.vector
            def _(dve):
                if part == 0:
                    for x in inputs:
                        dve.memset(bd[0][x][:, :, :], 0.0)
                    dve.drain().then_inc(cleared, 1)
                    for d in range(2):
                        dve.memset(W[d]["XT"][:, :, :], 0.0)
                        dve.memset(S[d][:, :, :], 0.0)
                    dve.drain()
                dve_o.start(dve)
                mask = lambda nm: g["mask"](nm).unsqueeze(1).to_broadcast([P, H, P])
                dh = [(d, h) for d in range(2) for h in range(2)]
                with dve.Fori(0, n) as i:
                    dve.drain()
                    for d in range(2):
                        chunk = dve.snap(i + first) if d == 0 else dve.snap(i * -1 + (first + n - 1))
                        dve.tensor_copy(PC[:, d, :], g["decay_end"][:, d, ds(chunk, 1), :].rearrange("p a i -> p (a i)"))

                    def product(stage, d, h):
                        dve.wait_ge(pe_s, pe_o.value(f"{stage}.{h}@{d}", i))
                        return ps(stage, d, h)

                    both = lambda d: g["mask"](("up_both", "low_both")[d])
                    for d, h in dh:
                        src = product("B", d, h)
                        dve.wait_ge(act_s, act_o.value(f"M.{h}@{d}", i))
                        if with_y:
                            dve_o.done(f"B.{h}@{d}", dve.tensor_tensor(half(Arb[d], h), src[:, :, C:P], both(d)[:, C:P].unsqueeze(1).to_broadcast([P, H, C]), ALU.mult))
                        else:
                            dve.sem_inc(dve_s, 1)
                            dve_o.next += 1
                    for d, h in dh:
                        dve.wait_ge(pool_s, pool_o.value(f"I.{d}", i))
                        dve.sem_inc(g["noted"]["dve"], 1)
                        dve_o.done(f"Tt1.{h}@{d}", dve.copy_predicated(half(W[d]["Tt"], h), mask(sets[d][0]).bitcast(U32), half(W[d]["M"], h)))
                    for d, h in dh:
                        src = product("Kh", d, h)
                        dve_o.done(f"Kh.{h}@{d}", dve.tensor_tensor(half(W[d]["Ak"], h), src[:, :, :], both(d).unsqueeze(1).to_broadcast([P, H, P]), ALU.mult))
                    for b in (*LEVELS, 32):
                        for d, h in dh:
                            src = product(f"X{b}", d, h)
                            dve.sem_inc(g["noted"]["dve"], 1)
                            mk = mask(f"{sets[d][1]}{b}" if b < 32 else sets[d][2]).bitcast(U32)
                            dve_o.done(f"X{b}.{h}@{d}", dve.copy_predicated(half(W[d]["T" if b < 32 else "Tt"], h), mk, src[:, :, :]))
                    if with_y:
                        for d, h in dh:
                            src = product("Y", d, h)
                            dve_o.done(f"Y.{h}@{d}", dve.tensor_tensor(half(yc[d], h), half(yc[d], h), src[:, :, 0:C], ALU.add))
                    for d, h in dh:
                        src = product("S", d, h)
                        dve.tensor_tensor(half(S[d], h), half(S[d], h), src[:, :, :], ALU.add)
                        dve.drain()
                        dve_o.done(f"S.{h}@{d}", dve.tensor_tensor(half(S[d], h), half(S[d], h), PC[:, d, H * h:H * h + H].unsqueeze(2).to_broadcast([P, H, P]), ALU.mult))


def pool_buffers(nc, ctx):
    sb = lambda n, s: ctx.enter_context(nc.sbuf_tensor(n, s, F32))
    space = sb("pl_w_box", [P, KT * D])
    return {"w": space[:, 0:KT * 512].rearrange("p (k n) -> p k n", k=KT), "pw": sb("pl_pw", [P, 4, P]), "u": sb("pl_u", [P, SEQ // P, 512]),
            "box": space[:, KT * 512:].rearrange("p (j t n) -> p j t n", j=2, n=SEQ), "w_out": space[:, :].rearrange("p (k n) -> p k n", k=KT),
            "pw_loaded": ctx.enter_context(nc.semaphore("pl_pw_loaded")),
            "loaded": ctx.enter_context(nc.semaphore("pl_loaded")), "boxed": [ctx.enter_context(nc.semaphore(f"pl_box{j}")) for j in range(2)]}


def read_out(nc, g, I, ry, pb):
    with ExitStack() as ctx:
        sb = lambda n, s, d=F32: ctx.enter_context(nc.sbuf_tensor(n, s, d))
        sem = lambda n: ctx.enter_context(nc.semaphore(n))
        g2, b2 = sb("ro_g2", [P, D]), sb("ro_b2", [P, KT])
        y = sb("ro_y", [P, 2, LAT_CHUNKS, KT, C])
        tile = lambda d, k: y[:, d, :, k, :]
        by_chunk = lambda x: x.rearrange("p (c t) -> p c t", t=C)
        sq, rs = sb("ro_sq", [P, 2, SEQ]), sb("ro_rs", [P, 4, SEQ])
        gates = ctx.enter_context(nc.psum_tensor("ro_gates", [P, SEQ], F32))
        means = [ctx.enter_context(nc.psum_tensor(f"ro_mean{k}", [P, SEQ], F32)) for k in range(2)]
        varis = [ctx.enter_context(nc.psum_tensor(f"ro_var{k}", [P, SEQ], F32)) for k in range(4)]
        inputs = ctx.enter_context(nc.psum_tensor("ro_pool", [P, 512], F32))
        u_made, u_read = sem("ro_u_made"), sem("ro_u_read")
        loaded, y_loaded = sem("ro_loaded"), [sem(f"ro_y{k}") for k in range(2)]
        mean_s, cen_s, sq_s, var_s, rs_s, yn_s = sem("ro_means"), sem("ro_centred"), sem("ro_squared"), sem("ro_vars"), sem("ro_rstd"), sem("ro_normed")
        gate, gated = sem("ro_gates"), sem("ro_gated")
        chan = g["chan"]
        N = 2 * KT
        with nc.Block() as block:
            @block.sync
            def _(sp):
                sp.dma_start(pb["w"][:, :, :], I["w_pool"]).then_inc(pb["loaded"], 16)
                sp.dma_start(g2[:, :], I["g2"]).then_inc(loaded, 16)
                for d in range(2):
                    sp.dma_start(y[:, d, :, :, :].rearrange("p c k t -> p c (k t)"),
                                 g["y_chunks"][d:d + 1, :].rearrange("a (c p n) -> (a p) c n", c=LAT_CHUNKS, p=P)).then_inc(y_loaded[d], 16)
                sp.dma_start(pb["pw"][:, :, :], I["pool_w"]).then_inc(pb["pw_loaded"], 16)
                for j in range(2):
                    sp.dma_start(pb["box"][:, j, :, :], I["pool_box"][j]).then_inc(pb["boxed"][j], 16)

            @block.tensor
            def _(pe):
                def pool_input(j):
                    t = j // 4
                    if j % 4 == 0 and t >= 1:
                        pe.wait_ge(u_read, t)
                    for k in (2 * (j % 4), 2 * (j % 4) + 1):
                        last = pe.matmul(inputs[:, :], g["hT"][:, k, CTX + t * P:CTX + t * P + P], pb["w"][:, k, :], start=(k == 0), stop=(k == KT - 1))
                    if j % 4 == 3:
                        last.then_inc(u_made, 1)

                pe.wait_ge(pb["loaded"], 16)
                for q in range(8):
                    pool_input(q)
                pe.wait_ge(loaded, 16)
                for j in range(N + 5):
                    if j < N and j % 2 == 1:
                        pool_input(8 + j // 2)
                    if j < N:
                        if j < 2:
                            pe.wait_ge(y_loaded[j], 16)
                        if j >= 2:
                            pe.wait_ge(cen_s, j - 1)
                        pe.matmul(means[j % 2][:, :], g["mean_w"], tile(j % 2, j // 2), start=True, stop=True).then_inc(mean_s, 1)
                    if 2 <= j < N + 2:
                        t = j - 2
                        pe.wait_ge(sq_s, t + 1)
                        if t >= 4:
                            pe.wait_ge(rs_s, t - 3)
                        pe.matmul(varis[t % 4][:, :], g["mean_w"], sq[:, t % 2, :], start=True, stop=True).then_inc(var_s, 1)
                    if j >= 6 and j % 2 == 0:
                        k = j // 2 - 3
                        if k >= 1:
                            pe.wait_ge(gated, k)
                        pe.matmul(gates[:, :], g2[:, k * P:k * P + P], g["xg"][:, :], start=True, stop=True).then_inc(gate, 1)

            @block.scalar
            def _(act):
                def read_input(t):
                    act.wait_ge(u_made, t + 1)
                    act.activation(pb["u"][:, t, :], inputs[:, :], ACT.Copy).then_inc(u_read, 1)

                read_input(0)
                read_input(1)
                for j in range(N + 2):
                    if j < N:
                        act.wait_ge(cen_s, j + 1)
                        if j >= 2:
                            act.wait_ge(var_s, j - 1)
                        act.activation(by_chunk(sq[:, j % 2, :]), tile(j % 2, j // 2), ACT.Square).then_inc(sq_s, 1)
                    if j >= 2:
                        t = j - 2
                        if t % 2 == 1:
                            act.wait_ge(var_s, t + 1)
                            if t >= 4:
                                act.wait_ge(yn_s, t - 3)
                            for v in range(2):
                                act.activation(rs[:, t % 4 - 1 + v, :], varis[t % 4 - 1 + v][:, :], ACT.Ln, bias=g["gn_eps"])
                            act.drain()
                            two = rs[:, t % 4 - 1:t % 4 + 1, :]
                            act.activation(two, two, ACT.Exp, scale=-0.5).then_inc(rs_s, 2)
                    if j in (7, 15):
                        read_input(2 + j // 8)

            @block.vector
            def _(dve):
                dve.tensor_scalar(b2[:, :], chan[:, 33:41], 2.0, None, ALU.mult)
                for j in range(N + 5):
                    if j < N:
                        dve.wait_ge(mean_s, j + 1)
                        dve.tensor_tensor(tile(j % 2, j // 2), tile(j % 2, j // 2), by_chunk(means[j % 2][:, :]), ALU.subtract).then_inc(cen_s, 1)
                    if j >= 5:
                        t = j - 5
                        dve.wait_ge(rs_s, t + 1)
                        yt = tile(t % 2, t // 2)
                        dve.tensor_tensor(yt, yt, by_chunk(rs[:, t % 4, :]), ALU.mult).then_inc(yn_s, 1)
                        if t % 2 == 1:
                            k = t // 2
                            out = ry[:, k, :]
                            dve.drain()
                            dve.tensor_tensor(by_chunk(out), tile(0, k), tile(1, k), ALU.add)
                            dve.drain()
                            dve.tensor_scalar(out, out, chan[:, 25 + k:26 + k], b2[:, k:k + 1], ALU.mult, ALU.add)
                            dve.drain()
                            dve.tensor_tensor(out, out, g["bonus"][:, k, :], ALU.add)
                            dve.drain()
                            dve.wait_ge(gate, k + 1)
                            dve.tensor_tensor(out, out, gates[:, :], ALU.mult).then_inc(gated, 1)


def pooling(nc, g, I, py, pb, next_loads):
    NT = SEQ // P
    with ExitStack() as ctx:
        sb = lambda n, s, d=F32: ctx.enter_context(nc.sbuf_tensor(n, s, d))
        sem = lambda n: ctx.enter_context(nc.semaphore(n))
        pw, u, box, boxed = pb["pw"], pb["u"], pb["box"], pb["boxed"]
        diff = sb("pl_diff", [P, 4, SEQ])
        ps = [ctx.enter_context(nc.psum_tensor(f"pl_ps{k}", [P, SEQ], F32)) for k in range(8)]
        d_ps, d_sb, y_ps = sem("pl_d_ps"), sem("pl_d_sb"), sem("pl_y_ps")
        with nc.Block() as block:
            @block.sync
            def _(sp):
                for j in (2, 3):
                    sp.wait_ge(d_ps, j - 1)
                    sp.dma_start(box[:, j % 2, :, :], I["pool_box"][j]).then_inc(boxed[j % 2], 16)
                next_loads(sp)

            @block.tensor
            def _(pe):
                pe.wait_ge(pb["pw_loaded"], 16)

                def make(j):
                    pe.wait_ge(d_sb, j + 1)
                    pe.matmul(ps[j][:, :], pw[:, j, :], diff[:, j, :], start=True, stop=True).then_inc(y_ps, 1)

                for j in range(4):
                    pe.wait_ge(boxed[j % 2], 16 * (j // 2 + 1))
                    for t in range(NT):
                        last = pe.matmul(ps[4 + j][:, :], u[:, t, j * P:j * P + P], box[:, j % 2, t, :], start=(t == 0), stop=(t == NT - 1))
                    last.then_inc(d_ps, 1)
                    if j:
                        make(j - 1)
                make(3)

            @block.vector
            def _(dve):
                for j in range(4):
                    dve.wait_ge(d_ps, j + 1)
                    dve.tensor_copy(diff[:, j, :], ps[4 + j][:, :]).then_inc(d_sb, 1)

            @block.scalar
            def _(act):
                for j in range(4):
                    act.wait_ge(y_ps, j + 1)
                    act.activation(py[:, j, :], ps[j][:, :], ACT.Copy, scale=g["chan"][:, 41 + j:42 + j])


MG = 2 * KT + 4 + KT


def merge_buffers(nc, ctx):
    return ctx.enter_context(nc.sbuf_tensor("mg_w", [P, 2, MG, P], F32)), [ctx.enter_context(nc.semaphore(f"mg_loaded{u}")) for u in range(2)]


def merge(nc, g, I, py, ry, merged, w, loaded, next_loads):
    with ExitStack() as ctx:
        sb = lambda n, s, d=F32: ctx.enter_context(nc.sbuf_tensor(n, s, d))
        sem = lambda n: ctx.enter_context(nc.semaphore(n))
        sig = sb("mg_sig", [P, 2, 2, SEQ])
        ps = [[ctx.enter_context(nc.psum_tensor(f"mg_ps{u}{k}", [P, SEQ], F32)) for k in range(4)] for u in range(2)]
        pe_s, act_s, dve_s = sem("mg_pe"), sem("mg_act"), sem("mg_dve")
        pe_o = Order(pe_s, ["gp", "gr", "pp", "rp"])
        act_o = Order(act_s, ["gp", "gr"])
        dve_o = Order(dve_s, ["pp", "rp", "out"])
        hT = g["hT"]
        NW = P * MG * P
        with nc.Block() as block:
            @block.sync
            def _(sp):
                next_loads(sp)
                with sp.Fori(0, KT // 2 - 1) as i:
                    for u in range(2):
                        at = sp.snap(i * 2 * NW + (u + 2) * NW)
                        sp.wait_ge(pe_s, i * 8 + 4 * u + 4)
                        sp.dma_start(w[:, u, :, :], flat(I["w_merge"], at, NW).rearrange("(p m n) -> p m n", p=P, m=MG)).then_inc(loaded[u], 16)

            @block.tensor
            def _(pe):
                with pe.Fori(0, KT // 2) as i:
                    for u in range(2):
                        m = i * 2 + u
                        pe.wait_ge(loaded[u], (i + 1) * 16)
                        pe.wait_ge(dve_s, i * 6)
                        for name, w0, n, src in (("gp", 0, KT, None), ("gr", KT, KT, None), ("pp", 2 * KT, 4, py), ("rp", 2 * KT + 4, KT, ry)):
                            for k in range(n):
                                rhs = hT[:, k, CTX:TOK] if src is None else src[:, k, :]
                                last = pe.matmul(ps[u]["gp gr pp rp".split().index(name)][:, :], w[:, u, w0 + k, :], rhs, start=(k == 0), stop=(k == n - 1))
                            pe_o.done(name, last)

            @block.scalar
            def _(act):
                with act.Fori(0, KT // 2) as i:
                    for u in range(2):
                        m = i * 2 + u
                        for k, name in enumerate(("gp", "gr")):
                            act.wait_ge(pe_s, m * 4 + k + 1)
                            if k == 0:
                                act.wait_ge(dve_s, i * 6)
                            act_o.done(name, act.activation(sig[:, u, k, :], ps[u][k][:, :], ACT.Sigmoid))

            @block.vector
            def _(dve):
                with dve.Fori(0, KT // 2) as i:
                    for u in range(2):
                        m = i * 2 + u
                        mr = dve.snap(i * 2 + u)
                        for k, name in enumerate(("pp", "rp")):
                            dve.wait_ge(act_s, m * 2 + k + 1)
                            dve.wait_ge(pe_s, m * 4 + 3 + k)
                            dve_o.done(name, dve.tensor_tensor(sig[:, u, k, :], sig[:, u, k, :], ps[u][2 + k][:, :], ALU.mult))
                        dve.drain()
                        dve_o.done("out", dve.tensor_tensor(merged[:, ds(mr, 1), :], sig[:, u, 0:1, :], sig[:, u, 1:2, :], ALU.add))


def project_out(nc, g, I, merged, x1, logits, w, w_loaded):
    NT = SEQ // P
    with ExitStack() as ctx:
        sb = lambda n, s, d=F32: ctx.enter_context(nc.sbuf_tensor(n, s, d))
        sem = lambda n: ctx.enter_context(nc.semaphore(n))
        rows = sb("po_rows", [P, 3, D])
        gains = sb("po_gains", [P, 2, D])
        rw, rb = sb("po_rw", [P, KT, 36]), sb("po_rb", [1, 36])
        sq = sb("po_sq", [P, D])
        f = sb("po_f", [P, 2, D])
        fT = sb("po_fT", [P, 2, KT, P])
        st = sb("po_st", [P, NT, 8])
        ps = [ctx.enter_context(nc.psum_tensor(f"po_ps{k}", [P, D], F32)) for k in range(2)]
        pt = ctx.enter_context(nc.psum_tensor("po_pt", [P, KT, P], F32))
        pl = ctx.enter_context(nc.psum_tensor("po_pl", [P, NT, P], F32))
        loaded, xload = sem("po_loaded"), sem("po_x")
        rows_ready = sem("po_rows_ready")
        pe_m, pe_t, pe_l = sem("po_product"), sem("po_turned"), sem("po_logits")
        act_sum, act_root, act_fT = sem("po_sum"), sem("po_root"), sem("po_fT_ready")
        dve_mean, dve_x, dve_f = sem("po_mean"), sem("po_x1"), sem("po_f_ready")
        fst = [sem("po_fst0"), sem("po_fst1")]
        with nc.Block() as block:
            @block.sync
            def _(sp):
                sp.dma_start(rw[:, :, :], I["router_w"]).then_inc(loaded, 16)
                sp.dma_start(rb[:, :], I["router_b"]).then_inc(loaded, 16)
                sp.dma_start(rows[:, :, :], g["mod_rows"][:, 0:3 * D].rearrange("p (a n) -> p a n", a=3)).then_inc(loaded, 16)
                for j in range(2):
                    sp.dma_start(gains[:, j, :], I["gains"][j:j + 1, :].to_broadcast([P, D])).then_inc(loaded, 16)
                for t in range(NT):
                    sp.dma_start(x1[:, t, :], I["x"][t * P:t * P + P, :]).then_inc(xload, 16)
                for t in range(NT):
                    sp.wait_ge(dve_f, t + 1)
                    sp.dma_start(g["f_dram"][t * P:t * P + P, :], f[:, t % 2, :]).then_inc(fst[t % 2], 16)
                for u in range(2):
                    sp.wait_ge(fst[u], NT // 2 * 16)

            @block.tensor
            def _(pe):
                pe.wait_ge(w_loaded, 16)

                def product(t):
                    if t >= 2:
                        pe.wait_ge(dve_x, t - 1)
                    for h in range(2):
                        for k in range(KT):
                            last = pe.matmul(ps[t % 2][:, h * 512:h * 512 + 512], merged[:, k, t * P:t * P + P], w[:, k, h * 512:h * 512 + 512], start=(k == 0), stop=(k == KT - 1))
                    last.then_inc(pe_m, 1)

                def turn(t):
                    pe.wait_ge(dve_f, t + 1)
                    if t:
                        pe.wait_ge(act_fT, t)
                    for k in range(KT):
                        last = pe.transpose(pt[:, k, :], f[:, t % 2, k * P:k * P + P], g["ident"])
                    last.then_inc(pe_t, 1)

                def route(t):
                    if t == 0:
                        pe.wait_ge(loaded, 80)
                    pe.wait_ge(act_fT, t + 1)
                    for k in range(KT):
                        pe.matmul(pl[:, t, 0:36], fT[:, t % 2, k, :], rw[:, k, :], start=(k == 0), stop=False)
                    pe.matmul(pl[:, t, 0:36], g["mask"]("ones")[0:1, :], rb[:, :], start=False, stop=True).then_inc(pe_l, 1)

                product(0)
                for t in range(NT):
                    if t + 1 < NT:
                        product(t + 1)
                    turn(t)
                    route(t)

            @block.scalar
            def _(act):
                for t in range(NT):
                    act.wait_ge(pe_m, t + 1)
                    act.activation(sq[:, :], ps[t % 2][:, :], ACT.Square, accum_out=st[:, t, 0:1])
                    act.drain().then_inc(act_sum, 1)
                    act.wait_ge(dve_mean, 2 * t + 1)
                    act.activation(st[:, t, 2:3], st[:, t, 1:2], ACT.Sqrt).then_inc(act_root, 1)
                    act.wait_ge(dve_x, t + 1)
                    act.activation(sq[:, :], x1[:, t, :], ACT.Square, accum_out=st[:, t, 4:5])
                    act.drain().then_inc(act_sum, 1)
                    act.wait_ge(dve_mean, 2 * t + 2)
                    act.activation(st[:, t, 6:7], st[:, t, 5:6], ACT.Sqrt).then_inc(act_root, 1)
                    act.wait_ge(pe_t, t + 1)
                    if t >= 2:
                        act.wait_ge(pe_l, t - 1)
                    act.activation(fT[:, t % 2, :, :], pt[:, :, :], ACT.Copy).then_inc(act_fT, 1)

            @block.vector
            def _(dve):
                dve.wait_ge(loaded, 80)
                dve.tensor_tensor(rows[:, 0, :], rows[:, 0, :], gains[:, 0, :], ALU.mult)
                dve.scalar_tensor_tensor(out=rows[:, 2, :], in0=rows[:, 2, :], scalar=1.0, in1=gains[:, 1, :], op0=ALU.add, op1=ALU.mult)
                dve.wait_ge(xload, NT * 16)
                dve.drain()
                for t in range(NT):
                    dve.wait_ge(act_sum, 2 * t + 1)
                    dve.tensor_scalar(st[:, t, 1:2], st[:, t, 0:1], 1.0 / D, RMS_EPS, ALU.mult, ALU.add).then_inc(dve_mean, 1)
                    dve.wait_ge(act_root, 2 * t + 1)
                    dve.reciprocal(st[:, t, 3:4], st[:, t, 2:3])
                    dve.drain()
                    if t >= 2:
                        dve.wait_ge(pe_t, t - 1)
                        dve.wait_ge(fst[t % 2], 16 * (t // 2))
                    ft = f[:, t % 2, :]
                    dve.scalar_tensor_tensor(out=ft, in0=ps[t % 2][:, :], scalar=st[:, t, 3:4], in1=rows[:, 0, :], op0=ALU.mult, op1=ALU.mult)
                    dve.drain()
                    dve.tensor_tensor(x1[:, t, :], x1[:, t, :], ft, ALU.add).then_inc(dve_x, 1)
                    dve.wait_ge(act_sum, 2 * t + 2)
                    dve.tensor_scalar(st[:, t, 5:6], st[:, t, 4:5], 1.0 / D, RMS_EPS, ALU.mult, ALU.add).then_inc(dve_mean, 1)
                    dve.wait_ge(act_root, 2 * t + 2)
                    dve.reciprocal(st[:, t, 7:8], st[:, t, 6:7])
                    dve.drain()
                    dve.scalar_tensor_tensor(out=ft, in0=x1[:, t, :], scalar=st[:, t, 7:8], in1=rows[:, 2, :], op0=ALU.mult, op1=ALU.mult)
                    dve.drain()
                    dve.tensor_tensor(ft, ft, rows[:, 1, :], ALU.add).then_inc(dve_f, 1)
                dve.wait_ge(pe_l, NT)
                dve.tensor_copy(logits[:, :, :], pl[:, :, 0:36])


SLOTS = P
SPILL = 7
TILES = NE + SPILL
WSLOTS = 4
EXPERT_W = KT * 2 * FE + 2 * D


def route(nc, g, I, logits, R, w, wl):
    NT = SEQ // P
    with ExitStack() as ctx:
        sb = lambda n, s, d=F32: ctx.enter_context(nc.sbuf_tensor(n, s, d))
        sem = lambda n: ctx.enter_context(nc.semaphore(n))
        t4 = lambda n: sb(n, [P, NT, 4])
        t8 = lambda n: sb(n, [P, NT, 8])
        t32 = lambda n: sb(n, [P, NT, NE])
        m1, s1 = sb("rt_m1", [P, NT, 1]), sb("rt_s1", [P, NT, 1])
        eg, tg, gh = t4("rt_eg"), t4("rt_tg"), t4("rt_gh")
        sel, te, oh1, oh2, msk = t8("rt_sel"), t8("rt_te"), t8("rt_oh1"), t8("rt_oh2"), t8("rt_msk")
        e32, O1, O2, both, pre, tmp = (t32(f"rt_x{j}") for j in range(6))
        ma, mb, e2, w1 = (sb(f"rt_m{j}", [P, NT, 1]) for j in "abcd")
        rev = sb("rt_rev", [P, 8])
        base, cnt, over, tmpc, incl = (sb(f"rt_c{j}", [P, NE]) for j in range(5))
        ovq = sb("rt_ovq", [P, SPILL])
        tokid = sb("rt_tokid", [P, NT])
        table = sb("rt_table", [TILES, P])
        ps = ctx.enter_context(nc.psum_tensor("rt_ps", [P, NT + 1, NE], F32))
        pt = ctx.enter_context(nc.psum_tensor("rt_pt", [P, TILES], F32))
        ex, ex_done, cst, both_ready, pref = sem("rt_exp_in"), sem("rt_exp"), sem("rt_cst"), sem("rt_both"), sem("rt_prefix")
        slots_ready, scattered, tab, turned = sem("rt_slots"), sem("rt_scattered"), sem("rt_tab"), sem("rt_turned")
        X = AX.X
        with nc.Block() as block:
            @block.sync
            def _(sp):
                for u in range(WSLOTS):
                    load_expert(sp, I, w, wl, u, u * P * EXPERT_W)

            @block.gpsimd
            def _(pool):
                pool.iota(rev[:, :], [[-1, 8]], base=8, channel_multiplier=0, allow_small_or_imprecise_dtypes=True)
                pool.iota(base[:, :], [[SLOTS, NE]], base=0, channel_multiplier=0, allow_small_or_imprecise_dtypes=True)
                pool.iota(tokid[:, :], [[P, NT]], base=0, channel_multiplier=1, allow_small_or_imprecise_dtypes=True)
                pool.drain().then_inc(cst, 1)
                pool.wait_ge(slots_ready, 1)
                for t in range(NT):
                    for j in range(2):
                        pool.indirect_dma_start(out=g["slot_tok"], out_offset=bass.IndirectOffsetOnAxis(ap=R["slot"][:, j, t:t + 1], axis=0),
                                                in_=tokid[:, t:t + 1], in_offset=None).then_inc(scattered, 16)
                pool.wait_ge(scattered, 2 * NT * 16)
                pool.dma_start(table[:, :], g["slot_tok"].rearrange("(t s) a -> t (s a)", t=TILES)).then_inc(tab, 16)

            @block.scalar
            def _(act):
                act.wait_ge(ex, 1)
                act.activation(eg[:, :, :], tg[:, :, :], ACT.Exp).then_inc(ex_done, 1)
                act.wait_ge(ex, 2)
                act.activation(e2[:, :, :], mb[:, :, :], ACT.Exp).then_inc(ex_done, 1)

            @block.tensor
            def _(pe):
                pe.wait_ge(both_ready, 1)
                for t in range(NT + 1):
                    for q in range(t):
                        last = pe.matmul(ps[:, t, :], g["mask"]("ones"), both[:, q, :], start=(q == 0), stop=(t == NT and q == t - 1))
                    if t < NT:
                        last = pe.matmul(ps[:, t, :], g["mask"]("before"), both[:, t, :], start=(t == 0), stop=True)
                last.then_inc(pref, 1)
                pe.wait_ge(tab, 16)
                pe.transpose(pt[:, :], table[:, :], g["ident"][0:TILES, 0:TILES]).then_inc(turned, 1)

            @block.vector
            def _(dve):
                def tt(o, a, b, op):
                    dve.tensor_tensor(o, a, b, op)
                    dve.drain()

                def ts(o, a, s0, s1_, op0, op1=ALU.bypass):
                    dve.tensor_scalar(o, a, s0, s1_, op0, op1)
                    dve.drain()

                def red(o, a, op):
                    dve.tensor_reduce(o, a, X, op)
                    dve.drain()

                def first_hot(out, score, best, n, tmp_):
                    red(best, score, ALU.max)
                    tt(tmp_, score, best.to_broadcast([P, NT, n]), ALU.is_equal)
                    tt(tmp_, tmp_, rev[:, 8 - n:8].unsqueeze(1).to_broadcast([P, NT, n]), ALU.mult)
                    red(s1[:, :, :], tmp_, ALU.max)
                    tt(out, tmp_, s1[:, :, :].to_broadcast([P, NT, n]), ALU.is_equal)

                gl = logits[:, :, 0:4]
                el = logits[:, :, 4:36]
                dve.wait_ge(cst, 1)
                first_hot(gh[:, :, :], gl, m1[:, :, :], 4, tg[:, :, :])
                tt(tg[:, :, :], gl, m1[:, :, :].to_broadcast([P, NT, 4]), ALU.subtract)
                dve.drain().then_inc(ex, 1)
                for q in range(4):
                    src = el[:, :, 8 * q:8 * q + 8]
                    if q == 0:
                        tt(sel[:, :, :], src, gh[:, :, 0:1].to_broadcast([P, NT, 8]), ALU.mult)
                    else:
                        tt(te[:, :, :], src, gh[:, :, q:q + 1].to_broadcast([P, NT, 8]), ALU.mult)
                        tt(sel[:, :, :], sel[:, :, :], te[:, :, :], ALU.add)
                first_hot(oh1[:, :, :], sel[:, :, :], ma[:, :, :], 8, te[:, :, :])
                dve.scalar_tensor_tensor(out=msk[:, :, :], in0=oh1[:, :, :], scalar=-3.0e38, in1=sel[:, :, :], op0=ALU.mult, op1=ALU.add)
                dve.drain()
                first_hot(oh2[:, :, :], msk[:, :, :], mb[:, :, :], 8, te[:, :, :])
                tt(mb[:, :, :], mb[:, :, :], ma[:, :, :], ALU.subtract)
                dve.drain().then_inc(ex, 1)
                for o, oh in ((O1, oh1), (O2, oh2)):
                    for q in range(4):
                        dve.tensor_tensor(o[:, :, 8 * q:8 * q + 8], oh[:, :, :], gh[:, :, q:q + 1].to_broadcast([P, NT, 8]), ALU.mult)
                dve.drain()
                tt(both[:, :, :], O1[:, :, :], O2[:, :, :], ALU.add)
                dve.drain().then_inc(both_ready, 1)
                dve.wait_ge(ex_done, 2)
                red(m1[:, :, :], eg[:, :, :], ALU.add)
                dve.reciprocal(m1[:, :, :], m1[:, :, :])
                ts(w1[:, :, :], e2[:, :, :], 1.0, None, ALU.add)
                dve.reciprocal(w1[:, :, :], w1[:, :, :])
                dve.drain()
                gate = lambda j: R["gate"][:, j, :].unsqueeze(2)
                tt(gate(0), m1[:, :, :], w1[:, :, :], ALU.mult)
                tt(gate(1), gate(0), e2[:, :, :], ALU.mult)
                dve.wait_ge(pref, 1)
                dve.tensor_copy(pre[:, :, :], ps[:, 0:NT, :])
                dve.tensor_copy(cnt[:, :], ps[:, NT, :])
                dve.drain()
                ts(over[:, :], cnt[:, :], float(SLOTS), None, ALU.is_gt)
                for j in (2, 3):
                    dve.scalar_tensor_tensor(out=over[:, :], in0=cnt[:, :], scalar=float(j * SLOTS), in1=over[:, :], op0=ALU.is_gt, op1=ALU.add)
                    dve.drain()
                ts(tmpc[:, :], over[:, :], 0.0, 1.0, ALU.mult, ALU.add)
                dve.tensor_tensor_scan(incl[:, :], tmpc[:, :], over[:, :], 0.0, ALU.mult, ALU.add)
                dve.drain()
                for q in range(SPILL):
                    dve.tensor_scalar(tmpc[:, :], incl[:, :], float(q), None, ALU.is_le)
                    dve.drain()
                    dve.tensor_reduce(ovq[:, q:q + 1], tmpc[:, :], X, ALU.add)
                    dve.drain()
                ts(ovq[:, :], ovq[:, :], float(NE - 1), None, ALU.min)
                dve.tensor_copy(R["spill_expert"][:, :], ovq[:, :])
                dve.tensor_copy(R["spill_tiles"][:, :], incl[:, NE - 1:NE])
                tt(tmpc[:, :], incl[:, :], over[:, :], ALU.subtract)
                ts(tmpc[:, :], tmpc[:, :], float(SLOTS), float((NE - 1) * SLOTS), ALU.mult, ALU.add)
                tt(tmpc[:, :], tmpc[:, :], base[:, :], ALU.subtract)
                ts(tmp[:, :, :], pre[:, :, :], float(SLOTS), None, ALU.is_ge)
                tt(tmp[:, :, :], tmp[:, :, :], tmpc[:, :].unsqueeze(1).to_broadcast([P, NT, NE]), ALU.mult)
                tt(pre[:, :, :], pre[:, :, :], tmp[:, :, :], ALU.add)
                tt(pre[:, :, :], pre[:, :, :], base[:, :].unsqueeze(1).to_broadcast([P, NT, NE]), ALU.add)
                for j, o in enumerate((O1, O2)):
                    tt(o[:, :, :], o[:, :, :], pre[:, :, :], ALU.mult)
                    red(s1[:, :, :], o[:, :, :], ALU.add)
                    dve.tensor_copy(R["slot"][:, j, :], s1[:, :, :].rearrange("p t a -> p (t a)"))
                    dve.drain()
                dve.drain().then_inc(slots_ready, 1)
                dve.wait_ge(turned, 1)
                dve.tensor_copy(R["tok"][:, :], pt[:, :])


def expert_weights(nc, ctx):
    w = ctx.enter_context(nc.sbuf_tensor("ex_w", [P, WSLOTS, EXPERT_W], F32))
    return w, [ctx.enter_context(nc.semaphore(f"ex_w{u}")) for u in range(WSLOTS)]


def load_expert(sp, I, w, wl, u, at):
    sp.dma_start(w[:, u, :], flat(I["w_experts"], at, P * EXPERT_W).rearrange("(p n) -> p n", p=P)).then_inc(wl[u], 16)


def experts(nc, g, I, R, w, wl):
    with ExitStack() as ctx:
        sb = lambda n, s, d=F32: ctx.enter_context(nc.sbuf_tensor(n, s, d))
        sem = lambda n: ctx.enter_context(nc.semaphore(n))
        idx = sb("ex_idx", [P, 2, 1], U32)
        xe = sb("ex_x", [P, 2, D])
        xT = sb("ex_xT", [P, 2, KT, P])
        sg = sb("ex_sig", [P, 2, FE])
        h = sb("ex_h", [P, 2, FE])
        hT = sb("ex_hT", [P, 2, 2, P])
        y = sb("ex_y", [P, 2, D])
        p_x = ctx.enter_context(nc.psum_tensor("ex_px", [P, KT, P], F32))
        p_gu = [ctx.enter_context(nc.psum_tensor(f"ex_pgu{u}", [P, 2 * FE], F32)) for u in range(2)]
        p_h = [ctx.enter_context(nc.psum_tensor(f"ex_ph{u}", [P, 2, P], F32)) for u in range(2)]
        p_y = ctx.enter_context(nc.psum_tensor("ex_py", [P, D], F32))
        NWE, NYE = P * EXPERT_W, SLOTS * D
        up = lambda u: w[:, u, 0:KT * 2 * FE].rearrange("p (k n) -> p k n", k=KT)
        dn = lambda u: w[:, u, KT * 2 * FE:].rearrange("p (k n) -> p k n", k=2)
        steps = ("idx", "turned", "xT", "gu", "sig", "h", "hturned", "hT", "down", "y")

        def index(pool, v, tile):
            return pool.tensor_copy(idx[:, v, :], R["tok"][:, ds(tile, 1)])

        def gather(pool, v):
            return pool.indirect_dma_start(out=xe[:, v, :], out_offset=None, in_=g["f_dram"],
                                           in_offset=bass.IndirectOffsetOnAxis(ap=idx[:, v, 0:1], axis=0))

        def turn(pe, v):
            for k in range(KT):
                last = pe.transpose(p_x[:, k, :], xe[:, v, k * P:k * P + P], g["ident"])
            return last

        def gate_up(pe, u, v):
            for k in range(KT):
                last = pe.matmul(p_gu[v][:, :], xT[:, v, k, :], up(u)[:, k, :], start=(k == 0), stop=(k == KT - 1))
            return last

        def turn_h(pe, v):
            for k in range(2):
                last = pe.transpose(p_h[v][:, k, :], h[:, v, k * P:k * P + P], g["ident"])
            return last

        def down(pe, u, v):
            for q in range(2):
                for k in range(2):
                    last = pe.matmul(p_y[:, q * 512:q * 512 + 512], hT[:, v, k, :], dn(u)[:, k, q * 512:q * 512 + 512], start=(k == 0), stop=(k == 1))
            return last

        def copy_xT(act, v):
            return act.activation(xT[:, v, :, :], p_x[:, :, :], ACT.Copy)

        def sigmoid(act, v):
            return act.activation(sg[:, v, :], p_gu[v][:, 0:FE], ACT.Sigmoid)

        def copy_y(act, v):
            return act.activation(y[:, v, :], p_y[:, :], ACT.Copy)

        def hidden(dve, v):
            dve.tensor_tensor(sg[:, v, :], sg[:, v, :], p_gu[v][:, 0:FE], ALU.mult)
            dve.drain()
            return dve.tensor_tensor(h[:, v, :], sg[:, v, :], p_gu[v][:, FE:2 * FE], ALU.mult)

        def copy_hT(dve, v):
            return dve.tensor_copy(hT[:, v, :, :], p_h[v][:, :, :])

        def store(sp, v, at, sem_):
            sp.dma_start(flat(g["y_dram"], at, NYE).rearrange("(p n) -> p n", p=P), y[:, v, :]).then_inc(sem_, 16)

        s = {n: sem(f"ex_{n}") for n in steps}
        yst = [sem(f"ex_y{v}_stored") for v in range(2)]
        LOOPED = (NE - 2) // WSLOTS

        def pipeline(eng, step):
            with eng.Fori(0, LOOPED) as i:
                for u in range(WSLOTS):
                    step(i * WSLOTS + u, i, u)
            for t in range(LOOPED * WSLOTS, NE - 2):
                step(t, t // WSLOTS, t % WSLOTS)

        with nc.Block() as block:
            @block.sync
            def _(sp):
                for v in range(2):
                    sp.sem_inc(yst[v], 16)
                with sp.Fori(0, NE // WSLOTS - 1) as i:
                    for u in range(WSLOTS):
                        at = sp.snap(i * WSLOTS * NWE + (u + WSLOTS) * NWE)
                        at_y = sp.snap(i * WSLOTS * NYE + u * NYE)
                        sp.wait_ge(s["down"], i * WSLOTS + u + 1)
                        load_expert(sp, I, w, wl, u, at)
                        sp.wait_ge(s["y"], i * WSLOTS + u + 2)
                        store(sp, u % 2, at_y, yst[u % 2])
                for t in range(NE - WSLOTS, NE):
                    sp.wait_ge(s["y"], t + 2)
                    store(sp, t % 2, t * NYE, yst[t % 2])
                for v in range(2):
                    sp.wait_ge(yst[v], (NE // 2 + 1) * 16)

            @block.gpsimd
            def _(pool):
                for v in range(2):
                    index(pool, v, v).then_inc(s["idx"], 1)
                pool.wait_ge(s["idx"], 2)
                for v in range(2):
                    gather(pool, v).then_inc(g["gathered"][v], 16)

                def step(t, i, u):
                    v = u % 2
                    tile = pool.snap(i * WSLOTS + u + 2) if not isinstance(t, int) else t + 2
                    pool.wait_ge(s["turned"], t + 1)
                    pool.sem_inc(g["noted"]["pool"], 1)
                    index(pool, v, tile).then_inc(s["idx"], 1)
                    pool.wait_ge(s["idx"], t + 3)
                    pool.sem_inc(g["noted"]["pool"], 1)
                    gather(pool, v).then_inc(g["gathered"][v], 16)
                pipeline(pool, step)

            @block.tensor
            def _(pe):
                def turn_tokens(t, v, round_):
                    pe.wait_ge(g["gathered"][v], (round_ + 1) * 16)
                    turn(pe, v).then_inc(s["turned"], 1)

                def make_gate_up(t, u, round_):
                    pe.wait_ge(wl[u], (round_ + 1) * 16)
                    pe.wait_ge(s["xT"], t + 1)
                    gate_up(pe, u, u % 2).then_inc(s["gu"], 1)

                def make_down(t, u):
                    pe.wait_ge(s["hT"], t + 1)
                    pe.wait_ge(s["y"], t + 1)
                    down(pe, u, u % 2).then_inc(s["down"], 1)

                def turn_hidden(t, v):
                    pe.wait_ge(s["h"], t + 1)
                    turn_h(pe, v).then_inc(s["hturned"], 1)

                turn_tokens(0, 0, 0)
                make_gate_up(0, 0, 0)
                turn_tokens(1, 1, 0)
                turn_hidden(0, 0)

                def step(t, i, u):
                    nxt = (u + 1) % WSLOTS
                    make_gate_up(t + 1, nxt, i + (u + 1) // WSLOTS)
                    turn_tokens(t + 2, u % 2, i * (WSLOTS // 2) + (u // 2 + 1))
                    make_down(t, u)
                    turn_hidden(t + 1, nxt % 2)
                pipeline(pe, step)
                t = NE - 2
                make_gate_up(t + 1, (t + 1) % WSLOTS, (t + 1) // WSLOTS)
                make_down(t, t % WSLOTS)
                turn_hidden(t + 1, (t + 1) % 2)
                make_down(t + 1, (t + 1) % WSLOTS)

            @block.scalar
            def _(act):
                act.sem_inc(s["y"], 1)

                def xt(t, v):
                    act.wait_ge(s["turned"], t + 1)
                    copy_xT(act, v).then_inc(s["xT"], 1)

                def sig(t, v):
                    act.wait_ge(s["gu"], t + 1)
                    sigmoid(act, v).then_inc(s["sig"], 1)

                def rows(t, v, round_):
                    act.wait_ge(s["down"], t + 1)
                    act.wait_ge(yst[v], (round_ + 1) * 16)
                    copy_y(act, v).then_inc(s["y"], 1)

                xt(0, 0)
                sig(0, 0)
                xt(1, 1)

                def step(t, i, u):
                    sig(t + 1, (u + 1) % 2)
                    xt(t + 2, u % 2)
                    rows(t, u % 2, i * (WSLOTS // 2) + u // 2)
                pipeline(act, step)
                t = NE - 2
                sig(t + 1, (t + 1) % 2)
                rows(t, t % 2, t // 2)
                rows(t + 1, (t + 1) % 2, (t + 1) // 2)

            @block.vector
            def _(dve):
                def make_h(t, v):
                    dve.wait_ge(s["sig"], t + 1)
                    hidden(dve, v).then_inc(s["h"], 1)

                def make_hT(t, v):
                    dve.wait_ge(s["hturned"], t + 1)
                    copy_hT(dve, v).then_inc(s["hT"], 1)

                make_h(0, 0)

                def step(t, i, u):
                    make_hT(t, u % 2)
                    make_h(t + 1, (u + 1) % 2)
                pipeline(dve, step)
                t = NE - 2
                make_hT(t, t % 2)
                make_h(t + 1, (t + 1) % 2)
                make_hT(t + 1, (t + 1) % 2)

        s = {n: sem(f"sp_{n}") for n in steps}
        loaded, gathered, stored = sem("sp_w"), sem("sp_gathered"), sem("sp_stored")

        def spill(eng, body):
            count = eng.value_load(R["spill_tiles"][0:1, 0:1], min_val=0, max_val=SPILL)
            with eng.Fori(0, SPILL) as i:
                with eng.If(count > i):
                    body(i)

        with nc.Block() as block:
            @block.sync
            def _(sp):
                sp.sem_inc(s["down"], 1)

                def body(i):
                    e = sp.value_load(R["spill_expert"][0:1, ds(i, 1)], min_val=0, max_val=NE - 1)
                    at = sp.snap(e * NWE)
                    at_y = sp.snap(i * NYE + NE * NYE)
                    sp.wait_ge(s["down"], i + 1)
                    load_expert(sp, I, w, [loaded], 0, at)
                    sp.wait_ge(s["y"], i + 1)
                    store(sp, 0, at_y, stored)
                    sp.wait_ge(stored, i * 16 + 16)
                    sp.sem_inc(g["noted"]["sp"], 1)
                spill(sp, body)

            @block.gpsimd
            def _(pool):
                pool.sem_inc(s["turned"], 1)

                def body(i):
                    tile = pool.snap(i + NE)
                    pool.wait_ge(s["turned"], i + 1)
                    pool.sem_inc(g["noted"]["pool"], 1)
                    index(pool, 0, tile).then_inc(s["idx"], 1)
                    pool.wait_ge(s["idx"], i + 1)
                    pool.sem_inc(g["noted"]["pool"], 1)
                    gather(pool, 0).then_inc(gathered, 16)
                spill(pool, body)

            @block.tensor
            def _(pe):
                def body(i):
                    pe.wait_ge(gathered, (i + 1) * 16)
                    turn(pe, 0).then_inc(s["turned"], 1)
                    pe.wait_ge(loaded, (i + 1) * 16)
                    pe.wait_ge(s["xT"], i + 1)
                    gate_up(pe, 0, 0).then_inc(s["gu"], 1)
                    pe.wait_ge(s["h"], i + 1)
                    turn_h(pe, 0).then_inc(s["hturned"], 1)
                    pe.wait_ge(s["hT"], i + 1)
                    down(pe, 0, 0).then_inc(s["down"], 1)
                spill(pe, body)

            @block.scalar
            def _(act):
                def body(i):
                    act.wait_ge(s["turned"], i + 2)
                    copy_xT(act, 0).then_inc(s["xT"], 1)
                    act.wait_ge(s["gu"], i + 1)
                    sigmoid(act, 0).then_inc(s["sig"], 1)
                    act.wait_ge(s["down"], i + 2)
                    copy_y(act, 0).then_inc(s["y"], 1)
                spill(act, body)

            @block.vector
            def _(dve):
                def body(i):
                    dve.wait_ge(s["sig"], i + 1)
                    hidden(dve, 0).then_inc(s["h"], 1)
                    dve.wait_ge(s["hturned"], i + 1)
                    copy_hT(dve, 0).then_inc(s["hT"], 1)
                spill(dve, body)


def combine(nc, g, I, R, x1, out):
    NT = SEQ // P
    with ExitStack() as ctx:
        sb = lambda n, s, d=F32: ctx.enter_context(nc.sbuf_tensor(n, s, d))
        sem = lambda n: ctx.enter_context(nc.semaphore(n))
        rows = sb("cb_rows", [P, NT, 2, D])
        gt, gain = sb("cb_gt", [P, D]), sb("cb_gain", [P, D])
        acc = sb("cb_acc", [P, NT, D])
        sq = sb("cb_sq", [P, D])
        st = sb("cb_st", [P, NT, 4])
        loaded, gath = sem("cb_loaded"), [sem(f"cb_g{t}") for t in range(NT)]
        acc_s, sum_s, mean_s, root_s, out_s, stored = sem("cb_acc_s"), sem("cb_sum"), sem("cb_mean"), sem("cb_root"), sem("cb_out"), sem("cb_stored")
        with nc.Block() as block:
            @block.gpsimd
            def _(pool):
                for t in range(NT):
                    for j in range(2):
                        pool.indirect_dma_start(out=rows[:, t, j, :], out_offset=None, in_=g["y_dram"],
                                                in_offset=bass.IndirectOffsetOnAxis(ap=R["slot"][:, j, t:t + 1], axis=0)).then_inc(gath[t], 16)

            @block.sync
            def _(sp):
                sp.dma_start(gt[:, :], g["mod_rows"][:, 3 * D:4 * D]).then_inc(loaded, 16)
                sp.dma_start(gain[:, :], I["gains"][2:3, :].to_broadcast([P, D])).then_inc(loaded, 16)
                for t in range(NT):
                    sp.wait_ge(out_s, t + 1)
                    sp.dma_start(out[0, t * P:t * P + P, :], acc[:, t, :]).then_inc(stored, 16)
                sp.wait_ge(stored, NT * 16)

            @block.scalar
            def _(act):
                for t in range(NT):
                    act.wait_ge(acc_s, t + 1)
                    act.activation(sq[:, :], acc[:, t, :], ACT.Square, accum_out=st[:, t, 0:1])
                    act.drain().then_inc(sum_s, 1)
                    act.wait_ge(mean_s, t + 1)
                    act.activation(st[:, t, 2:3], st[:, t, 1:2], ACT.Sqrt).then_inc(root_s, 1)

            @block.vector
            def _(dve):
                dve.wait_ge(loaded, 32)
                dve.tensor_tensor(gt[:, :], gt[:, :], gain[:, :], ALU.mult)
                for t in range(NT):
                    dve.wait_ge(gath[t], 32)
                    dve.tensor_scalar(rows[:, t, 0, :], rows[:, t, 0, :], R["gate"][:, 0, t:t + 1], None, ALU.mult)
                    dve.drain()
                    dve.scalar_tensor_tensor(out=acc[:, t, :], in0=rows[:, t, 1, :], scalar=R["gate"][:, 1, t:t + 1], in1=rows[:, t, 0, :], op0=ALU.mult, op1=ALU.add).then_inc(acc_s, 1)
                for t in range(NT):
                    dve.wait_ge(sum_s, t + 1)
                    dve.tensor_scalar(st[:, t, 1:2], st[:, t, 0:1], 1.0 / D, RMS_EPS, ALU.mult, ALU.add).then_inc(mean_s, 1)
                    dve.wait_ge(root_s, t + 1)
                    dve.reciprocal(st[:, t, 3:4], st[:, t, 2:3])
                    dve.drain()
                    dve.scalar_tensor_tensor(out=acc[:, t, :], in0=acc[:, t, :], scalar=st[:, t, 3:4], in1=gt[:, :], op0=ALU.mult, op1=ALU.mult)
                    dve.drain()
                    dve.tensor_tensor(acc[:, t, :], acc[:, t, :], x1[:, t, :], ALU.add).then_inc(out_s, 1)


def layout(a):
    a = {k: np.asarray(v) for k, v in a.items()}
    L = {k: (v[0] if k not in ("x", "ctx", "c", "c_ctx") else v) for k, v in a.items()}
    out = {}
    cols = lambda v: v.reshape(-1, P).T
    out["x"], out["ctx"] = a["x"][0], a["ctx"][0]
    out["cvecs"] = np.stack([cols(a["c"][0]), cols(a["c_ctx"])], 1)
    out["ada_b"] = L["ada_b"][None]
    out["ada_w"] = L["ada_w"].reshape(KT, P, ADA_N, 512).transpose(2, 1, 0, 3)
    out["masks"] = mask_table()
    conv = L["conv_w"]
    chan = np.zeros((P, 64), np.float32)
    chan[:, 0:8] = cols(L["norm_gains"][0])
    for j in range(3):
        chan[:, 16 + 3 * j:19 + 3 * j] = conv[:, 3 * D + j * P:3 * D + (j + 1) * P].T
    chan[:, 25:33], chan[:, 33:41] = cols(L["lnx_w"]), cols(L["lnx_b"])
    chan[:, 41:45] = cols(L["pool_scale"])
    out["chan"] = chan
    win = L["w_in"]
    tiles = lambda w: w.reshape(KT, P, -1, P).transpose(2, 1, 0, 3)
    c0 = 512
    out["w_lr"] = tiles(win[:, c0 + 3 * D:c0 + 3 * D + 3 * P]).transpose(1, 0, 2, 3)
    r, k, v = (tiles(win[:, c0 + j * D:c0 + (j + 1) * D]) for j in range(3))
    w2 = L["w2"].reshape(P, KT, P).transpose(1, 0, 2)[:, :, None]
    a2 = L["a2"].reshape(P, KT, P).transpose(1, 0, 2)[:, :, None]
    out["w_prep"] = np.concatenate([r, k, v, w2, a2], 2).reshape(KT, P, PREPW)
    par = [conv[q, j * D:(j + 1) * D] for j in range(3) for q in range(3)]
    par += [L["w0"][0], L["w0"][1], L["a0"][0], L["a0"][1], L["k_k"], L["k_a"], L["r_k"].reshape(-1)]
    out["p_prep"] = np.stack([q.reshape(KT, P) for q in par], 2)
    out["g2"] = L["g2"]
    out["w_pool"] = win[:, 0:512].reshape(KT, P, 512).transpose(1, 0, 2)
    out["pool_w"] = L["pool_w"].transpose(1, 0, 2)
    out["pool_box"] = pool_table()
    gates = tiles(win[:, 512 + 3456:])
    pp, rp = (w.reshape(-1, P, KT, P).transpose(2, 1, 0, 3) for w in (L["pool_proj"], L["rwkv_proj"]))
    out["w_merge"] = np.concatenate([gates[0:KT], gates[KT:], pp, rp], 2).reshape(KT, P, MG * P)
    out["w_out"] = L["w_out"].reshape(KT, P, D).transpose(1, 0, 2)
    out["router_w"] = np.concatenate([L["router_group_w"], L["router_expert_w"]], 1).reshape(KT, P, 36).transpose(1, 0, 2)
    out["router_b"] = np.concatenate([L["router_group_b"], L["router_expert_b"]])[None]
    out["gains"] = L["norm_gains"][1:4]
    gu = np.concatenate([L["expert_w_gate"], L["expert_w_up"]], 2).reshape(NE, KT, P, 2 * FE).transpose(0, 2, 1, 3).reshape(NE, P, -1)
    dn = L["expert_w_down"].reshape(NE, 2, P, D).transpose(0, 2, 1, 3).reshape(NE, P, -1)
    out["w_experts"] = np.concatenate([gu, dn], 2)
    return {k: np.ascontiguousarray(v) for k, v in out.items()}


def program(nc, I, out):
    with ExitStack() as ctx:
        sb = lambda n, s, d=F32: ctx.enter_context(nc.sbuf_tensor(n, s, d))
        dram = lambda n, s, d=F32: nc.dram_tensor(n, s, d, kind="Internal").ap()
        g = {"masks": sb("masks_sb", [P, NM, P]), "chan": sb("chan_sb", [P, 64]), "mod": sb("mod_cols", [P, 2 * KT, 2])}
        g["noted"] = {e: ctx.enter_context(nc.semaphore(f"noted_{e}")) for e in ("dve", "pool", "sp")}
        g["mask"] = lambda n: g["masks"][:, MASKS.index(n), :]
        g["ident"] = g["mask"]("ident")
        g["mod_rows"] = dram("mod_rows_dram", [P, 4 * D])
        g["y_chunks"] = dram("y_chunks", [2, LAT_CHUNKS * P * KT * C])
        g["v_dram"] = dram("v_chunks", [KT, CHUNKS * P * C])
        g["kr_dram"] = dram("kr_chunks", [2, KT, CHUNKS * P * 2 * C])
        g["bk_dram"] = dram("bk_chunks", [2, KT, CHUNKS * P * 2 * C])
        g["hT"] = sb("hT", [P, KT, TOK])
        g["xg"] = sb("xg_sb", [P, SEQ])
        g["bonus"] = sb("bonus_sb", [P, KT, SEQ])
        g["decay_end"] = sb("decay_end", [P, 2, CHUNKS, KT])
        g["small"] = sb("small_sb", [P, 4])
        g["gn_eps"] = g["small"][:, 0:1]
        mean_w = sb("mean_w", [P, P])
        g["mean_w"] = mean_w[:, :]
        g["f_dram"] = dram("f_rows", [SEQ, D])
        g["slot_tok"] = dram("slot_tok", [TILES * SLOTS, 1])
        g["y_dram"] = dram("y_rows", [TILES * SLOTS, D])
        with ExitStack() as inner:
            tb = token_buffers(nc, inner)
            modulation(nc, g, I, tb)
            norm_and_turn(nc, g, I, tb)
        with ExitStack() as inner:
            g["xw"] = inner.enter_context(nc.sbuf_tensor("xw_sb", [P, 2, TOK], F32))
            g["xa"] = inner.enter_context(nc.sbuf_tensor("xa_sb", [P, 2, TOK], F32))
            low_rank_inputs(nc, g, I)
            prepare(nc, g, I)
        x1 = g["hT"][:, :, :].rearrange("p k t -> p (k t)")[:, 0:SEQ * KT].rearrange("p (t e) -> p t e", e=D)
        logits = sb("logits", [P, SEQ // P, 36])
        with ExitStack() as mixers:
            msb = lambda n, s: mixers.enter_context(nc.sbuf_tensor(n, s, F32))
            with ExitStack() as inner:
                S = [inner.enter_context(nc.sbuf_tensor(f"state{d}", [P, KT, P], F32)) for d in range(2)]
                q = recurrence_buffers(nc, inner)
                recurrence(nc, g, 0, S, q)
                recurrence(nc, g, 1, S, q)
            ry, merged = msb("rwkv_y", [P, KT, SEQ]), msb("merged", [P, KT, SEQ])
            pb = pool_buffers(nc, mixers)
            read_out(nc, g, I, ry, pb)
            py = msb("pool_y", [P, 4, SEQ])
            w_merge, merge_loaded = merge_buffers(nc, mixers)

            def load_merge(sp):
                for u in range(2):
                    sp.dma_start(w_merge[:, u, :, :], I["w_merge"][u].rearrange("p (m n) -> p m n", m=MG)).then_inc(merge_loaded[u], 16)

            pooling(nc, g, I, py, pb, load_merge)
            w_out, w_out_loaded = pb["w_out"], mixers.enter_context(nc.semaphore("w_out_loaded"))

            def load_out(sp):
                sp.dma_start(w_out[:, :, :], I["w_out"]).then_inc(w_out_loaded, 16)

            merge(nc, g, I, py, ry, merged, w_merge, merge_loaded, load_out)
            project_out(nc, g, I, merged, x1, logits, w_out, w_out_loaded)
        R = {"slot": sb("slot", [P, 2, SEQ // P], U32), "gate": sb("gate", [P, 2, SEQ // P]), "tok": sb("tok", [P, TILES], U32),
             "spill_expert": sb("spill_expert", [P, SPILL], I32), "spill_tiles": sb("spill_tiles", [P, 1], I32)}
        with ExitStack() as inner:
            w, wl = expert_weights(nc, inner)
            route(nc, g, I, logits, R, w, wl)
            g["gathered"] = [inner.enter_context(nc.semaphore(f"ex_gathered{v}")) for v in range(2)]
            experts(nc, g, I, R, w, wl)
        combine(nc, g, I, R, x1, out)


def kernel(**inputs):
    import concourse.bacc as bacc
    from concourse.bass_utils import run_bass_kernel_spmd

    nc = bacc.Bacc("TRN2", target_bir_lowering=False, num_devices=1)
    arrays = {f"in_{k}": v for k, v in layout(inputs).items()}
    aps = {k[3:]: nc.dram_tensor(k, v.shape, mybir.dt.from_np(v.dtype), kind="ExternalInput").ap() for k, v in arrays.items()}
    out = nc.dram_tensor("out", (1, SEQ, D), F32, kind="ExternalOutput").ap()
    program(nc, aps, out)
    r = run_bass_kernel_spmd(nc, [arrays], core_ids=[0])
    return r.results[0]["out"]
```
